# Optimizing a Trainium2 kernel written in Bass

```python
import jax, jax.numpy as jnp
from jax import lax
import numpy as np
import jax
import jax.numpy as jnp

D_MODEL = 1024
BATCH = 1
SEQ = 256
DEPTH = 2

HEAD_DIM = 64
SWA_Q_HEADS = 8
SWA_KV_HEADS = 2
SWA_WINDOW = 128
SB_HEADS = 8
SB_Q_BLOCK = 128
MOBA_HEADS = 8
MOBA_BLOCK = 256
MOBA_TOPK = 3
MOBA_Q_CHUNK = 16
BRANCH_WIDTH = 512
N_BRANCHES = 3
D_FF = 2816
CONV_WIDTH = 3
ROPE_THETA = 10000.0
RMS_EPS = 1e-6

IN_SIZES = (
    SWA_Q_HEADS * HEAD_DIM, SWA_KV_HEADS * HEAD_DIM, SWA_KV_HEADS * HEAD_DIM,
    SB_HEADS * HEAD_DIM, SB_HEADS * HEAD_DIM, SB_HEADS * HEAD_DIM,
    MOBA_HEADS * HEAD_DIM, MOBA_HEADS * HEAD_DIM, MOBA_HEADS * HEAD_DIM,
    N_BRANCHES * D_MODEL,
)
D_IN = sum(IN_SIZES)


def rmsnorm(x, g):
    xf = x.astype(jnp.float32)
    y = xf * lax.rsqrt(jnp.mean(xf * xf, axis=-1, keepdims=True) + RMS_EPS)
    return (y * g.astype(jnp.float32)).astype(x.dtype)

def rope_tables(seq):
    inv = ROPE_THETA ** (-jnp.arange(0, HEAD_DIM, 2, dtype=jnp.float32) / HEAD_DIM)
    ang = jnp.arange(seq, dtype=jnp.float32)[:, None] * inv[None, :]
    return jnp.cos(ang), jnp.sin(ang)

def apply_rope(x, cos, sin):
    x1, x2 = jnp.split(x.astype(jnp.float32), 2, axis=-1)
    c = cos[None, :, None, :]
    s = sin[None, :, None, :]
    return jnp.concatenate([x1 * c - x2 * s, x2 * c + x1 * s], axis=-1).astype(x.dtype)

def swa_sink_attention(q, k, v, sinks):
    B, S = q.shape[0], q.shape[1]
    W = SWA_WINDOW
    nblk = S // W
    G = SWA_Q_HEADS // SWA_KV_HEADS
    scale = HEAD_DIM ** -0.5
    qb = q.reshape(B, nblk, W, SWA_KV_HEADS, G, HEAD_DIM)
    kb = k.reshape(B, nblk, W, SWA_KV_HEADS, HEAD_DIM)
    vb = v.reshape(B, nblk, W, SWA_KV_HEADS, HEAD_DIM)
    pad = ((0, 0), (1, 0), (0, 0), (0, 0), (0, 0))
    kk = jnp.concatenate([jnp.pad(kb, pad)[:, :-1], kb], axis=2)
    vv = jnp.concatenate([jnp.pad(vb, pad)[:, :-1], vb], axis=2)
    scores = jnp.einsum('bnqhgd,bnkhd->bnhgqk', qb, kk).astype(jnp.float32) * scale
    qpos = jnp.arange(W)[:, None] + W
    kpos = jnp.arange(2 * W)[None, :]
    diff = qpos - kpos
    band = (diff >= 0) & (diff < W)
    blk = jnp.arange(nblk)[:, None, None]
    valid = band[None] & ((blk * W + kpos[None] - W) >= 0)
    scores = jnp.where(valid[None, :, None, None], scores, -jnp.inf)
    sink = sinks.astype(jnp.float32).reshape(SWA_KV_HEADS, G)[None, None, :, :, None, None]
    sink = jnp.broadcast_to(sink, scores.shape[:-1] + (1,))
    probs = jax.nn.softmax(jnp.concatenate([scores, sink], axis=-1), axis=-1)[..., :-1]
    out = jnp.einsum('bnhgqk,bnkhd->bnqhgd', probs.astype(v.dtype), vv)
    return out.reshape(B, S, SWA_Q_HEADS * HEAD_DIM)

def stick_breaking_attention(q, k, v):
    B, S, H, dh = q.shape
    nblk = S // SB_Q_BLOCK
    scale = dh ** -0.5
    q_blocks = q.reshape(B, nblk, SB_Q_BLOCK, H, dh).transpose(1, 0, 2, 3, 4)
    kpos = jnp.arange(S)

    def block(args):
        q_blk, i = args
        z = jnp.einsum('bqhd,bkhd->bhqk', q_blk, k).astype(jnp.float32) * scale
        qpos = i * SB_Q_BLOCK + jnp.arange(SB_Q_BLOCK)
        past = kpos[None, :] < qpos[:, None]
        log_beta = jax.nn.log_sigmoid(z)
        log_one_minus = jnp.where(past, jax.nn.log_sigmoid(-z), 0.0)
        remain = lax.cumsum(log_one_minus, axis=3, reverse=True) - log_one_minus
        w = jnp.where(past, jnp.exp(log_beta + remain), 0.0)
        return jnp.einsum('bhqk,bkhd->bqhd', w.astype(v.dtype), v)

    out = lax.map(block, (q_blocks, jnp.arange(nblk)))
    return out.transpose(1, 0, 2, 3, 4).reshape(B, S, H * dh)

def moba_attention(q, k, v):
    B, S, H, dh = q.shape
    nb = -(-S // MOBA_BLOCK)
    pad = nb * MOBA_BLOCK - S
    ksel = min(MOBA_TOPK, nb)
    scale = dh ** -0.5
    kp = jnp.pad(k, ((0, 0), (0, pad), (0, 0), (0, 0)))
    vp = jnp.pad(v, ((0, 0), (0, pad), (0, 0), (0, 0)))
    kb = kp.reshape(B, nb, MOBA_BLOCK, H, dh)
    vb = vp.reshape(B, nb, MOBA_BLOCK, H, dh)
    k_mean = jnp.mean(kb.astype(jnp.float32), axis=2)
    gate = jnp.einsum('bshd,bnhd->bhsn', q.astype(jnp.float32), k_mean)
    q_blk = jnp.arange(S) // MOBA_BLOCK
    past_blk = jnp.arange(nb)[None, :] < q_blk[:, None]
    gate = jnp.where(past_blk[None, None], gate, -jnp.inf)
    _, sel = lax.top_k(gate, ksel)
    sel_valid = sel < q_blk[None, None, :, None]

    C = MOBA_Q_CHUNK
    nchunk = S // C
    q_c = q.reshape(B, nchunk, C, H, dh).transpose(1, 0, 2, 3, 4)
    sel_c = sel.reshape(B, H, nchunk, C, ksel).transpose(2, 0, 1, 3, 4)
    valid_c = sel_valid.reshape(B, H, nchunk, C, ksel).transpose(2, 0, 1, 3, 4)
    kb_h = kb.transpose(0, 3, 1, 2, 4)
    vb_h = vb.transpose(0, 3, 1, 2, 4)
    gather = jax.vmap(jax.vmap(lambda blocks, idx: blocks[idx]))

    def chunk(args):
        q_blk, sel_blk, valid_blk, i = args
        t0 = i * C
        qpos = t0 + jnp.arange(C)
        own_start = (t0 // MOBA_BLOCK) * MOBA_BLOCK
        k_own = lax.dynamic_slice_in_dim(kp, own_start, MOBA_BLOCK, axis=1)
        v_own = lax.dynamic_slice_in_dim(vp, own_start, MOBA_BLOCK, axis=1)
        k_sel = gather(kb_h, sel_blk)
        v_sel = gather(vb_h, sel_blk)
        s_sel = jnp.einsum('bqhd,bhqnkd->bhqnk', q_blk, k_sel).astype(jnp.float32) * scale
        s_sel = jnp.where(valid_blk[..., None], s_sel, -jnp.inf).reshape(B, H, C, ksel * MOBA_BLOCK)
        s_own = jnp.einsum('bqhd,bkhd->bhqk', q_blk, k_own).astype(jnp.float32) * scale
        kpos_own = own_start + jnp.arange(MOBA_BLOCK)
        s_own = jnp.where(kpos_own[None, :] <= qpos[:, None], s_own, -jnp.inf)
        p = jax.nn.softmax(jnp.concatenate([s_sel, s_own], axis=-1), axis=-1)
        p_sel = p[..., :ksel * MOBA_BLOCK].reshape(B, H, C, ksel, MOBA_BLOCK).astype(v.dtype)
        p_own = p[..., ksel * MOBA_BLOCK:].astype(v.dtype)
        return (jnp.einsum('bhqnk,bhqnkd->bqhd', p_sel, v_sel)
                + jnp.einsum('bhqk,bkhd->bqhd', p_own, v_own))

    out = lax.map(chunk, (q_c, sel_c, valid_c, jnp.arange(nchunk)))
    return out.transpose(1, 0, 2, 3, 4).reshape(B, S, H * dh)

def causal_depthwise_conv(u, w, b):
    S = u.shape[1]
    up = jnp.pad(u, ((0, 0), (CONV_WIDTH - 1, 0), (0, 0)))
    out = b
    for tap in range(CONV_WIDTH):
        out = out + w[tap] * up[:, tap:tap + S]
    return out

def hybrid_layer(x, cos, sin, norm_mix, w_in, b_gate, sinks, w_branch, w_out,
                 norm_ffn, w_up, conv_w, conv_b, w_down):
    B, S, _ = x.shape
    h = rmsnorm(x, norm_mix)
    proj = h @ w_in
    points = np.cumsum(IN_SIZES)[:-1].tolist()
    qa, ka, va, qb, kb, vb, qc, kc, vc, gates = jnp.split(proj, points, axis=-1)
    heads = lambda t, n: t.reshape(B, S, n, HEAD_DIM)
    o_a = swa_sink_attention(apply_rope(heads(qa, SWA_Q_HEADS), cos, sin),
                             apply_rope(heads(ka, SWA_KV_HEADS), cos, sin),
                             heads(va, SWA_KV_HEADS), sinks)
    o_b = stick_breaking_attention(heads(qb, SB_HEADS), heads(kb, SB_HEADS), heads(vb, SB_HEADS))
    o_c = moba_attention(apply_rope(heads(qc, MOBA_HEADS), cos, sin),
                         apply_rope(heads(kc, MOBA_HEADS), cos, sin),
                         heads(vc, MOBA_HEADS))
    g = jax.nn.sigmoid(gates.reshape(B, S, N_BRANCHES, D_MODEL) + b_gate.reshape(N_BRANCHES, D_MODEL))
    merged = (g[:, :, 0] * (o_a @ w_branch[0])
              + g[:, :, 1] * (o_b @ w_branch[1])
              + g[:, :, 2] * (o_c @ w_branch[2]))
    x = x + merged @ w_out
    h = rmsnorm(x, norm_ffn)
    u = causal_depthwise_conv(h @ w_up, conv_w, conv_b)
    u_a, u_v = jnp.split(u, 2, axis=-1)
    return x + (jax.nn.silu(u_a) * u_v) @ w_down

def first_inputs(seed: int = 0) -> dict:
    key = jax.random.key(seed)
    ks = jax.random.split(key, 13)
    f32 = jnp.float32
    nrm = lambda k, shape, s: jax.random.normal(k, shape, f32) * s
    return {
        "x": nrm(ks[0], (BATCH, SEQ, D_MODEL), 1.0),
        "norm_mix": 1.0 + nrm(ks[1], (DEPTH, D_MODEL), 0.02),
        "w_in": nrm(ks[2], (DEPTH, D_MODEL, D_IN), D_MODEL ** -0.5),
        "b_gate": nrm(ks[3], (DEPTH, N_BRANCHES * D_MODEL), 0.1),
        "sinks": nrm(ks[4], (DEPTH, SWA_Q_HEADS), 0.5),
        "w_branch": nrm(ks[5], (DEPTH, N_BRANCHES, BRANCH_WIDTH, D_MODEL), BRANCH_WIDTH ** -0.5),
        "w_out": nrm(ks[6], (DEPTH, D_MODEL, D_MODEL), D_MODEL ** -0.5),
        "norm_ffn": 1.0 + nrm(ks[7], (DEPTH, D_MODEL), 0.02),
        "w_up": nrm(ks[8], (DEPTH, D_MODEL, 2 * D_FF), D_MODEL ** -0.5),
        "conv_w": nrm(ks[9], (DEPTH, CONV_WIDTH, 2 * D_FF), CONV_WIDTH ** -0.5),
        "conv_b": nrm(ks[10], (DEPTH, 2 * D_FF), 0.01),
        "w_down": nrm(ks[11], (DEPTH, D_FF, D_MODEL), D_FF ** -0.5),
        "norm_final": 1.0 + nrm(ks[12], (D_MODEL,), 0.02),
    }

def first_block(x, norm_mix, w_in, b_gate, sinks, w_branch, w_out, norm_ffn,
              w_up, conv_w, conv_b, w_down, norm_final):
    cos, sin = rope_tables(x.shape[1])
    for layer in range(DEPTH):
        x = hybrid_layer(x, cos, sin, norm_mix[layer], w_in[layer], b_gate[layer],
                         sinks[layer], w_branch[layer], w_out[layer], norm_ffn[layer],
                         w_up[layer], conv_w[layer], conv_b[layer], w_down[layer])
    return rmsnorm(x, norm_final)


CHUNK = 64
Q_BLOCK = 128
ROPE_BASE = 10000.0
LN_EPS = 1e-5
NEG = -1e30

RET_HEADS = 4
RET_DIM = 64
RET_W = RET_HEADS * RET_DIM
MLA_HEADS = 8
MLA_NOPE = 64
MLA_ROPE = 32
MLA_V = 64
MLA_Q_RANK = 256
MLA_KV_RANK = 128
MLA_W = MLA_HEADS * MLA_V
MLSTM_HEADS = 4
MLSTM_DIM = 64
MLSTM_W = MLSTM_HEADS * MLSTM_DIM
MLSTM_CONV = 4
MIX_W = RET_W + MLA_W + MLSTM_W

IN_SIZES_2 = (RET_W, RET_W, RET_W, RET_W, MLA_Q_RANK, MLA_KV_RANK, MLA_ROPE, MLSTM_W, MLSTM_W, MLSTM_W, MLSTM_W, MLSTM_HEADS, MLSTM_HEADS)
IN_IS_VALUE = (False, False, True, False, False, False, False, False, False, True, False, False, False)
D_IN_2 = sum(IN_SIZES_2)

N_EXPERTS = 8
TOP_K = 2
D_FF_EXPERT = 3584
N_DENSE = (DEPTH + 1) // 2
N_MOE = DEPTH // 2

DN_ALPHA = (2 * DEPTH) ** 0.25
DN_BETA = (8 * DEPTH) ** -0.25


def layer_norm(x, w, b):
    x32 = x.astype(jnp.float32)
    mu = x32.mean(-1, keepdims=True)
    var = jnp.square(x32 - mu).mean(-1, keepdims=True)
    return ((x32 - mu) * lax.rsqrt(var + LN_EPS) * w + b).astype(x.dtype)

def rms_norm(x, w):
    x32 = x.astype(jnp.float32)
    y = x32 * lax.rsqrt(jnp.square(x32).mean(-1, keepdims=True) + LN_EPS) * w
    return y.astype(x.dtype)

def head_norm(x, w, n_heads):
    b, s, wd = x.shape
    xh = x.astype(jnp.float32).reshape(b, s, n_heads, wd // n_heads)
    mu = xh.mean(-1, keepdims=True)
    var = jnp.square(xh - mu).mean(-1, keepdims=True)
    return ((xh - mu) * lax.rsqrt(var + LN_EPS)).reshape(b, s, wd) * w

def to_heads(x, n):
    b, s, w = x.shape
    return x.reshape(b, s, n, w // n).transpose(0, 2, 1, 3)

def from_heads(x):
    b, h, s, d = x.shape
    return x.transpose(0, 2, 1, 3).reshape(b, s, h * d)

def rope(x, pos):
    half = x.shape[-1] // 2
    inv = ROPE_BASE ** (-jnp.arange(half, dtype=jnp.float32) / half)
    ang = pos[:, None] * inv[None, :]
    cos, sin = jnp.cos(ang), jnp.sin(ang)
    x32 = x.astype(jnp.float32)
    x1, x2 = x32[..., :half], x32[..., half:]
    return jnp.concatenate([x1 * cos - x2 * sin, x1 * sin + x2 * cos], -1).astype(x.dtype)

def retention(q, k, v):
    b, h, s, d = q.shape
    L = CHUNK
    nc = s // L
    log_gamma = jnp.log(1.0 - 2.0 ** (-5.0 - jnp.arange(h, dtype=jnp.float32)))
    idx = jnp.arange(L, dtype=jnp.float32)
    diff = idx[:, None] - idx[None, :]
    inner_decay = jnp.where(diff >= 0, jnp.exp(diff[None] * log_gamma[:, None, None]), 0.0)
    qc = q.astype(jnp.float32).reshape(b, h, nc, L, d)
    kc = (k.astype(jnp.float32) * d ** -0.5).reshape(b, h, nc, L, d)
    vc = v.astype(jnp.float32).reshape(b, h, nc, L, d)
    scores = jnp.einsum('bhcld,bhcmd->bhclm', qc, kc) * inner_decay[None, :, None]
    inner = jnp.einsum('bhclm,bhcme->bhcle', scores, vc)
    kv_w = jnp.exp((L - 1 - idx)[None, :] * log_gamma[:, None])
    local = jnp.einsum('bhcmd,bhcme->bhcde', kc * kv_w[None, :, None, :, None], vc)
    chunk_decay = jnp.exp(L * log_gamma)[None, :, None, None]

    def step(state, loc):
        return chunk_decay * state + loc, state

    _, r_prev = lax.scan(step, jnp.zeros((b, h, d, d), jnp.float32), jnp.moveaxis(local, 2, 0))
    r_prev = jnp.moveaxis(r_prev, 0, 2)
    q_w = jnp.exp((idx + 1.0)[None, :] * log_gamma[:, None])
    cross = jnp.einsum('bhcld,bhcde->bhcle', qc, r_prev) * q_w[None, :, None, :, None]
    return (inner + cross).reshape(b, h, s, d)

def mlstm(q, k, v, ig, fg):
    b, h, s, d = q.shape
    L = CHUNK
    nc = s // L
    qc = q.astype(jnp.float32).reshape(b, h, nc, L, d)
    kc = (k.astype(jnp.float32) * d ** -0.5).reshape(b, h, nc, L, d)
    vc = v.astype(jnp.float32).reshape(b, h, nc, L, d)
    ic = ig.astype(jnp.float32).reshape(b, h, nc, L)
    lf = jax.nn.log_sigmoid(fg.astype(jnp.float32)).reshape(b, h, nc, L)
    bcum = jnp.cumsum(lf, axis=-1)
    g = bcum[..., -1]
    a = g[..., None] - bcum + ic
    amax = a.max(-1)
    wa = jnp.exp(a - amax[..., None])
    loc_c = jnp.einsum('bhcl,bhcld,bhcle->bhcde', wa, kc, vc)
    loc_n = jnp.einsum('bhcl,bhcld->bhcd', wa, kc)

    def step(carry, xs):
        c_s, n_s, m_s = carry
        g_c, amax_c, lc, ln = xs
        m_new = jnp.maximum(g_c + m_s, amax_c)
        sp = jnp.exp(g_c + m_s - m_new)
        sl = jnp.exp(amax_c - m_new)
        c_new = sp[..., None, None] * c_s + sl[..., None, None] * lc
        n_new = sp[..., None] * n_s + sl[..., None] * ln
        return (c_new, n_new, m_new), (c_s, n_s, m_s)

    init = (jnp.zeros((b, h, d, d), jnp.float32), jnp.zeros((b, h, d), jnp.float32), jnp.full((b, h), NEG, jnp.float32))
    xs = (jnp.moveaxis(g, 2, 0), jnp.moveaxis(amax, 2, 0), jnp.moveaxis(loc_c, 2, 0), jnp.moveaxis(loc_n, 2, 0))
    _, (c_prev, n_prev, m_prev) = lax.scan(step, init, xs)
    c_prev = jnp.moveaxis(c_prev, 0, 2)
    n_prev = jnp.moveaxis(n_prev, 0, 2)
    m_prev = jnp.moveaxis(m_prev, 0, 2)
    idx = jnp.arange(L)
    causal = idx[:, None] >= idx[None, :]
    log_d = jnp.where(causal, bcum[..., :, None] - bcum[..., None, :] + ic[..., None, :], NEG)
    inter = bcum + m_prev[..., None]
    m_t = jnp.maximum(inter, log_d.max(-1))
    dw = jnp.exp(log_d - m_t[..., None])
    cmat = jnp.einsum('bhcld,bhcmd->bhclm', qc, kc) * dw
    si = jnp.exp(inter - m_t)
    num = jnp.einsum('bhclm,bhcme->bhcle', cmat, vc) + si[..., None] * jnp.einsum('bhcld,bhcde->bhcle', qc, c_prev)
    den = cmat.sum(-1) + si * jnp.einsum('bhcld,bhcd->bhcl', qc, n_prev)
    hcell = num / jnp.maximum(jnp.abs(den), jnp.exp(-m_t))[..., None]
    return hcell.reshape(b, h, s, d)

def mla_attention(q_nope, q_rope, k_nope, k_rope, v):
    b, h, s, dn = q_nope.shape
    dr = q_rope.shape[-1]
    nq = s // Q_BLOCK
    scale = (dn + dr) ** -0.5
    kpos = jnp.arange(s)
    qn_b = q_nope.reshape(b, h, nq, Q_BLOCK, dn).transpose(2, 0, 1, 3, 4)
    qr_b = q_rope.reshape(b, h, nq, Q_BLOCK, dr).transpose(2, 0, 1, 3, 4)

    def block(args):
        qn, qr, i = args
        sc = jnp.einsum('bhqd,bhkd->bhqk', qn, k_nope) + jnp.einsum('bhqr,bkr->bhqk', qr, k_rope)
        sc = sc.astype(jnp.float32) * scale
        qpos = i * Q_BLOCK + jnp.arange(Q_BLOCK)
        limit = (qpos // CHUNK + 1) * CHUNK
        sc = jnp.where(kpos[None, :] < limit[:, None], sc, NEG)
        p = jax.nn.softmax(sc, axis=-1).astype(v.dtype)
        return jnp.einsum('bhqk,bhkd->bhqd', p, v)

    out = lax.map(block, (qn_b, qr_b, jnp.arange(nq)))
    return out.transpose(1, 2, 0, 3, 4).reshape(b, h, s, v.shape[-1])

def causal_dwconv(x, w, bias):
    kw, c = w.shape
    y = lax.conv_general_dilated(x, w.reshape(kw, 1, c).astype(x.dtype), window_strides=(1,), padding=[(kw - 1, 0)], dimension_numbers=('NWC', 'WIO', 'NWC'), feature_group_count=c)
    return y + bias

def hybrid_mixer(x, pos, w_in, ret_gn_w, mla_q_norm_w, mla_w_uq, mla_kv_norm_w, mla_w_ukv, conv_w, conv_b, b_i, b_f, mlstm_gn_w, w_out):
    bsz, s, _ = x.shape
    hcat = x @ w_in
    offsets = np.cumsum(IN_SIZES_2)[:-1].tolist()
    (r_q, r_k, r_v, r_g, c_q, c_kv, k_r, m_q, m_k, m_v, m_o, m_i, m_f) = jnp.split(hcat, offsets, axis=-1)
    rq = rope(to_heads(r_q, RET_HEADS), pos)
    rk = rope(to_heads(r_k, RET_HEADS), pos)
    ret = retention(rq, rk, to_heads(r_v, RET_HEADS))
    ret_out = jax.nn.silu(r_g.astype(jnp.float32)) * head_norm(from_heads(ret), ret_gn_w, RET_HEADS)
    qf = (rms_norm(c_q, mla_q_norm_w) @ mla_w_uq).reshape(bsz, s, MLA_HEADS, MLA_NOPE + MLA_ROPE).transpose(0, 2, 1, 3)
    q_nope, q_rope = qf[..., :MLA_NOPE], rope(qf[..., MLA_NOPE:], pos)
    kvf = (rms_norm(c_kv, mla_kv_norm_w) @ mla_w_ukv).reshape(bsz, s, MLA_HEADS, MLA_NOPE + MLA_V).transpose(0, 2, 1, 3)
    k_nope, v_mla = kvf[..., :MLA_NOPE], kvf[..., MLA_NOPE:]
    k_rope = rope(k_r, pos)
    att_out = from_heads(mla_attention(q_nope, q_rope, k_nope, k_rope, v_mla))
    qk = jax.nn.silu(causal_dwconv(jnp.concatenate([m_q, m_k], -1), conv_w, conv_b))
    mq, mk = qk[..., :MLSTM_W], qk[..., MLSTM_W:]
    ig = (m_i + b_i).transpose(0, 2, 1)
    fg = (m_f + b_f).transpose(0, 2, 1)
    hcell = mlstm(to_heads(mq, MLSTM_HEADS), to_heads(mk, MLSTM_HEADS), to_heads(m_v, MLSTM_HEADS), ig, fg)
    h_gated = jax.nn.sigmoid(m_o.astype(jnp.float32)) * from_heads(hcell)
    mlstm_out = head_norm(h_gated, mlstm_gn_w, MLSTM_HEADS)
    merged = jnp.concatenate([ret_out.astype(x.dtype), att_out.astype(x.dtype), mlstm_out.astype(x.dtype)], -1)
    return merged @ w_out

def swiglu(x, wg, wu, wd):
    return (jax.nn.silu(x @ wg) * (x @ wu)) @ wd

def moe_swiglu(x, router, wg, wu, wd):
    bsz, s, d = x.shape
    t = x.reshape(bsz * s, d)
    logits = (t @ router).astype(jnp.float32)
    top_v, top_i = lax.top_k(logits, TOP_K)
    top_w = jax.nn.softmax(top_v, axis=-1)
    gate = jnp.sum(jax.nn.one_hot(top_i, N_EXPERTS, dtype=jnp.float32) * top_w[..., None], axis=1)
    y = jnp.zeros((bsz * s, d), jnp.float32)
    for e in range(N_EXPERTS):
        y = y + gate[:, e:e + 1] * swiglu(t, wg[e], wu[e], wd[e]).astype(jnp.float32)
    return y.astype(x.dtype).reshape(bsz, s, d)

def second_inputs(seed: int = 0) -> dict:
    key = jax.random.key(seed)
    ks = jax.random.split(key, 24)
    L = DEPTH

    def nrm(k, shape, scale):
        return jax.random.normal(k, shape, jnp.float32) * scale

    col_scale = np.concatenate([np.full(n, DN_BETA if isv else 1.0, np.float32) for n, isv in zip(IN_SIZES_2, IN_IS_VALUE)])
    ukv_scale = np.tile(np.concatenate([np.ones(MLA_NOPE, np.float32), np.full(MLA_V, DN_BETA, np.float32)]), MLA_HEADS)
    return {
        'x': nrm(ks[0], (BATCH, SEQ, D_MODEL), 1.0),
        'w_in': nrm(ks[1], (L, D_MODEL, D_IN_2), D_MODEL ** -0.5) * jnp.asarray(col_scale),
        'ret_gn_w': 1.0 + nrm(ks[2], (L, RET_W), 0.01),
        'mla_q_norm_w': 1.0 + nrm(ks[3], (L, MLA_Q_RANK), 0.01),
        'mla_w_uq': nrm(ks[4], (L, MLA_Q_RANK, MLA_HEADS * (MLA_NOPE + MLA_ROPE)), MLA_Q_RANK ** -0.5),
        'mla_kv_norm_w': 1.0 + nrm(ks[5], (L, MLA_KV_RANK), 0.01),
        'mla_w_ukv': nrm(ks[6], (L, MLA_KV_RANK, MLA_HEADS * (MLA_NOPE + MLA_V)), MLA_KV_RANK ** -0.5) * jnp.asarray(ukv_scale),
        'mlstm_conv_w': nrm(ks[7], (L, MLSTM_CONV, 2 * MLSTM_W), MLSTM_CONV ** -0.5),
        'mlstm_conv_b': nrm(ks[8], (L, 2 * MLSTM_W), 0.01),
        'mlstm_b_i': nrm(ks[9], (L, MLSTM_HEADS), 0.1),
        'mlstm_b_f': jnp.linspace(3.0, 6.0, MLSTM_HEADS, dtype=jnp.float32)[None, :] + nrm(ks[10], (L, MLSTM_HEADS), 0.01),
        'mlstm_gn_w': 1.0 + nrm(ks[11], (L, MLSTM_W), 0.01),
        'w_out': nrm(ks[12], (L, MIX_W, D_MODEL), MIX_W ** -0.5 * DN_BETA),
        'ln1_w': 1.0 + nrm(ks[13], (L, D_MODEL), 0.01),
        'ln1_b': nrm(ks[14], (L, D_MODEL), 0.01),
        'ffn_w_gate': nrm(ks[15], (N_DENSE, D_MODEL, D_FF), D_MODEL ** -0.5),
        'ffn_w_up': nrm(ks[16], (N_DENSE, D_MODEL, D_FF), D_MODEL ** -0.5 * DN_BETA),
        'ffn_w_down': nrm(ks[17], (N_DENSE, D_FF, D_MODEL), D_FF ** -0.5 * DN_BETA),
        'moe_router': nrm(ks[18], (N_MOE, D_MODEL, N_EXPERTS), D_MODEL ** -0.5),
        'moe_w_gate': nrm(ks[19], (N_MOE, N_EXPERTS, D_MODEL, D_FF_EXPERT), D_MODEL ** -0.5),
        'moe_w_up': nrm(ks[20], (N_MOE, N_EXPERTS, D_MODEL, D_FF_EXPERT), D_MODEL ** -0.5 * DN_BETA),
        'moe_w_down': nrm(ks[21], (N_MOE, N_EXPERTS, D_FF_EXPERT, D_MODEL), D_FF_EXPERT ** -0.5 * DN_BETA),
        'ln2_w': 1.0 + nrm(ks[22], (L, D_MODEL), 0.01),
        'ln2_b': nrm(ks[23], (L, D_MODEL), 0.01),
    }

def second_block(x, w_in, ret_gn_w, mla_q_norm_w, mla_w_uq, mla_kv_norm_w, mla_w_ukv, mlstm_conv_w, mlstm_conv_b, mlstm_b_i, mlstm_b_f, mlstm_gn_w, w_out, ln1_w, ln1_b, ffn_w_gate, ffn_w_up, ffn_w_down, moe_router, moe_w_gate, moe_w_up, moe_w_down, ln2_w, ln2_b):
    pos = jnp.arange(x.shape[1], dtype=jnp.float32)
    for l in range(DEPTH):
        mix = hybrid_mixer(x, pos, w_in[l], ret_gn_w[l], mla_q_norm_w[l], mla_w_uq[l], mla_kv_norm_w[l], mla_w_ukv[l], mlstm_conv_w[l], mlstm_conv_b[l], mlstm_b_i[l], mlstm_b_f[l], mlstm_gn_w[l], w_out[l])
        x = layer_norm(DN_ALPHA * x + mix, ln1_w[l], ln1_b[l])
        if l % 2 == 0:
            f = swiglu(x, ffn_w_gate[l // 2], ffn_w_up[l // 2], ffn_w_down[l // 2])
        else:
            f = moe_swiglu(x, moe_router[l // 2], moe_w_gate[l // 2], moe_w_up[l // 2], moe_w_down[l // 2])
        x = layer_norm(DN_ALPHA * x + f, ln2_w[l], ln2_b[l])
    return x


def setup_inputs(seed=0):
    out = dict(first_inputs(seed))
    for name, value in second_inputs(seed + 1).items():
        if name != "x":
            out[name + "_2"] = value
    return out


def reference(
    x, norm_mix, w_in, b_gate, sinks, w_branch, w_out, norm_ffn, w_up, conv_w, conv_b, w_down,
    norm_final, w_in_2, ret_gn_w_2, mla_q_norm_w_2, mla_w_uq_2, mla_kv_norm_w_2, mla_w_ukv_2,
    mlstm_conv_w_2, mlstm_conv_b_2, mlstm_b_i_2, mlstm_b_f_2, mlstm_gn_w_2, w_out_2, ln1_w_2,
    ln1_b_2, ffn_w_gate_2, ffn_w_up_2, ffn_w_down_2, moe_router_2, moe_w_gate_2, moe_w_up_2,
    moe_w_down_2, ln2_w_2, ln2_b_2,
):
    x = first_block(
        x, norm_mix, w_in, b_gate, sinks, w_branch, w_out, norm_ffn, w_up, conv_w, conv_b,
        w_down, norm_final,
    )
    return second_block(
        x, w_in_2, ret_gn_w_2, mla_q_norm_w_2, mla_w_uq_2, mla_kv_norm_w_2, mla_w_ukv_2,
        mlstm_conv_w_2, mlstm_conv_b_2, mlstm_b_i_2, mlstm_b_f_2, mlstm_gn_w_2, w_out_2,
        ln1_w_2, ln1_b_2, ffn_w_gate_2, ffn_w_up_2, ffn_w_down_2, moe_router_2, moe_w_gate_2,
        moe_w_up_2, moe_w_down_2, ln2_w_2, ln2_b_2,
    )


_drawn_inputs = setup_inputs


def setup_inputs(seed=0):
    import zlib

    import numpy as np

    out = dict(_drawn_inputs(seed))
    spreads = {}
    factors = {'norm_mix': 2.988,
     'sinks': 4.243,
     'conv_b': 4.336,
     'ret_gn_w_2': 27.938,
     'mla_q_norm_w_2': 8.0,
     'mla_kv_norm_w_2': 8.0,
     'mlstm_conv_b_2': 7.128,
     'mlstm_b_i_2': 24.879,
     'mlstm_gn_w_2': 32.802,
     'ln1_w_2': 3.454,
     'ln1_b_2': 3.196,
     'ln2_w_2': 3.613,
     'ln2_b_2': 3.276}
    for name, (base, spread) in spreads.items():
        noise = np.random.default_rng([zlib.crc32(name.encode()), seed]).standard_normal(out[name].shape)
        drawn = base * np.exp(spread * noise) if base else spread * noise
        out[name] = jnp.asarray(drawn.astype(out[name].dtype))
    for name, factor in factors.items():
        out[name] = (out[name] * factor).astype(out[name].dtype)
    return out
```

```python
from contextlib import ExitStack, contextmanager

import numpy as np

import concourse.bass as bass
from concourse import mybir

F32 = mybir.dt.float32
F32R = mybir.dt.float32r
I32 = mybir.dt.int32
ALU = mybir.AluOpType
ACT = mybir.ActivationFunctionType
AX = mybir.AxisListType

P = 128
S = 256
TT = S // P
D = 1024
KT = D // P
DEPTH = 2
DH = 64
D_FF = 2816
D_EXP = 3584
N_EXP = 8
CH = 2048
RAW = 6
SPLIT = 3
AHEAD = 2
NEG = -1e30
SCALE = DH**-0.5
FF_SUBS = D_FF // 256
EXP_STEPS = D_EXP // 512

A_LAYER = 15 + 18 + 6 + 3 * FF_SUBS
assert A_LAYER % RAW == 0


FREE_AT_START = {"hi_ready": RAW, "lo_ready": RAW, "w_used": RAW, "probs_turned": 4, "weighed": 2, "h_rows": 1}
FREE_AT_START.update({f"bank_free{i}": 1 for i in range(8)})


class Waits:

    def __init__(self, engine):
        self.engine = engine
        self.passed = {}
        self.turns = {}
        self.chunk = 0
        self.rings = 1

    def _count(self, key, n, start):
        self.passed[key] = self.passed.get(key, 0) + n
        return self.turns.get(key, 0) + (start + self.passed[key])

    def next(self, sem, n=1):
        return self._count(sem.name, n, FREE_AT_START.get(sem.name, 0))

    def reuse(self, sem):
        return self._count("reuse " + sem.name, 1, 0)

    def all_free(self, sem):
        return self._count("reuse " + sem.name, 0, FREE_AT_START[sem.name])

    def skip(self, sem, n):
        self._count(sem.name, n, 0)

    def product_done(self):
        return self.rings * RAW + (self.chunk - AHEAD)

    @contextmanager
    def repeat(self, count, per, end=lambda: None):
        before, turns, chunk, rings = dict(self.passed), dict(self.turns), self.chunk, self.rings
        with self.engine.Fori(0, count) as i:
            for name, n in per.items():
                if name != "chunks":
                    self.turns[name] = i * n + turns.get(name, 0)
            if per.get("chunks"):
                self.rings = i * (per["chunks"] // RAW) + rings
            yield i
            found = {k: v - before.get(k, 0) for k, v in self.passed.items() if v != before.get(k, 0)}
            if self.chunk != chunk:
                found["chunks"] = self.chunk - chunk
            assert found == per, f"{self.engine.engine}: a turn waits for {found}, not {per}"
        self.passed, self.turns, self.chunk, self.rings = before, turns, chunk, rings
        for name, n in per.items():
            if name == "chunks":
                if type(count) is int:
                    self.chunk = chunk + count * n
                else:
                    self.rings = count * (n // RAW) + rings
            elif type(count) is int:
                self.passed[name] = before.get(name, 0) + count * n
            else:
                self.turns[name] = count * n + turns.get(name, 0)

    def take(self):
        c, self.chunk = self.chunk, self.chunk + 1
        return c % RAW, c % SPLIT, self.rings + c // RAW, self.rings * RAW + c



def table_columns(parts):
    at, out = 0, {}
    for name, n in parts:
        out[name] = (at, at + n)
        at += n
    return out, at


SHARED_TABLES = [("ident", P), ("rot64", P), ("cos64", S), ("sin64", S)]
A_TABLES, A_COLS = table_columns(SHARED_TABLES + [
    ("band", S), ("causal", S), ("before01", 3 * P), ("before", 3 * P), ("tri", P), ("ones", P)])
B_TABLES, B_COLS = table_columns(SHARED_TABLES + [
    ("rot32", P), ("cos32", S), ("sin32", S), ("blocks", S), ("decay", 4 * 2 * P), ("causalT", P),
    ("ones", P), ("below", P), ("slots", P)])
TAB = max(A_COLS, B_COLS)

COUNT = 12
HALF = 56
QA, KA, QB, KB, QC, KC, A_TILES = 0, 4, 5, 9, 13, 17, 21


class Memory:

    def __init__(self, nc, ctx):
        def sb(name, shape, dt=F32):
            return ctx.enter_context(nc.sbuf_tensor(name, shape, dt))

        def sem(name):
            return ctx.enter_context(nc.semaphore(name))

        self.raw = sb("raw", [P, RAW, CH])
        self.w_hi = sb("w_hi", [P, SPLIT, CH], F32R)
        self.w_lo = sb("w_lo", [P, SPLIT, CH], F32R)
        self.hT_hi = sb("hT_hi", [P, KT, S], F32R)
        self.hT_lo = sb("hT_lo", [P, KT, S], F32R)
        self.oT_hi = sb("oT_hi", [P, 12, S], F32R)
        self.oT_lo = sb("oT_lo", [P, 12, S], F32R)
        self.x = sb("x_tok", [P, TT, D])
        self.nat = sb("nat", [P, TT, D])
        self.arena = sb("arena", [P, 7680])
        self.probs = sb("probs", [P, 4, 384])
        self.probsT = sb("probsT", [P, 2, 384])
        self.tables = sb("tables", [P, TAB])
        self.all_cols = sb("all_cols", [P, DEPTH * A_PARAMS])
        self.cols = sb("cols", [P, A_PARAMS])
        self.small = sb("small", [P, 256])
        self.units = sb("units", [P, COUNT + 1], I32)
        self.zeros = sb("zeros", [P, P], F32R)
        self.bank = [ctx.enter_context(nc.psum_tensor(f"bank{i}", [P, 512], F32))[:] for i in range(8)]

        self.raw_full = [sem(f"raw_full{i}") for i in range(RAW)]
        self.hi_ready = sem("hi_ready")
        self.lo_ready = sem("lo_ready")
        self.w_used = sem("w_used")
        self.to_act = [sem(f"to_act{i}") for i in range(8)]
        self.to_dve = [sem(f"to_dve{i}") for i in range(8)]
        self.free = [sem(f"bank_free{i}") for i in range(8)]
        self.x_loaded = sem("x_loaded")
        self.tables_loaded = sem("tables_loaded")
        self.cols_loaded = sem("cols_loaded")
        self.tables_b_loaded = sem("tables_b_loaded")
        self.cols_b_loaded = sem("cols_b_loaded")
        self.rows_loaded = sem("rows_loaded")
        self.stored = sem("stored")
        self.start = sem("start")
        self.cols_ready = sem("cols_ready")
        self.squares = sem("squares")
        self.rstd_in = sem("rstd_in")
        self.rstd = sem("rstd")
        self.nat_ready = sem("nat_ready")
        self.act_hi = sem("act_hi")
        self.hT_ready = sem("hT_ready")
        self.x_ready = sem("x_ready")
        self.kq_copied = sem("kq_copied")
        self.roped = sem("roped")
        self.copied = sem("copied")
        self.negm = sem("negm")
        self.exped = sem("exped")
        self.probs_ready = sem("probs_ready")
        self.probs_turned = sem("probs_turned")
        self.pt_ready = sem("pt_ready")
        self.weighed = sem("weighed")
        self.oT_ready = sem("oT_ready")
        self.probs_free = sem("probs_free")
        self.l_ready = sem("l_ready")
        self.z_ready = sem("z_ready")
        self.scans_ready = sem("scans_ready")
        self.cols_turned = sem("cols_turned")
        self.decay_ready = sem("decay_ready")
        self.conv_in = sem("conv_in")
        self.conv_out = sem("conv_out")
        self.pairs_ready = sem("pairs_ready")
        self.selected = sem("selected")
        self.placed = sem("placed")
        self.d_ready = sem("d_ready")
        self.e_ready = sem("e_ready")
        self.units_ready = sem("units_ready")
        self.picks_ready = sem("picks_ready")
        self.x_here = sem("x_here")
        self.result_ready = sem("result_ready")
        self.h_rows = sem("h_rows")
        self.y_rows = sem("y_rows")
        self.n_ready = sem("n_ready")
        self.lom_ready = sem("lom_ready")
        self.logw_ready = sem("logw_ready")
        self.gate_in = sem("gate_in")
        self.gate_out = sem("gate_out")
        self.silu_in = sem("silu_in")
        self.silu_done = sem("silu_done")
        self.hid = sem("hid")
        self.hid_hi = sem("hid_hi")
        self.hid_ready = sem("hid_ready")

    def tab(self, tables, name, a=0, b=None):
        lo, hi = tables[name]
        return self.tables[:, lo + a:hi if b is None else lo + b]



class Engine:
    def __init__(self, nc, mem, engine, isa, before=None):
        self.nc, self.m, self.eng, self.isa = nc, mem, engine, isa
        self.w = before.w if before else Waits(engine)


class Tensor(Engine):

    def __init__(self, nc, mem, engine, isa, before=None):
        super().__init__(nc, mem, engine, isa, before)
        self.known = set()

    def bank(self, b):
        if b in self.known:
            self.known.remove(b)
        else:
            self.eng.wait_ge(self.m.free[b], self.w.reuse(self.m.free[b]))
        return self.m.bank[b]

    def chunk(self):
        _, slot, _, number = self.w.take()
        self.eng.wait_ge(self.m.lo_ready, number + 1)
        return self.m.w_hi[:, slot, :], self.m.w_lo[:, slot, :]

    def three(self, out, st, mv, start, stop):
        mm = self.isa.matmul
        mm(out, st[0], mv[0], start=start, stop=False, skip_group_check=True)
        mm(out, st[0], mv[1], start=False, stop=False, skip_group_check=True)
        return mm(out, st[1], mv[0], start=False, stop=stop, skip_group_check=True)

    def turned(self, outs, w, width, x, kt, n=S, col=0, m=P, k0=0):
        hi, lo = (a[:, 0:kt * width].rearrange("p (k c) -> p k c", k=kt) for a in w)
        for g, out in enumerate(outs):
            for k in range(kt):
                c = slice(col + g * m, col + (g + 1) * m)
                last = self.three(out, (hi[:, k, c], lo[:, k, c]),
                                  (x[0][:, k0 + k, 0:n], x[1][:, k0 + k, 0:n]), k == 0, k == kt - 1)
        return last

    def rows(self, outs, w, width, x, kt, k0, total, col=0, n=512, opened=False, t0=0):
        hi, lo = (a[:, 0:kt * width].rearrange("p (k c) -> p k c", k=kt) for a in w)
        for k in range(kt):
            for t, out in enumerate(outs):
                tok = slice((t0 + t) * P, (t0 + t + 1) * P)
                last = self.three(out, (x[0][:, k0 + k, tok], x[1][:, k0 + k, tok]),
                                  (hi[:, k, col:col + n], lo[:, k, col:col + n]),
                                  k0 + k == 0 and not opened, k0 + k == total - 1)
        return last

    def zero(self, b):
        bank, zeros = self.bank(b), self.m.zeros[:]
        for i in range(4):
            self.isa.matmul(bank[:, i * P:(i + 1) * P], zeros, zeros, start=i == 0, stop=False,
                            skip_group_check=True)

    def used(self, last):
        last.then_inc(self.m.w_used, 1)

    def turn_rows(self, src, banks, ident, tiles=KT):
        for j, b in enumerate(banks):
            bank = self.bank(b)
            for k in range(2 * j, min(2 * j + 2, tiles)):
                for t in range(TT):
                    at = (k % 2) * S + t * P
                    last = self.isa.transpose(bank[:, at:at + P], src[:, t, k * P:(k + 1) * P], ident)
            last.then_inc(self.m.to_act[b], 1)

    def rotate(self, src, b, rot, n):
        m = self.m
        self.eng.wait_ge(m.kq_copied, self.w.next(m.kq_copied))
        bank = self.bank(b)
        last = self.isa.matmul(bank[:, 0:n * S], rot, src, start=True, stop=True)
        last.then_inc(m.to_dve[b], 1)

    def scores(self, b, parts):
        bank = self.bank(b)
        for at, q0, n in ((0, 0, P), (P, P, S)):
            for i, (q, k) in enumerate(parts):
                last = self.isa.matmul(bank[:, at:at + n], q[:, q0:q0 + P], k[:, 0:n],
                                       start=i == 0, stop=i == len(parts) - 1, skip_group_check=True)
        last.then_inc(self.m.to_dve[b], 1)

    def turn_probs(self, hh, b, ident):
        m = self.m
        self.eng.wait_ge(m.probs_ready, self.w.next(m.probs_ready))
        bank = self.bank(b)
        for i in range(3):
            last = self.isa.transpose(bank[:, i * P:(i + 1) * P], m.probs[:, hh, i * P:(i + 1) * P], ident)
        last.then_inc(m.probs_turned, 1)

    def weigh(self, h, v, turn_bank=None):
        m = self.m
        self.eng.wait_ge(m.pt_ready, self.w.next(m.pt_ready))
        if turn_bank is not None:
            self.known.add(turn_bank)
        b = 6 + (h // 2) % 2
        if h % 2 == 0:
            self.bank(b)
        pt = m.probsT[:, h % 2, :]
        base = (h % 2) * DH
        out = m.bank[b][base:base + DH, 0:S]
        self.isa.matmul(out, v[0], pt[:, 0:S], start=True, stop=False, skip_group_check=True)
        self.isa.matmul(out[:, P:S], v[1], pt[:, S:S + P], start=False, stop=True,
                        skip_group_check=True).then_inc(m.weighed, 1)

    def softmax_heads(self, parts_of, v_of, ident):
        for h in range(8):
            self.scores(h % 4, parts_of(h))
        for h in range(8):
            self.turn_probs(h % 4, 4 + h % 2, ident)
            if h:
                self.weigh(h - 1, v_of(h - 1), 4 + (h - 1) % 2)
        self.weigh(7, v_of(7), 5)

    def stick_heads(self, q_of, k_of, v_of, tri, ones):
        m = self.m
        for step in range(8 + 3):
            if step < 8:
                h = step
                bank, q, k = self.bank(h % 4), q_of(h), k_of(h)
                self.isa.matmul(bank[:, 0:S], k[:, 0:P], q, start=True, stop=False, skip_group_check=True)
                self.isa.matmul(bank[:, S:S + P], k[:, P:S], q[:, P:S], start=False, stop=False,
                                skip_group_check=True).then_inc(m.to_act[h % 4], 1)
            if 1 <= step < 9:
                h = step - 1
                bank, lom = m.bank[h % 4], m.probs[:, h % 4, :]
                self.eng.wait_ge(m.lom_ready, self.w.next(m.lom_ready))
                self.isa.matmul(bank[:, 0:S], tri, lom[:, 0:S], start=False, stop=False, skip_group_check=True)
                self.isa.matmul(bank[:, P:S], ones, lom[:, S:S + P], start=False, stop=False, skip_group_check=True)
                self.isa.matmul(bank[:, S:S + P], tri, lom[:, S:S + P], start=False, stop=True,
                                skip_group_check=True).then_inc(m.to_dve[h % 4], 1)
            if step >= 3:
                self.weigh(step - 3, v_of(step - 3))


class Scalar(Engine):

    def settle(self):
        self.eng.drain()

    def split(self, n=1):
        m = self.m
        for _ in range(n):
            raw, slot, loads, number = self.w.take()
            self.eng.wait_ge(m.raw_full[raw], loads * 16)
            self.eng.wait_ge(m.w_used, number + 1 - SPLIT)
            self.isa.copy(m.w_hi[:, slot, :], m.raw[:, raw, :]).then_inc(m.hi_ready, 1)

    def squares(self, x):
        m = self.m
        for t in range(TT):
            last = self.isa.activation(m.nat[:, t, :], x[:, t, :], ACT.Square, accum_out=m.small[:, t:t + 1])
        last.then_inc(m.squares, 1)

    def high_turned(self, banks, hi, scales=None, tiles=range(KT)):
        m = self.m
        for j, b in enumerate(banks):
            self.eng.wait_ge(m.to_act[b], self.w.next(m.to_act[b]))
            for k in range(2 * j, min(2 * j + 2, len(tiles))):
                at = (k % 2) * S
                last = self.isa.activation(hi[:, tiles[k], :], m.bank[b][:, at:at + S], ACT.Copy,
                                           scale=1.0 if scales is None else scales[:, k:k + 1])
            last.then_inc(m.act_hi, 1)

    def copy_out(self, b, pairs, to=None, scale=1.0):
        m = self.m
        for dst, src in pairs:
            last = self.isa.activation(dst, src, ACT.Copy, scale=scale)
        last.then_inc(m.free[b] if to is None else to, 1)
        if to is not None:
            self.eng.drain().then_inc(m.free[b], 1)

    def exp_group(self, sinks):
        m = self.m
        self.eng.wait_ge(m.negm, self.w.next(m.negm))
        for hh in range(4):
            for t, a, b in ((0, 0, P), (1, P, 384)):
                i = 2 * hh + t
                last = self.isa.activation(m.probs[:, hh, a:b], m.probs[:, hh, a:b], ACT.Exp,
                                           bias=m.small[:, 24 + i:25 + i], accum_out=m.small[:, 32 + i:33 + i])
        if sinks:
            last = self.isa.activation(m.small[:, 40:48], m.small[:, 48:56], ACT.Exp)
        last.then_inc(m.exped, 1)

    def softmax_heads(self, tile0, sinks=False):
        m = self.m
        self.exp_group(sinks)
        for h in range(8):
            self.eng.wait_ge(m.probs_turned, self.w.next(m.probs_turned))
            self.eng.wait_ge(m.weighed, self.w.reuse(m.weighed))
            self.isa.copy(m.probsT[:, h % 2, :], m.bank[4 + h % 2][:, 0:384]).then_inc(m.pt_ready, 1)
            if h >= 1:
                self.oT_high(h - 1, tile0)
            if h == 3:
                self.exp_group(sinks)
        self.oT_high(7, tile0)

    def oT_high(self, h, tile0):
        m = self.m
        if h % 2:
            self.eng.wait_ge(m.weighed, self.w.next(m.weighed, 2))
            self.isa.copy(m.oT_hi[:, tile0 + h // 2, :], m.bank[6 + (h // 2) % 2][:, 0:S]).then_inc(m.act_hi, 1)

    def stick_heads(self, tile0):
        m = self.m
        for step in range(8 + 3):
            if step < 8:
                a = m.probs[:, step % 4, :]
                self.settle()
                self.eng.wait_ge(m.to_act[step % 4], self.w.next(m.to_act[step % 4]))
                if step == 0:
                    self.eng.wait_ge(m.probs_free, self.w.next(m.probs_free))
                self.isa.activation(a, m.bank[step % 4][:, 0:384], ACT.Abs)
                self.settle()
                self.isa.activation(a, a, ACT.Exp, scale=-1.0)
                self.settle()
                self.isa.activation(a, a, ACT.Ln, bias=1.0).then_inc(m.l_ready, 1)
            if 2 <= step < 10:
                h = step - 2
                self.eng.wait_ge(m.logw_ready, self.w.next(m.logw_ready))
                self.eng.wait_ge(m.weighed, self.w.reuse(m.weighed))
                self.isa.activation(m.probsT[:, h % 2, :], m.probs[:, h % 4, :], ACT.Exp).then_inc(m.pt_ready, 1)
            if step >= 3:
                self.oT_high(step - 3, tile0)


class Vector(Engine):

    def settle(self):
        self.eng.drain()

    def split(self, n=1):
        m = self.m
        for _ in range(n):
            raw, slot, _, number = self.w.take()
            self.eng.wait_ge(m.hi_ready, number + 1)
            self.isa.tensor_tensor(m.w_lo[:, slot, :], m.raw[:, raw, :], m.w_hi[:, slot, :].bitcast(F32),
                                   ALU.subtract).then_inc(m.lo_ready, 1)

    def low_turned(self, banks, hi, lo, ready, scales=None, tiles=range(KT)):
        m = self.m
        for j, b in enumerate(banks):
            self.eng.wait_ge(m.act_hi, self.w.next(m.act_hi))
            for k in range(2 * j, min(2 * j + 2, len(tiles))):
                at = (k % 2) * S
                src = m.bank[b][:, at:at + S]
                h = hi[:, tiles[k], :].bitcast(F32)
                if scales is None:
                    last = self.isa.tensor_tensor(lo[:, tiles[k], :], src, h, ALU.subtract)
                else:
                    last = self.isa.scalar_tensor_tensor(lo[:, tiles[k], :], src, scales[:, k:k + 1], h,
                                                         ALU.mult, ALU.subtract)
            last.then_inc(m.free[b], 1)
        self.eng.drain().then_inc(ready, 1)

    def rms_rows(self, x, width, eps):
        m = self.m
        self.eng.wait_ge(m.squares, self.w.next(m.squares))
        self.isa.tensor_scalar(m.small[:, 2:4], m.small[:, 0:2], 1.0 / width, eps, ALU.mult, ALU.add) \
            .then_inc(m.rstd_in, 1)
        self.eng.wait_ge(m.rstd, self.w.next(m.rstd))
        for t in range(TT):
            last = self.isa.tensor_scalar(m.nat[:, t, :], x[:, t, :], m.small[:, 4 + t:5 + t], None, ALU.mult)
        last.then_inc(m.nat_ready, 1)

    def roped(self, b, tile, n, cos, sin, last_tiles=False):
        m = self.m
        self.settle()
        self.eng.wait_ge(m.to_dve[b], self.w.next(m.to_dve[b]))
        dst = m.arena[:, tile * S:(tile + n) * S].rearrange("p (n s) -> p n s", n=n)
        rot = m.bank[b][:, 0:n * S].rearrange("p (n s) -> p n s", n=n)
        tmp = m.probs[:, 0:2, 0:S][:, 0:n, :]
        c = cos.unsqueeze(1).to_broadcast([P, n, S])
        s = sin.unsqueeze(1).to_broadcast([P, n, S])
        self.isa.tensor_tensor(dst, dst, c, ALU.mult)
        self.isa.tensor_tensor(tmp, rot, s, ALU.mult).then_inc(m.free[b], 1)
        self.settle()
        self.isa.tensor_tensor(dst, dst, tmp, ALU.add).then_inc(m.roped, 1)

    def maxima(self, h, mask, first):
        m = self.m
        b, hh = h % 4, h % 4
        self.settle()
        self.eng.wait_ge(m.to_dve[b], self.w.next(m.to_dve[b]))
        self.eng.wait_ge(m.probs_turned, self.w.reuse(m.probs_turned))
        self.isa.memset(m.small[:, 10:11], 0.0)
        for t, a, e, mk in ((0, 0, P, mask[:, P:S]), (1, P, 384, mask)):
            i = 2 * hh + t
            last = self.isa.tensor_tensor_reduce(m.probs[:, hh, a:e], m.bank[b][:, a:e], mk, self.scale, first(h),
                                                 ALU.add, ALU.max, m.small[:, 16 + i:17 + i])
        last.then_inc(m.free[b], 1)

    def softmax_heads(self, tile0, mask, scale, sink=None):
        m = self.m
        self.scale = scale
        for g in range(2):
            for hh in range(4):
                self.maxima(4 * g + hh, mask, lambda h: NEG if sink is None else sink[:, h:h + 1])
            self.settle()
            if sink is not None:
                for t in range(TT):
                    pair = m.small[:, 48:56].rearrange("p (h t) -> p h t", t=TT)[:, :, t]
                    maxi = m.small[:, 16:24].rearrange("p (h t) -> p h t", t=TT)[:, :, t]
                    self.isa.tensor_tensor(pair, sink[:, 4 * g:4 * g + 4], maxi, ALU.subtract)
            self.isa.tensor_scalar(m.small[:, 24:32], m.small[:, 16:24], -1.0, None, ALU.mult)
            self.eng.drain().then_inc(m.negm, 1)
            self.eng.wait_ge(m.exped, self.w.next(m.exped))
            if sink is not None:
                self.isa.tensor_tensor(m.small[:, 32:40], m.small[:, 32:40], m.small[:, 40:48], ALU.add)
                self.settle()
            self.isa.reciprocal(m.small[:, 32:40], m.small[:, 32:40])
            self.settle()
            for hh in range(4):
                for t, a, b in ((0, 0, P), (1, P, 384)):
                    i = 2 * hh + t
                    last = self.isa.tensor_scalar(m.probs[:, hh, a:b], m.probs[:, hh, a:b],
                                                  m.small[:, 32 + i:33 + i], None, ALU.mult)
                last.then_inc(m.probs_ready, 1)
            if g:
                self.oT_low(0, tile0)
                self.oT_low(1, tile0)
        self.oT_low(2, tile0)
        self.oT_low(3, tile0)

    def oT_low(self, pair, tile0):
        m = self.m
        b = 6 + pair % 2
        self.eng.wait_ge(m.act_hi, self.w.next(m.act_hi))
        self.isa.tensor_tensor(m.oT_lo[:, tile0 + pair, :], m.bank[b][:, 0:S],
                               m.oT_hi[:, tile0 + pair, :].bitcast(F32), ALU.subtract).then_inc(m.free[b], 1)

    def stick_heads(self, tile0, neg):
        m = self.m
        self.settle()
        self.eng.wait_ge(m.probs_turned, self.w.all_free(m.probs_turned))
        self.isa.memset(m.small[:, 11:12], 0.0).then_inc(m.probs_free, 1)
        for step in range(8 + 3):
            if 1 <= step < 9:
                h = step - 1
                a = m.probs[:, h % 4, :]
                self.eng.wait_ge(m.l_ready, self.w.next(m.l_ready))
                self.isa.scalar_tensor_tensor(a, m.bank[h % 4][:, 0:384], 0.0, a, ALU.max, ALU.add) \
                    .then_inc(m.n_ready, 1)
            if 2 <= step < 10:
                h = step - 2
                self.eng.wait_ge(m.to_dve[h % 4], self.w.next(m.to_dve[h % 4]))
                self.isa.tensor_tensor(m.probs[:, h % 4, :], m.bank[h % 4][:, 0:384], neg, ALU.add) \
                    .then_inc(m.logw_ready, 1)
                self.eng.drain().then_inc(m.free[h % 4], 1)
            if step >= 5 and step % 2 == 1:
                self.oT_low((step - 5) // 2, tile0)
        self.oT_low(3, tile0)


class Pool(Engine):

    def power(self, a, b):
        m = self.m
        n = a[1] - a[0]
        self.eng.wait_ge(m.rstd_in, self.w.next(m.rstd_in))
        self.isa.tensor_tensor(m.small[:, b:b + n], m.small[:, a[0]:a[1]], m.small[:, HALF:HALF + n], ALU.pow) \
            .then_inc(m.rstd, 1)

    def stick_heads(self, before):
        m = self.m
        for h in range(8):
            a = m.probs[:, h % 4, :]
            self.eng.wait_ge(m.n_ready, self.w.next(m.n_ready))
            self.isa.tensor_tensor(a, a, before, ALU.mult).then_inc(m.lom_ready, 1)



A_QKV = [
    ("turned", QA, 4, 0), ("turned", QA + 2, 5, 1), ("k and v", KA, 6, 2),
    ("turned", QB, 7, None), ("turned", QB + 2, 4, None), ("turned", KB, 5, None), ("turned", KB + 2, 6, None),
    ("rows", P, (7, 4), None),
    ("turned", QC, 5, 3), ("turned", QC + 2, 6, 0), ("turned", KC, 7, 1), ("turned", KC + 2, 4, 2),
    ("rows", P + 512, (5, 6), None),
]
A_V = A_TILES * S
A_VW = P + 512 + 512
NORM_MIX, NORM_FFN, CONV, SINKS, A_PARAMS = 0, 8, 16, 16 + 16 * FF_SUBS, 24 + 16 * FF_SUBS


def a_tile(m, i, n=1):
    return m.arena[:, i * S:(i + n) * S]


def a_v(m, t, a, b):
    return m.arena[:, A_V + t * A_VW + a:A_V + t * A_VW + b]


class TensorA(Tensor):
    def layer(self):
        m, w = self.m, self.w
        ident, rot = m.tab(A_TABLES, "ident"), m.tab(A_TABLES, "rot64")
        hT = (m.hT_hi, m.hT_lo)
        oT = (m.oT_hi, m.oT_lo)
        self.eng.wait_ge(m.nat_ready, w.next(m.nat_ready))
        self.turn_rows(m.nat, (0, 1, 2, 3), ident)
        self.eng.wait_ge(m.hT_ready, w.next(m.hT_ready))

        def rotation(job):
            kind, tile, _, b = job
            if b is not None:
                n = 1 if kind == "k and v" else 2
                self.rotate(a_tile(m, tile, n), b, rot, n)

        for i, (kind, tile, b, _) in enumerate(A_QKV):
            if kind == "rows":
                banks = [self.bank(x) for x in b]
                for half in range(2):
                    last = self.rows(banks, self.chunk(), 512, hT, 4, 4 * half, KT)
                    if half == 0:
                        self.used(last)
                self.used(last)
            else:
                bank, c = self.bank(b), self.chunk()
                if kind == "turned":
                    last = self.turned([bank[:, 0:S], bank[:, S:2 * S]], c, S, hT, KT)
                else:
                    self.turned([bank[:, 0:S]], c, S, hT, KT)
                    for t in range(TT):
                        last = self.rows([bank[:, S + t * P:S + (t + 1) * P]], c, S, hT, KT, 0, KT, col=P, n=P, t0=t)
                self.used(last)
            if i:
                rotation(A_QKV[i - 1])
        rotation(A_QKV[-1])

        self.eng.wait_ge(m.roped, w.next(m.roped, 3))
        self.softmax_heads(
            lambda h: [(a_tile(m, QA + h % 4)[(h // 4) * DH:(h // 4 + 1) * DH, :],
                        a_tile(m, KA)[(h // 4) * DH:(h // 4 + 1) * DH, :])],
            lambda h: [a_v(m, t, (h // 4) * DH, (h // 4 + 1) * DH) for t in range(TT)], ident)
        self.eng.wait_ge(m.copied, w.next(m.copied, 6))
        self.stick_heads(
            lambda h: a_tile(m, QB + h // 2)[(h % 2) * DH:(h % 2 + 1) * DH, :],
            lambda h: a_tile(m, KB + h // 2)[(h % 2) * DH:(h % 2 + 1) * DH, :],
            lambda h: [a_v(m, t, P + h * DH, P + (h + 1) * DH) for t in range(TT)],
            m.tab(A_TABLES, "tri"), m.tab(A_TABLES, "ones"))
        self.eng.wait_ge(m.roped, w.next(m.roped, 4))
        self.eng.wait_ge(m.copied, w.next(m.copied, 2))
        self.softmax_heads(
            lambda h: [(a_tile(m, QC + h // 2)[(h % 2) * DH:(h % 2 + 1) * DH, :],
                        a_tile(m, KC + h // 2)[(h % 2) * DH:(h % 2 + 1) * DH, :])],
            lambda h: [a_v(m, t, P + 512 + h * DH, P + 512 + (h + 1) * DH) for t in range(TT)], ident)

        self.eng.wait_ge(m.oT_ready, w.next(m.oT_ready))
        for u in range(6):
            base = 4 * (u % 2)
            gates = [self.bank(base), self.bank(base + 1)]
            for half in range(2):
                self.used(self.rows(gates, self.chunk(), 512, hT, 4, 4 * half, KT))
            outs = [self.bank(base + 2), self.bank(base + 3)]
            branch = tuple(a[:, 4 * (u // 2):4 * (u // 2) + 4, :] for a in oT)
            self.used(self.rows(outs, self.chunk(), 512, branch, 4, 0, 4))
        self.eng.wait_ge(m.nat_ready, w.next(m.nat_ready))
        self.turn_rows(m.nat, (0, 1, 2, 3), ident)
        self.eng.wait_ge(m.hT_ready, w.next(m.hT_ready))
        self.project((2, 2, 1, 1, 1, 1))
        self.eng.wait_ge(m.nat_ready, w.next(m.nat_ready))
        self.turn_rows(m.nat, (0, 1, 2, 3), ident)
        self.eng.wait_ge(m.hT_ready, w.next(m.hT_ready))
        self.feed_forward()

    def project(self, tiles, x=None):
        m = self.m
        acc = [self.bank(b) for b in (4, 5, 6, 7)]
        k0 = 0
        for kt in tiles:
            c = self.chunk()
            for half in range(2):
                last = self.rows(acc[2 * half:2 * half + 2], c, D, x or (m.hT_hi, m.hT_lo), kt, k0, KT, col=512 * half)
            self.used(last)
            k0 += kt

    def up(self, p):
        m = self.m
        for b in (2 * p, 2 * p + 1):
            bank = self.bank(b)
            self.used(self.turned([bank[:, 0:S], bank[:, S:2 * S]], self.chunk(), S, (m.hT_hi, m.hT_lo), KT))

    def down(self, p, last_step=False):
        m = self.m
        self.eng.wait_ge(m.hid_ready, self.w.next(m.hid_ready))
        c = self.chunk()
        hid = (m.oT_hi[:, 2 * p:2 * p + 2, :], m.oT_lo[:, 2 * p:2 * p + 2, :])
        for half in range(2):
            last = self.rows([m.bank[4 + 2 * half], m.bank[5 + 2 * half]], c, D, hid, 2, 0, 2 if last_step else 3,
                             col=512 * half, opened=True)
        self.used(last)

    def feed_forward(self):
        m = self.m
        for b in (4, 5, 6, 7):
            self.zero(b)
        self.up(0)
        with self.w.repeat((FF_SUBS - 1) // 2, PE_FFN_TURN):
            for p in (1, 0):
                self.up(p)
                self.down(1 - p)
        self.down(0, last_step=True)


class ScalarA(Scalar):
    def layer(self):
        m = self.m
        self.eng.wait_ge(m.x_ready, self.w.next(m.x_ready))
        self.squares(m.x)
        self.high_turned((0, 1, 2, 3), m.hT_hi, m.cols[:, NORM_MIX:NORM_MIX + KT])
        for kind, tile, b, rot in A_QKV:
            if kind == "rows":
                self.split(2)
                self.eng.wait_ge(m.w_used, self.w.product_done())
                for t in range(TT):
                    self.copy_out(b[t], [(a_v(m, t, tile, tile + 512), m.bank[b[t]][:])], m.copied)
            elif kind == "turned":
                self.split(1)
                self.eng.wait_ge(m.w_used, self.w.product_done())
                self.copy_out(b, [(a_tile(m, tile, 2), m.bank[b][:])], m.kq_copied if rot is not None else m.copied,
                              SCALE if tile in (QB, QB + 2) else 1.0)
            else:
                self.split(1)
                self.eng.wait_ge(m.w_used, self.w.product_done())
                self.copy_out(b, [(a_tile(m, tile), m.bank[b][:, 0:S])]
                              + [(a_v(m, t, 0, P), m.bank[b][:, S + t * P:S + (t + 1) * P]) for t in range(TT)],
                              m.kq_copied)
        self.softmax_heads(0, sinks=True)
        self.stick_heads(4)
        self.softmax_heads(8)
        for u in range(6):
            self.split(2)
            for t in range(TT):
                self.eng.wait_ge(m.gate_in, self.w.next(m.gate_in))
                g = gate_rows(m, t)
                self.isa.activation(g, g, ACT.Sigmoid).then_inc(m.gate_out, 1)
            self.split(1)
        self.high_turned((0, 1, 2, 3), m.hT_hi)
        self.split(6)
        self.eng.wait_ge(m.x_ready, self.w.next(m.x_ready))
        self.squares(m.x)
        self.high_turned((0, 1, 2, 3), m.hT_hi, m.cols[:, NORM_FFN:NORM_FFN + KT])
        self.split(2)
        self.hidden(0)
        with self.w.repeat((FF_SUBS - 1) // 2, ACT_FFN_TURN):
            for p in (1, 0):
                self.split(2)
                self.hidden(p)
                self.split(1)
        self.split(1)

    def hidden(self, p):
        m = self.m
        self.eng.wait_ge(m.silu_in, self.w.next(m.silu_in))
        g = hidden_gate(m)
        self.isa.activation(g, g, ACT.Silu).then_inc(m.silu_done, 1)
        self.eng.wait_ge(m.hid, self.w.next(m.hid))
        self.isa.copy(m.oT_hi[:, 2 * p:2 * p + 2, :], hidden_value(m)).then_inc(m.hid_hi, 1)


def gate_rows(m, t):
    return m.probs[:, :, :].rearrange("p a b -> p (a b)")[:, t * 512:(t + 1) * 512]


def hidden_gate(m):
    return m.probs[:, :, :].rearrange("p a b -> p (a b)")[:, 0:512]


def hidden_value(m):
    return m.probs[:, :, :].rearrange("p a b -> p (a b)")[:, 512:1024].rearrange("p (a b) -> p a b", a=2)


class VectorA(Vector):
    def layer(self, layer):
        m, w = self.m, self.w
        self.isa.tensor_copy(m.cols[:, 0:A_PARAMS], m.all_cols[:, bass.ds(layer * A_PARAMS, A_PARAMS)]) \
            .then_inc(m.cols_ready, 1)
        sinks = m.cols[:, SINKS:SINKS + 8]
        self.rms_rows(m.x, D, 1e-6)
        self.low_turned((0, 1, 2, 3), m.hT_hi, m.hT_lo, m.hT_ready, m.cols[:, NORM_MIX:NORM_MIX + KT])
        cos, sin = m.tab(A_TABLES, "cos64"), m.tab(A_TABLES, "sin64")

        def rope(job):
            kind, tile, _, b = job
            if b is not None:
                self.roped(b, tile, 1 if kind == "k and v" else 2, cos, sin)

        for i, job in enumerate(A_QKV):
            self.split(2 if job[0] == "rows" else 1)
            if i:
                rope(A_QKV[i - 1])
        rope(A_QKV[-1])
        self.softmax_heads(0, m.tab(A_TABLES, "band"), SCALE, sinks)
        self.stick_heads(4, m.tab(A_TABLES, "before"))
        self.softmax_heads(8, m.tab(A_TABLES, "causal"), SCALE)
        self.eng.drain().then_inc(m.oT_ready, 1)
        self.eng.wait_ge(m.probs_turned, w.all_free(m.probs_turned))
        self.eng.wait_ge(m.rows_loaded, w.next(m.rows_loaded, 16))
        for u in range(6):
            i, half, base = u // 2, u % 2, 4 * (u % 2)
            bias = m.arena[:, i * D + 512 * half:i * D + 512 * half + 512]
            self.split(2)
            self.settle()
            self.eng.wait_ge(m.w_used, self.w.product_done())
            for t in range(TT):
                self.isa.tensor_tensor(gate_rows(m, t), m.bank[base + t][:], bias, ALU.add).then_inc(m.gate_in, 1)
                self.eng.drain().then_inc(m.free[base + t], 1)
            self.split(1)
            self.eng.wait_ge(m.w_used, self.w.product_done())
            for t in range(TT):
                self.eng.wait_ge(m.gate_out, w.next(m.gate_out))
                out = m.nat[:, t, 512 * half:512 * half + 512]
                dst = gate_rows(m, t) if i else out
                self.isa.tensor_tensor(dst, gate_rows(m, t), m.bank[base + 2 + t][:], ALU.mult) \
                    .then_inc(m.free[base + 2 + t], 1)
                if i:
                    self.settle()
                    self.isa.tensor_tensor(out, out, dst, ALU.add)
        self.eng.drain().then_inc(m.nat_ready, 1)
        self.low_turned((0, 1, 2, 3), m.hT_hi, m.hT_lo, m.hT_ready)
        self.split(6)
        self.add_banks()
        self.rms_rows(m.x, D, 1e-6)
        self.low_turned((0, 1, 2, 3), m.hT_hi, m.hT_lo, m.hT_ready, m.cols[:, NORM_FFN:NORM_FFN + KT])
        self.hidden(0, 0)
        with w.repeat((FF_SUBS - 1) // 2, DVE_FFN_TURN) as i:
            for n, p in enumerate((1, 0)):
                self.hidden(p, i * 2 + (n + 1))
                self.split(1)
        self.split(1)
        self.add_banks()

    def add_banks(self):
        m = self.m
        self.eng.wait_ge(m.w_used, self.w.product_done())
        for half in range(2):
            for t in range(TT):
                b = 4 + 2 * half + t
                x = m.x[:, t, 512 * half:512 * half + 512]
                self.isa.tensor_tensor(x, x, m.bank[b][:], ALU.add).then_inc(m.free[b], 1)
        self.eng.drain().then_inc(m.x_ready, 1)

    def conv(self, bank, dst, at):
        m = self.m

        def col(g, i):
            if type(at) is int:
                return m.cols[:, at + 4 * g + i:at + 4 * g + i + 1]
            return m.cols[:, bass.ds(at + (4 * g + i), 1)]

        for g in range(2):
            src = bank[:, g * S:(g + 1) * S]
            self.isa.tensor_scalar(dst[:, g, :], src, col(g, 2), col(g, 3), ALU.mult, ALU.add)
        for back in (1, 2):
            self.settle()
            for g in range(2):
                out = dst[:, g, back:S]
                last = self.isa.scalar_tensor_tensor(out, bank[:, g * S:(g + 1) * S - back], col(g, 2 - back), out,
                                                     ALU.mult, ALU.add)
        return last

    def hidden(self, p, j):
        m = self.m
        gate = hidden_gate(m).rearrange("p (a b) -> p a b", a=2)
        value = hidden_value(m)
        for b, dst, half in ((2 * p, gate, 0), (2 * p + 1, value, 1)):
            self.split(1)
            self.settle()
            self.eng.wait_ge(m.w_used, self.w.product_done())
            last = self.conv(m.bank[b], dst, j * 16 + (CONV + 8 * half))
            last.then_inc(m.silu_in if half == 0 else m.free[b], 1)
            if half == 0:
                self.eng.drain().then_inc(m.free[b], 1)
        self.settle()
        self.eng.wait_ge(m.silu_done, self.w.next(m.silu_done))
        self.isa.tensor_tensor(value, value, gate, ALU.mult).then_inc(m.hid, 1)
        self.eng.wait_ge(m.hid_hi, self.w.next(m.hid_hi))
        self.isa.tensor_tensor(m.oT_lo[:, 2 * p:2 * p + 2, :], value, m.oT_hi[:, 2 * p:2 * p + 2, :].bitcast(F32),
                               ALU.subtract).then_inc(m.hid_ready, 1)



RQ, RK, KR, MQ, MK, QN, QR, KN, B_TILES = 0, 2, 4, 5, 7, 9, 13, 15, 19
B_RV = B_TILES * S
B_VA = B_RV + TT * S
B_VM = B_VA + TT * 4 * (DH + 1)
B_ROWS = B_VM + TT * 512
B_EXP = 0
B_MIXER = 17
UNIT = 6 * EXP_STEPS
FIXED = DEPTH * (A_LAYER + B_MIXER) + 3 * FF_SUBS + 1
SHARED = B_TABLES["rot32"][0]
ALPHA = (2 * DEPTH) ** 0.25

LN1, LN2 = 0, 2 * D
QKV_NORM, GN, CONV4, BIAS_I, BIAS_F, B_PARAMS = 0, 3, 7, 27, 28, 29
ST, MV, VAR, RSTD8 = 96, 80, 64, 72
CSS, CMS, CRS = 144, 148, 152
AT, EN, DEN = 156, 164, 172
LG = 180


def b_tile(m, i, n=1):
    return m.arena[:, i * S:(i + n) * S]


def gate_row(m, i):
    if i < 2:
        return m.arena[0:4, B_ROWS + i * S:B_ROWS + (i + 1) * S]
    return m.probsT[0:4, i - 2, 0:S]


def r_v(m, t):
    return m.arena[:, B_RV + t * S:B_RV + (t + 1) * S]


def v_aug(m, t):
    w = 4 * (DH + 1)
    return m.arena[:, B_VA + t * w:B_VA + (t + 1) * w].rearrange("p (h d) -> p h d", h=4)


def v_mla(m, t, a=0, b=512):
    return m.arena[:, B_VM + t * 512 + a:B_VM + t * 512 + b]


def by_head(ap, h=4):
    return ap.rearrange("p (h d) -> p h d", h=h)


class TensorB(TensorA):
    def mixer(self):
        m, w = self.m, self.w
        ident = m.tab(B_TABLES, "ident")
        rot64, rot32 = m.tab(B_TABLES, "rot64"), m.tab(B_TABLES, "rot32")
        hT = (m.hT_hi, m.hT_lo)
        self.eng.wait_ge(m.nat_ready, w.next(m.nat_ready))
        self.turn_rows(m.x, (0, 1, 2, 3), ident)
        self.eng.wait_ge(m.hT_ready, w.next(m.hT_ready))

        def two_tiles(b):
            bank = self.bank(b)
            self.used(self.turned([bank[:, 0:S], bank[:, S:2 * S]], self.chunk(), S, hT, KT))

        def two_chunks(b, n):
            banks = [self.bank(b)[:, 0:n], self.bank(b + 1)[:, 0:n]]
            for half in range(2):
                self.used(self.rows(banks, self.chunk(), n, hT, 4, 4 * half, KT, n=n))

        two_tiles(4)
        two_tiles(5)
        self.rotate(b_tile(m, RQ, 2), 0, rot64, 2)
        c, keys, gates = self.chunk(), self.bank(6), self.bank(7)
        self.turned([keys[:, 0:S]], c, P + 8, hT, KT)
        self.turned([gates[0:4, 0:S]], c, P + 8, hT, KT, col=P, m=4)
        self.used(self.turned([gates[0:4, S:2 * S]], c, P + 8, hT, KT, col=P + 4, m=4))
        self.rotate(b_tile(m, RK, 2), 1, rot64, 2)
        two_chunks(4, 512)
        self.rotate(b_tile(m, KR), 2, rot32, 1)
        two_chunks(6, 384)
        two_tiles(0)
        two_tiles(1)
        two_chunks(4, 512)
        self.eng.wait_ge(m.nat_ready, w.next(m.nat_ready))
        self.turn_rows(m.probs[:, 2:4, :], (2, 3), ident, 3)
        self.eng.wait_ge(m.hT_ready, w.next(m.hT_ready))
        c = self.chunk()
        cq, ckv = ((m.oT_hi[:, a:b, :], m.oT_lo[:, a:b, :]) for a, b in ((8, 10), (10, 11)))
        outs = []
        for b in (6, 7, 0):
            bank = self.bank(b)
            outs += [bank[:, 0:S], bank[:, S:2 * S]]
        self.used(self.turned(outs, c, 768, cq, 2))
        c, outs = self.chunk(), []
        for b in (2, 3):
            bank = self.bank(b)
            outs += [bank[:, 0:S], bank[:, S:2 * S]]
        self.turned(outs, c, D, ckv, 1)
        self.used(self.rows([self.bank(4), self.bank(5)], c, D, ckv, 1, 0, 1, col=512))
        self.rotate(b_tile(m, QR, 2), 1, rot32, 2)

        self.eng.wait_ge(m.scans_ready, w.next(m.scans_ready))
        bank = self.bank(0)
        for i, row in enumerate((gate_row(m, 2), gate_row(m, 0))):
            for t in range(TT):
                last = self.isa.transpose(bank[:, 8 * i + 4 * t:8 * i + 4 * t + 4], row[:, t * P:(t + 1) * P],
                                          ident[0:4, 0:4])
        last.then_inc(m.to_dve[0], 1)

        self.eng.wait_ge(m.roped, w.next(m.roped, 2))
        self.eng.wait_ge(m.copied, w.next(m.copied, 2))
        self.key_rows(RQ, RK)
        self.out_rows(lambda t, h: r_v(m, t)[:, h * DH:(h + 1) * DH], DH)
        self.eng.wait_ge(m.conv_out, w.next(m.conv_out, 2))
        for h in range(4):
            pick = ident[0:4, h:h + 1].to_broadcast([4, P])
            bank = self.bank(4 + h)
            mm = self.isa.matmul
            mm(bank[:, 0:S], pick, gate_row(m, 3), start=True, stop=False, skip_group_check=True)
            mm(bank[:, S:S + P], pick, gate_row(m, 3)[:, P:S], start=False, stop=False, skip_group_check=True)
            for at in (0, S):
                last = mm(bank[:, at:at + P], ident, m.tab(B_TABLES, "causalT"), start=False, stop=at == S,
                          skip_group_check=True)
            last.then_inc(m.to_act[4 + h], 1)
        self.key_rows(MQ, MK)
        self.eng.wait_ge(m.copied, w.next(m.copied, 2))
        self.out_rows(lambda t, h: v_aug(m, t)[:, h, :], DH + 1)

        self.eng.wait_ge(m.roped, w.next(m.roped, 2))
        self.eng.wait_ge(m.copied, w.next(m.copied, 6))
        self.softmax_heads(
            lambda h: [(b_tile(m, a + h // 2)[(h % 2) * DH:(h % 2 + 1) * DH, :],
                        b_tile(m, b + h // 2)[(h % 2) * DH:(h % 2 + 1) * DH, :]) for a, b in ((QN, KN),)]
            + [(b_tile(m, QR + h // 4)[(h % 4) * 32:(h % 4 + 1) * 32, :],
                b_tile(m, KR)[(h % 4) * 32:(h % 4 + 1) * 32, :])],
            lambda h: [v_mla(m, t, h * DH, (h + 1) * DH) for t in range(TT)], ident)
        self.eng.wait_ge(m.nat_ready, w.next(m.nat_ready))
        self.turn_rows(m.nat[:, :, 0:512], (0, 1), ident, 4)
        self.eng.wait_ge(m.hT_ready, w.next(m.hT_ready))
        self.project((2, 2, 2, 2), (m.oT_hi, m.oT_lo))

    def key_rows(self, q, k):
        m = self.m
        for h in range(4):
            bank = self.bank(h)
            qh, kh = (b_tile(m, x + h // 2)[(h % 2) * DH:(h % 2 + 1) * DH, :] for x in (q, k))
            self.isa.matmul(bank[:, 0:S], kh[:, 0:P], qh, start=True, stop=False, skip_group_check=True)
            self.isa.matmul(bank[:, S:S + P], kh[:, P:S], qh[:, P:S], start=False, stop=True,
                            skip_group_check=True).then_inc(m.to_dve[h], 1)

    def out_rows(self, v_of, n):
        m = self.m
        banks = [self.bank(4), self.bank(5)]
        for h in range(4):
            self.eng.wait_ge(m.pairs_ready, self.w.next(m.pairs_ready))
            pt = m.probs[:, h, :]
            at = slice(h * n, (h + 1) * n)
            mm = self.isa.matmul
            first = mm(banks[0][:, at], pt[:, 0:P], v_of(0, h), start=True, stop=True, skip_group_check=True)
            mm(banks[1][:, at], pt[:, P:S], v_of(0, h), start=True, stop=False, skip_group_check=True)
            last = mm(banks[1][:, at], pt[:, S:S + P], v_of(1, h), start=False, stop=True, skip_group_check=True)
        first.then_inc(m.to_dve[4], 1)
        last.then_inc(m.to_dve[5], 1)

    def route(self):
        m, w = self.m, self.w
        logits = [self.bank(b)[:, 0:N_EXP] for b in range(TT)]
        self.used(self.rows(logits, self.chunk(), N_EXP, (m.hT_hi, m.hT_lo), KT, 0, KT, n=N_EXP))
        self.eng.wait_ge(m.selected, w.next(m.selected))
        bank = self.bank(2)
        below, ones = m.tab(B_TABLES, "below"), m.tab(B_TABLES, "ones")
        sel = [chosen(m, t) for t in range(TT)]
        mm = self.isa.matmul
        mm(bank[:, 0:8], below, sel[0], start=True, stop=True, skip_group_check=True)
        mm(bank[:, 8:16], ones, sel[0], start=True, stop=False, skip_group_check=True)
        mm(bank[:, 8:16], below, sel[1], start=False, stop=True, skip_group_check=True)
        mm(bank[:, 16:24], ones, sel[0], start=True, stop=False, skip_group_check=True)
        mm(bank[:, 16:24], ones, sel[1], start=False, stop=True, skip_group_check=True).then_inc(m.placed, 1)

    def experts(self):
        m, w = self.m, self.w
        self.eng.wait_ge(m.units_ready, w.next(m.units_ready))
        units = self.isa.value_load(m.units[0:1, COUNT:COUNT + 1], min_val=8, max_val=11)
        self.gather()
        self.eng.wait_ge(m.x_here, w.next(m.x_here))
        with w.repeat(units, PE_UNIT):
            self.rows_up(0)
            self.rows_up(1)
            for b in (4, 5):
                self.zero(b)
            self.scatter()
            self.turn_picks()
            with w.repeat(EXP_STEPS - 1, PE_STEP):
                self.rows_up(0)
                self.turn_hidden()
                self.rows_up(1)
                self.rows_down()
            self.turn_hidden()
            self.gather()
            self.rows_down(last_step=True)
            self.eng.wait_ge(m.x_here, w.next(m.x_here))
        self.scatter()

    def gather(self):
        m = self.m
        self.eng.wait_ge(m.picks_ready, self.w.next(m.picks_ready))
        for j, b in enumerate((6, 7)):
            bank = self.bank(b)
            for k in range(4 * j, 4 * j + 4):
                for t in range(TT):
                    last = self.isa.matmul(bank[:, (k % 4) * P:(k % 4 + 1) * P], m.x[:, t, k * P:(k + 1) * P],
                                           picks(m, t), start=t == 0, stop=t == TT - 1, skip_group_check=True)
            last.then_inc(m.to_act[b], 1)

    def rows_up(self, b):
        m = self.m
        bank = self.bank(b)
        for half in range(2):
            self.used(self.rows([bank], self.chunk(), 512, (m.hT_hi, m.hT_lo), 4, 4 * half, KT))

    def turn_hidden(self):
        m = self.m
        self.eng.wait_ge(m.h_rows, self.w.next(m.h_rows))
        bank = self.bank(2)
        for k in range(4):
            last = self.isa.transpose(bank[:, k * P:(k + 1) * P], h_rows(m)[:, k * P:(k + 1) * P],
                                      m.tab(B_TABLES, "ident"))
        last.then_inc(m.to_act[2], 1)

    def rows_down(self, last_step=False):
        m = self.m
        self.eng.wait_ge(m.hid_ready, self.w.next(m.hid_ready))
        for c in range(2):
            chunk = self.chunk()
            hid = tuple(a[:, 2 * c:2 * c + 2, 0:P] for a in (m.oT_hi, m.oT_lo))
            for half in range(2):
                last = self.rows([m.bank[4 + half]], chunk, D, hid, 2, 0, 2 if last_step and c else 3,
                                 col=512 * half, opened=True)
            self.used(last)

    def turn_picks(self):
        m = self.m
        bank = self.bank(6)
        for t in range(TT):
            last = self.isa.transpose(bank[:, t * P:(t + 1) * P], weighted(m, t), m.tab(B_TABLES, "ident"))
        last.then_inc(m.to_dve[6], 1)

    def scatter(self):
        m = self.m
        self.eng.wait_ge(m.y_rows, self.w.next(m.y_rows))
        for t, banks in ((0, (6, 7)), (1, (3, 2))):
            for half, b in enumerate(banks):
                self.isa.matmul(self.bank(b), picksT(m)[:, t * P:(t + 1) * P], y_rows(m)[:, 512 * half:512 * half + 512],
                                start=True, stop=True).then_inc(m.to_dve[b], 1)


def arena_part(at, n):
    return lambda m, t=0: m.arena[:, at + t * n:at + (t + 1) * n]


picks, weighted, picksT = arena_part(0, P), arena_part(2 * P, P), arena_part(4 * P, S)
g_rows, h_rows = arena_part(768, 512), arena_part(1280, 512)
UPOS, UGATE, ROUTE = 4 * D, 4 * D + 24, 4 * D + 48


def y_rows(m):
    return m.probs[:, :, :].rearrange("p a b -> p (a b)")[:, 0:D]


def route_part(m, i, n=16):
    return m.arena[:, ROUTE + 16 * i:ROUTE + 16 * i + n]


def chosen(m, t):
    return route_part(m, 0)[:, 8 * t:8 * t + 8]


class ScalarB(ScalarA):
    def mixer(self, layer):
        m, w = self.m, self.w
        par = m.all_cols[:, layer * B_PARAMS:(layer + 1) * B_PARAMS]
        self.high_turned((0, 1, 2, 3), m.hT_hi)
        for tile, b, n in ((RQ, 4, 2), (RK, 5, 2), (KR, 6, 1)):
            self.split(1)
            self.eng.wait_ge(m.w_used, self.w.product_done())
            self.copy_out(b, [(b_tile(m, tile, n), m.bank[b][:, 0:n * S])], m.kq_copied)
        self.split(2)
        self.eng.wait_ge(m.w_used, self.w.product_done())
        for t in range(TT):
            self.isa.activation(r_v(m, t), m.bank[4 + t][:, 0:S], ACT.Copy)
            self.isa.activation(m.nat[:, t, 512:768], m.bank[4 + t][:, S:2 * S], ACT.Silu).then_inc(m.free[4 + t], 1)
            self.eng.drain().then_inc(m.copied, 1)
        self.split(2)
        self.eng.wait_ge(m.w_used, self.w.product_done())
        for t in range(TT):
            c = m.probs[:, 2 + t, :]
            self.isa.activation(c, m.bank[6 + t][:, 0:384], ACT.Copy)
            self.settle()
            self.isa.activation(m.bank[6 + t][:, 0:S], c[:, 0:S], ACT.Square, accum_out=m.small[:, CSS + t:CSS + t + 1])
            self.isa.activation(m.bank[6 + t][:, S:S + P], c[:, S:S + P], ACT.Square,
                                accum_out=m.small[:, CSS + 2 + t:CSS + 3 + t])
            self.eng.drain().then_inc(m.free[6 + t], 1)
        self.eng.drain().then_inc(m.squares, 1)
        self.split(2)
        z, l = gate_row(m, 0), gate_row(m, 1)
        self.eng.wait_ge(m.z_ready, w.next(m.z_ready))
        self.isa.activation(l, z, ACT.Abs)
        self.settle()
        self.isa.activation(l, l, ACT.Exp, scale=-1.0)
        self.settle()
        self.isa.activation(l, l, ACT.Ln, bias=1.0).then_inc(m.l_ready, 1)
        for tile in (MQ, MK):
            self.eng.wait_ge(m.conv_in, w.next(m.conv_in))
            self.isa.activation(b_tile(m, tile, 2), b_tile(m, tile, 2), ACT.Silu).then_inc(m.conv_out, 1)
        self.split(2)
        self.eng.wait_ge(m.w_used, self.w.product_done())
        for t in range(TT):
            self.isa.activation(v_aug(m, t)[:, :, 0:DH], by_head(m.bank[4 + t][:, 0:S]), ACT.Copy)
            self.isa.activation(m.nat[:, t, 768:D], m.bank[4 + t][:, S:2 * S], ACT.Sigmoid).then_inc(m.free[4 + t], 1)
            self.eng.drain().then_inc(m.copied, 1)
        self.high_turned((2, 3), m.oT_hi, par[:, QKV_NORM:QKV_NORM + 3], (8, 9, 10))
        self.split(1)
        self.eng.wait_ge(m.w_used, self.w.product_done())
        for b, tile, to in ((6, QN, m.copied), (7, QN + 2, m.copied), (0, QR, m.kq_copied)):
            self.copy_out(b, [(b_tile(m, tile, 2), m.bank[b])], to)
        self.split(1)
        self.eng.wait_ge(m.w_used, self.w.product_done())
        for b, tile in ((2, KN), (3, KN + 2)):
            self.copy_out(b, [(b_tile(m, tile, 2), m.bank[b])], m.copied)
        for t in range(TT):
            self.copy_out(4 + t, [(v_mla(m, t), m.bank[4 + t])], m.copied)
        self.eng.wait_ge(m.cols_turned, w.next(m.cols_turned))
        w.skip(m.pairs_ready, 4)
        self.isa.activation(m.small[:, EN:EN + 8], m.small[:, EN:EN + 8], ACT.Exp)
        for h in range(4):
            if h >= 2:
                self.settle()
                self.eng.wait_ge(m.pairs_ready, w.next(m.pairs_ready))
            self.eng.wait_ge(m.to_act[4 + h], w.next(m.to_act[4 + h]))
            e = decays(m, h)
            for a, b, t in ((0, S, 0), (S, 384, 1)):
                last = self.isa.activation(e[:, a:b], m.bank[4 + h][:, a:b], ACT.Exp, scale=-1.0,
                                           bias=m.small[:, AT + 4 * t + h:AT + 4 * t + h + 1])
            last.then_inc(m.free[4 + h], 1)
            self.eng.drain().then_inc(m.decay_ready, 1)
        w.skip(m.pairs_ready, 2)
        self.softmax_heads(2)
        self.high_turned((0, 1), m.oT_hi, par[:, GN:GN + 4], (0, 1, 6, 7))
        self.split(4)

    def feed_forward(self):
        m, w = self.m, self.w
        self.high_turned((0, 1, 2, 3), m.hT_hi)
        self.hidden(0)
        with w.repeat((FF_SUBS - 1) // 2, ACT_SWIGLU_TURN):
            for p in (1, 0):
                self.hidden(p)
                self.split(1)
        self.split(1)

    def hidden(self, p):
        m = self.m
        self.split(1)
        self.settle()
        self.eng.wait_ge(m.w_used, self.w.product_done())
        self.isa.activation(hidden_gate(m), m.bank[2 * p], ACT.Silu).then_inc(m.silu_done, 1)
        self.eng.drain().then_inc(m.free[2 * p], 1)
        self.split(1)
        self.eng.wait_ge(m.hid, self.w.next(m.hid))
        self.isa.copy(m.oT_hi[:, 2 * p:2 * p + 2, :], hidden_value(m)).then_inc(m.hid_hi, 1)

    def experts(self):
        m, w = self.m, self.w
        self.high_turned((0, 1, 2, 3), m.hT_hi)
        self.split(1)
        self.eng.wait_ge(m.d_ready, w.next(m.d_ready))
        d = route_part(m, 10, 2)
        self.isa.activation(d, d, ACT.Exp).then_inc(m.e_ready, 1)
        self.eng.wait_ge(m.units_ready, w.next(m.units_ready))
        units = self.isa.value_load(m.units[0:1, COUNT:COUNT + 1], min_val=8, max_val=11)
        self.gathered()
        with w.repeat(units, ACT_UNIT):
            self.split(2)
            self.gate_rows()
            self.split(2)
            with w.repeat(EXP_STEPS - 1, ACT_STEP):
                self.split(2)
                self.gate_rows()
                self.hidden_turned()
                self.split(4)
            self.hidden_turned()
            self.gathered()
            self.split(2)
            self.eng.wait_ge(m.w_used, self.w.product_done())
            for half in range(2):
                self.isa.activation(y_rows(m)[:, 512 * half:512 * half + 512], m.bank[4 + half], ACT.Copy) \
                    .then_inc(m.free[4 + half], 1)
            self.eng.drain().then_inc(m.y_rows, 1)

    def gate_rows(self):
        m = self.m
        self.eng.wait_ge(m.h_rows, self.w.reuse(m.h_rows))
        self.eng.wait_ge(m.w_used, self.w.product_done())
        self.isa.activation(g_rows(m), m.bank[0], ACT.Silu).then_inc(m.silu_done, 1)
        self.eng.drain().then_inc(m.free[0], 1)

    def hidden_turned(self):
        m = self.m
        self.eng.wait_ge(m.to_act[2], self.w.next(m.to_act[2]))
        self.isa.copy(m.oT_hi[:, 0:4, 0:P], by_head(m.bank[2])).then_inc(m.hid_hi, 1)

    def gathered(self):
        m = self.m
        for j, b in enumerate((6, 7)):
            self.eng.wait_ge(m.to_act[b], self.w.next(m.to_act[b]))
            self.isa.copy(m.hT_hi[:, 4 * j:4 * j + 4, 0:P], by_head(m.bank[b])).then_inc(m.act_hi, 1)


def decays(m, h):
    return m.arena[:, B_EXP + (h % 2) * 512:B_EXP + (h % 2) * 512 + 384]


class VectorB(VectorA):
    def normed_start(self):
        m = self.m
        self.rms_rows(m.x, D, 1e-6)
        self.eng.wait_ge(m.rows_loaded, self.w.next(m.rows_loaded, 16))
        self.settle()
        for t in range(TT):
            self.isa.tensor_tensor(m.x[:, t, :], m.nat[:, t, :], m.arena[:, 0:D], ALU.mult)
            self.isa.memset(v_aug(m, t)[:, :, DH], 1.0)
        self.eng.drain().then_inc(m.nat_ready, 1)

    def mixer(self, layer):
        m, w = self.m, self.w
        par = m.all_cols[:, layer * B_PARAMS:(layer + 1) * B_PARAMS]
        self.low_turned((0, 1, 2, 3), m.hT_hi, m.hT_lo, m.hT_ready)
        cos64, sin64 = m.tab(B_TABLES, "cos64"), m.tab(B_TABLES, "sin64")
        cos32, sin32 = m.tab(B_TABLES, "cos32"), m.tab(B_TABLES, "sin32")
        self.split(3)
        self.eng.wait_ge(m.w_used, self.w.product_done())
        gates = m.bank[7][0:4, :]
        self.isa.tensor_scalar(gate_row(m, 2), gates[:, 0:S], par[0:4, BIAS_I:BIAS_I + 1], None, ALU.add)
        self.isa.tensor_scalar(gate_row(m, 0), gates[:, S:2 * S], par[0:4, BIAS_F:BIAS_F + 1], None, ALU.add) \
            .then_inc(m.free[7], 1)
        self.eng.drain().then_inc(m.z_ready, 1)
        self.roped(0, RQ, 2, cos64, sin64)
        self.split(2)
        self.roped(1, RK, 2, cos64, sin64)
        self.split(2)
        self.roped(2, KR, 1, cos32, sin32)
        self.eng.wait_ge(m.squares, w.next(m.squares))
        self.isa.tensor_scalar(m.small[:, CMS:CMS + 2], m.small[:, CSS:CSS + 2], 1 / 256, 1e-5, ALU.mult, ALU.add)
        self.isa.tensor_scalar(m.small[:, CMS + 2:CMS + 4], m.small[:, CSS + 2:CSS + 4], 1 / P, 1e-5, ALU.mult, ALU.add)
        self.eng.drain().then_inc(m.rstd_in, 1)
        self.eng.wait_ge(m.rstd, w.next(m.rstd))
        for t in range(TT):
            c = m.probs[:, 2 + t, :]
            for a, b, i in ((0, S, t), (S, 384, 2 + t)):
                self.isa.tensor_scalar(c[:, a:b], c[:, a:b], m.small[:, CRS + i:CRS + i + 1], None, ALU.mult)
        self.eng.drain().then_inc(m.nat_ready, 1)
        for tile, b in ((MQ, 0), (MK, 1)):
            self.split(1)
            self.settle()
            self.eng.wait_ge(m.w_used, self.w.product_done())
            self.conv4(m.bank[b], b_tile(m, tile, 2), par[:, CONV4 + 5 * (tile - MQ):CONV4 + 5 * (tile - MQ) + 10])
            self.eng.drain().then_inc(m.free[b], 1)
        r0, r1, r2, r3 = (gate_row(m, i) for i in range(4))
        self.isa.tensor_scalar(m.small[0:4, 11:12], m.small[0:4, 11:12], 0.0, None, ALU.mult)
        self.eng.wait_ge(m.l_ready, w.next(m.l_ready))
        self.isa.tensor_scalar(r0, r0, -1.0, 0.0, ALU.mult, ALU.max)
        self.settle()
        self.isa.tensor_tensor(r0, r0, r1, ALU.add)
        self.settle()
        one = m.tab(B_TABLES, "ones")[0:4, 0:1].to_broadcast([4, S])
        self.isa.tensor_tensor_scan(r1, one, r0, 0.0, ALU.mult, ALU.add)
        self.settle()
        self.isa.tensor_tensor(r2, r2, r1, ALU.add)
        self.settle()
        self.isa.tensor_tensor_scan(r3, r2, r2, NEG, ALU.max, ALU.max)
        self.settle()
        self.isa.tensor_tensor(r0, r1, r3, ALU.subtract)
        self.eng.drain().then_inc(m.scans_ready, 1)
        self.split(2)
        self.low_turned((2, 3), m.oT_hi, m.oT_lo, m.hT_ready, par[:, QKV_NORM:QKV_NORM + 3], (8, 9, 10))
        self.split(2)
        self.roped(1, QR, 2, cos32, sin32)
        self.eng.wait_ge(m.to_dve[0], w.next(m.to_dve[0]))
        self.isa.tensor_copy(m.small[:, AT:AT + 16], m.bank[0][:, 0:16]).then_inc(m.free[0], 1)
        self.eng.drain().then_inc(m.cols_turned, 1)

        for h in range(4):
            self.eng.wait_ge(m.to_dve[h], w.next(m.to_dve[h]))
            if h == 0:
                self.eng.wait_ge(m.probs_turned, w.all_free(m.probs_turned))
            decay = m.tab(B_TABLES, "decay", h * S, (h + 1) * S)
            self.isa.tensor_tensor(m.probs[:, h, 0:S], m.bank[h][:, 0:S], decay, ALU.mult)
            self.isa.tensor_tensor(m.probs[:, h, S:384], m.bank[h][:, S:384], decay[:, 0:P], ALU.mult) \
                .then_inc(m.free[h], 1)
            self.eng.drain().then_inc(m.pairs_ready, 1)
        for t in range(TT):
            self.eng.wait_ge(m.to_dve[4 + t], w.next(m.to_dve[4 + t]))
            self.head_stats(t, by_head(m.bank[4 + t][:, 0:S]))
        self.head_norm(lambda t: by_head(m.bank[4 + t][:, 0:S]), 0)
        for t in range(TT):
            self.isa.tensor_tensor(m.nat[:, t, 0:S], m.nat[:, t, 0:S], m.nat[:, t, 512:768], ALU.mult) \
                .then_inc(m.free[4 + t], 1)
        for h in range(4):
            self.settle()
            self.eng.wait_ge(m.decay_ready, w.next(m.decay_ready))
            self.eng.wait_ge(m.to_dve[h], w.next(m.to_dve[h]))
            self.isa.scalar_tensor_tensor(m.probs[:, h, :], m.bank[h][:, 0:384], SCALE, decays(m, h),
                                          ALU.mult, ALU.mult).then_inc(m.pairs_ready, 1)
            self.eng.drain().then_inc(m.free[h], 1)
        for t in range(TT):
            out = by_head(m.bank[4 + t][:, 0:4 * (DH + 1)])
            den = out[:, :, DH]
            e = m.small[:, EN + 4 * t:EN + 4 * t + 4]
            d = m.small[:, DEN + 4 * t:DEN + 4 * t + 4]
            self.eng.wait_ge(m.to_dve[4 + t], w.next(m.to_dve[4 + t]))
            self.isa.scalar_tensor_tensor(d, den, -1.0, e, ALU.mult, ALU.max)
            self.settle()
            self.isa.tensor_tensor(d, den, d, ALU.max)
            self.settle()
            self.isa.reciprocal(d, d)
            self.settle()
            h = by_head(m.nat[:, t, S:2 * S])
            self.isa.tensor_tensor(h, out[:, :, 0:DH], d.unsqueeze(2).to_broadcast([P, 4, DH]), ALU.mult) \
                .then_inc(m.free[4 + t], 1)
            self.settle()
            self.isa.tensor_tensor(m.nat[:, t, S:2 * S], m.nat[:, t, S:2 * S], m.nat[:, t, 768:D], ALU.mult)
            self.settle()
            self.head_stats(t, h)
        self.head_norm(lambda t: by_head(m.nat[:, t, S:2 * S]), S)
        self.eng.drain().then_inc(m.nat_ready, 1)
        self.softmax_heads(2, m.tab(B_TABLES, "blocks"), (DH + 32) ** -0.5)
        self.low_turned((0, 1), m.oT_hi, m.oT_lo, m.hT_ready, par[:, GN:GN + 4], (0, 1, 6, 7))
        self.split(4)
        self.eng.wait_ge(m.w_used, self.w.product_done())
        self.scaled_add_banks()
        self.layer_norm(LN1, load=True)

    def conv4(self, bank, dst, par):
        m = self.m
        for g in range(2):
            self.isa.tensor_scalar(dst[:, g * S:(g + 1) * S], bank[:, g * S:(g + 1) * S], par[:, 5 * g + 3:5 * g + 4],
                                   par[:, 5 * g + 4:5 * g + 5], ALU.mult, ALU.add)
        for back in (1, 2, 3):
            self.settle()
            for g in range(2):
                out = dst[:, g * S + back:(g + 1) * S]
                last = self.isa.scalar_tensor_tensor(out, bank[:, g * S:(g + 1) * S - back],
                                                     par[:, 5 * g + 3 - back:5 * g + 4 - back], out, ALU.mult, ALU.add)
        self.eng.drain().then_inc(m.conv_in, 1)

    def head_stats(self, t, rows):
        m = self.m
        for h in range(4):
            i = 4 * t + h
            self.isa.bn_stats(m.small[:, ST + 6 * i:ST + 6 * i + 6], rows[:, h, :])
        self.settle()
        for h in range(4):
            i = 4 * t + h
            self.isa.bn_aggr(m.small[:, MV + 2 * i:MV + 2 * i + 2], m.small[:, ST + 6 * i:ST + 6 * i + 6])
        self.settle()

    def head_norm(self, rows_of, col):
        m = self.m
        mv = m.small[:, MV:MV + 16].rearrange("p (i two) -> p i two", two=2)
        self.isa.tensor_scalar(m.small[:, VAR:VAR + 8], mv[:, :, 1], 1e-5, None, ALU.add).then_inc(m.rstd_in, 1)
        self.eng.wait_ge(m.rstd, self.w.next(m.rstd))
        for t in range(TT):
            for h in range(4):
                i = 4 * t + h
                self.isa.tensor_scalar(m.nat[:, t, col + h * DH:col + (h + 1) * DH], rows_of(t)[:, h, :],
                                       m.small[:, MV + 2 * i:MV + 2 * i + 1], m.small[:, RSTD8 + i:RSTD8 + i + 1],
                                       ALU.subtract, ALU.mult)
        self.settle()

    def scaled_add_banks(self):
        m = self.m
        for half in range(2):
            for t in range(TT):
                b = 4 + 2 * half + t
                x = m.x[:, t, 512 * half:512 * half + 512]
                self.isa.scalar_tensor_tensor(x, x, ALPHA, m.bank[b], ALU.mult, ALU.add).then_inc(m.free[b], 1)
        self.settle()

    def layer_norm(self, at, load=False):
        m = self.m
        for t in range(TT):
            for half in range(2):
                i = ST + 12 * t + 6 * half
                self.isa.bn_stats(m.small[:, i:i + 6], m.x[:, t, 512 * half:512 * half + 512])
        self.settle()
        for t in range(TT):
            self.isa.bn_aggr(m.small[:, MV + 2 * t:MV + 2 * t + 2], m.small[:, ST + 12 * t:ST + 12 * t + 12])
        self.settle()
        mv = m.small[:, MV:MV + 4].rearrange("p (i two) -> p i two", two=2)
        self.isa.tensor_scalar(m.small[:, VAR:VAR + 2], mv[:, :, 1], 1e-5, None, ALU.add).then_inc(m.rstd_in, 1)
        self.eng.wait_ge(m.rstd, self.w.next(m.rstd))
        if load:
            self.eng.wait_ge(m.rows_loaded, self.w.next(m.rows_loaded, 16))
        for t in range(TT):
            self.isa.tensor_scalar(m.x[:, t, :], m.x[:, t, :], m.small[:, MV + 2 * t:MV + 2 * t + 1],
                                   m.small[:, RSTD8 + t:RSTD8 + t + 1], ALU.subtract, ALU.mult)
        for op, a in ((ALU.mult, at), (ALU.add, at + D)):
            self.settle()
            for t in range(TT):
                self.isa.tensor_tensor(m.x[:, t, :], m.x[:, t, :], m.arena[:, a:a + D], op)
        self.eng.drain().then_inc(m.nat_ready, 1)

    def feed_forward(self):
        m, w = self.m, self.w
        self.low_turned((0, 1, 2, 3), m.hT_hi, m.hT_lo, m.hT_ready)
        self.hidden(0)
        with w.repeat((FF_SUBS - 1) // 2, DVE_SWIGLU_TURN):
            for p in (1, 0):
                self.hidden(p)
                self.split(1)
        self.split(1)
        self.eng.wait_ge(m.w_used, self.w.product_done())
        self.scaled_add_banks()
        self.layer_norm(LN2)

    def hidden(self, p):
        m = self.m
        self.split(2)
        self.settle()
        self.eng.wait_ge(m.silu_done, self.w.next(m.silu_done))
        self.eng.wait_ge(m.w_used, self.w.product_done())
        self.isa.tensor_tensor(hidden_value(m), hidden_gate(m).rearrange("p (a b) -> p a b", a=2),
                               by_head(m.bank[2 * p + 1], 2), ALU.mult).then_inc(m.hid, 1)
        self.eng.wait_ge(m.hid_hi, self.w.next(m.hid_hi))
        self.isa.tensor_tensor(m.oT_lo[:, 2 * p:2 * p + 2, :], hidden_value(m), m.oT_hi[:, 2 * p:2 * p + 2, :].bitcast(F32),
                               ALU.subtract).then_inc(m.hid_ready, 1)
        self.eng.drain().then_inc(m.free[2 * p + 1], 1)

    def route(self):
        m, w = self.m, self.w
        self.low_turned((0, 1, 2, 3), m.hT_hi, m.hT_lo, m.hT_ready)
        self.split(1)
        self.settle()
        self.eng.wait_ge(m.w_used, self.w.product_done())
        tt, ts = self.isa.tensor_tensor, self.isa.tensor_scalar
        sel, lg, gate, place = (route_part(m, i) for i in (0, 1, 2, 3))
        best, second, tmp = (route_part(m, i) for i in (4, 5, 6))
        vals, d, s = route_part(m, 8, 4), route_part(m, 10, 2), route_part(m, 11, 4)
        counts = route_part(m, 12, 8)
        pairs = [m.arena[:, ROUTE + 256 + 64 * i:ROUTE + 320 + 64 * i].rearrange("p (e j) -> p e j", e=8)
                 for i in range(2)]
        for t in range(TT):
            self.isa.tensor_copy(lg[:, 8 * t:8 * t + 8], m.bank[t][:, 0:8]).then_inc(m.free[t], 1)
        slots = m.tab(B_TABLES, "slots")
        for t in range(TT):
            l = lg[:, 8 * t:8 * t + 8]
            mine, other = l.unsqueeze(2).to_broadcast([P, 8, 8]), l.unsqueeze(1).to_broadcast([P, 8, 8])
            j, e = (slots[:, 0:8].unsqueeze(a).to_broadcast([P, 8, 8]) for a in (1, 2))
            self.settle()
            tt(pairs[0], other, mine, ALU.is_equal)
            tt(pairs[1], j, e, ALU.is_lt)
            self.settle()
            tt(pairs[0], pairs[0], pairs[1], ALU.mult)
            self.settle()
            tt(pairs[1], other, mine, ALU.is_gt)
            self.settle()
            tt(pairs[0], pairs[0], pairs[1], ALU.add)
            self.settle()
            self.isa.tensor_reduce(tmp[:, 8 * t:8 * t + 8], pairs[0], AX.X, ALU.add)
        self.settle()
        ts(best, tmp, 0.0, None, ALU.is_equal)
        ts(second, tmp, 1.0, None, ALU.is_equal)
        ts(sel, tmp, 1.5, None, ALU.is_lt)
        self.eng.drain().then_inc(m.selected, 1)
        for i, which in ((0, best), (1, second)):
            tt(tmp, which, lg, ALU.mult)
            self.settle()
            self.isa.tensor_reduce(vals[:, 2 * i:2 * i + 2], tmp.rearrange("p (t e) -> p t e", t=TT), AX.X, ALU.add)
            self.settle()
        tt(d, vals[:, 2:4], vals[:, 0:2], ALU.subtract).then_inc(m.d_ready, 1)
        self.eng.wait_ge(m.e_ready, w.next(m.e_ready))
        ts(s[:, 0:2], d, 1.0, None, ALU.add)
        self.settle()
        self.isa.reciprocal(s[:, 0:2], s[:, 0:2])
        self.settle()
        tt(s[:, 2:4], s[:, 0:2], d, ALU.mult)
        self.settle()
        for t in range(TT):
            c = slice(8 * t, 8 * t + 8)
            ts(gate[:, c], best[:, c], s[:, t:t + 1], None, ALU.mult)
        self.settle()
        for t in range(TT):
            c = slice(8 * t, 8 * t + 8)
            self.isa.scalar_tensor_tensor(gate[:, c], second[:, c], s[:, 2 + t:3 + t], gate[:, c], ALU.mult, ALU.add)
        self.eng.wait_ge(m.placed, w.next(m.placed))
        self.isa.scalar_tensor_tensor(place, m.bank[2][:, 0:16], 1.0, sel, ALU.add, ALU.mult)
        self.isa.tensor_copy(counts, m.bank[2][:, 16:24]).then_inc(m.free[2], 1)
        self.settle()
        ts(place, place, -1.0, None, ALU.add)
        full, rank, mine = (route_part(m, i, 8) for i in (4, 5, 6))
        ts(full, counts, float(P), None, ALU.is_gt)
        self.settle()
        one = m.tab(B_TABLES, "ones")[:, 0:8]
        self.isa.tensor_tensor_scan(rank, one, full, 0.0, ALU.mult, ALU.add)
        upos, ugate = (m.arena[:, a:a + 24].rearrange("p (t u) -> p t u", t=TT) for a in (UPOS, UGATE))
        self.isa.memset(m.arena[:, UPOS:UPOS + 48], -1.0)
        self.isa.tensor_copy(m.units[:, 0:8], slots[:, 0:8])
        self.isa.tensor_scalar(m.units[:, 11:12], slots[:, 0:1], 0.0, None, ALU.mult)
        self.settle()
        ts(m.units[:, COUNT:COUNT + 1], rank[:, 7:8], 8.0, None, ALU.add)
        for t in range(TT):
            self.isa.tensor_copy(upos[:, t, 0:8], place[:, 8 * t:8 * t + 8])
            self.isa.tensor_copy(ugate[:, t, 0:8], gate[:, 8 * t:8 * t + 8])
        for k in range(3):
            ts(mine, rank, float(k + 1), None, ALU.is_equal)
            self.settle()
            tt(mine, mine, full, ALU.mult)
            self.settle()
            tt(counts, mine, slots[:, 0:8], ALU.mult)
            self.settle()
            self.isa.tensor_reduce(s[:, 0:1], counts, AX.X, ALU.add)
            self.settle()
            self.isa.tensor_copy(m.units[:, 8 + k:9 + k], s[:, 0:1])
            for t in range(TT):
                for src, dst, shift in ((place, upos, -float(P)), (gate, ugate, 0.0)):
                    self.settle()
                    tt(counts, mine, src[:, 8 * t:8 * t + 8], ALU.mult)
                    self.settle()
                    self.isa.tensor_reduce(s[:, 1:2], counts, AX.X, ALU.add)
                    self.settle()
                    ts(dst[:, t, 8 + k:9 + k], s[:, 1:2], shift, None, ALU.add)
            self.settle()
        self.isa.memset(m.nat[:, :, :], 0.0)
        self.isa.memset(y_rows(m), 0.0)
        self.isa.memset(picksT(m), 0.0)
        self.eng.drain().then_inc(m.y_rows, 1)
        self.make_picks(0)
        self.eng.drain().then_inc(m.units_ready, 1)

    def make_picks(self, unit):
        m = self.m
        slots = m.tab(B_TABLES, "slots")
        for t in range(TT):
            if type(unit) is int:
                pos, gate = (m.arena[:, a + 12 * t + unit:a + 12 * t + unit + 1] for a in (UPOS, UGATE))
            else:
                pos, gate = (m.arena[:, bass.ds(unit + (a + 12 * t), 1)] for a in (UPOS, UGATE))
            self.isa.tensor_scalar(picks(m, t), slots, pos, None, ALU.is_equal)
            self.isa.tensor_scalar(weighted(m, t), slots, pos, gate, ALU.is_equal, ALU.mult)
        self.eng.drain().then_inc(m.picks_ready, 1)

    def gathered(self):
        m = self.m
        for j, b in enumerate((6, 7)):
            self.eng.wait_ge(m.act_hi, self.w.next(m.act_hi))
            self.isa.tensor_tensor(m.hT_lo[:, 4 * j:4 * j + 4, 0:P], by_head(m.bank[b]),
                                   m.hT_hi[:, 4 * j:4 * j + 4, 0:P].bitcast(F32), ALU.subtract).then_inc(m.free[b], 1)
        self.eng.drain().then_inc(m.x_here, 1)

    def hidden_rows(self):
        m = self.m
        self.settle()
        self.eng.wait_ge(m.silu_done, self.w.next(m.silu_done))
        self.eng.wait_ge(m.w_used, self.w.product_done())
        self.isa.tensor_tensor(h_rows(m), g_rows(m), m.bank[1], ALU.mult).then_inc(m.h_rows, 1)
        self.eng.drain().then_inc(m.free[1], 1)

    def hidden_turned(self):
        m = self.m
        self.eng.wait_ge(m.hid_hi, self.w.next(m.hid_hi))
        self.isa.tensor_tensor(m.oT_lo[:, 0:4, 0:P], by_head(m.bank[2]), m.oT_hi[:, 0:4, 0:P].bitcast(F32),
                               ALU.subtract).then_inc(m.hid_ready, 1)
        self.eng.drain().then_inc(m.free[2], 1)

    def gather_shares(self):
        m = self.m
        self.settle()
        for t, banks in ((0, (6, 7)), (1, (3, 2))):
            for half, b in enumerate(banks):
                y = m.nat[:, t, 512 * half:512 * half + 512]
                self.eng.wait_ge(m.to_dve[b], self.w.next(m.to_dve[b]))
                self.isa.tensor_tensor(y, y, m.bank[b], ALU.add).then_inc(m.free[b], 1)

    def experts(self):
        m, w = self.m, self.w
        self.eng.wait_ge(m.units_ready, w.next(m.units_ready))
        units = self.isa.value_load(m.units[0:1, COUNT:COUNT + 1], min_val=8, max_val=11)
        self.gathered()
        with w.repeat(units, DVE_UNIT) as u:
            self.split(4)
            self.hidden_rows()
            self.gather_shares()
            self.eng.wait_ge(m.to_dve[6], w.next(m.to_dve[6]))
            self.isa.tensor_copy(picksT(m), m.bank[6][:, 0:S]).then_inc(m.free[6], 1)
            self.make_picks(u + 1)
            with w.repeat(EXP_STEPS - 1, DVE_STEP):
                self.split(2)
                self.hidden_turned()
                self.split(2)
                self.hidden_rows()
                self.split(2)
            self.hidden_turned()
            self.gathered()
            self.split(2)
        self.gather_shares()
        self.settle()
        for t in range(TT):
            self.isa.scalar_tensor_tensor(m.x[:, t, :], m.x[:, t, :], ALPHA, m.nat[:, t, :], ALU.mult, ALU.add)
        self.settle()
        self.layer_norm(LN2)
        self.eng.drain().then_inc(m.result_ready, 1)


PE_FFN_TURN = {
    "reuse bank_free0": 1, "reuse bank_free1": 1, "reuse bank_free2": 1, "reuse bank_free3": 1,
    "hid_ready": 2, "chunks": 6}
ACT_FFN_TURN = {"silu_in": 2, "hid": 2, "chunks": 6}
DVE_FFN_TURN = {"silu_done": 2, "hid_hi": 2, "chunks": 6}
ACT_SWIGLU_TURN = {"hid": 2, "chunks": 6}
DVE_SWIGLU_TURN = {"silu_done": 2, "hid_hi": 2, "chunks": 6}
PE_LAYER = {
    "nat_ready": 3, "reuse bank_free0": 20, "reuse bank_free1": 20, "reuse bank_free2": 19,
    "reuse bank_free3": 18, "hT_ready": 3, "reuse bank_free4": 9, "reuse bank_free5": 9, "kq_copied": 7,
    "reuse bank_free6": 15, "reuse bank_free7": 14, "roped": 7, "probs_ready": 16, "pt_ready": 24,
    "copied": 8, "lom_ready": 8, "oT_ready": 1, "hid_ready": 11, "chunks": 72}
ACT_LAYER = {
    "x_ready": 2, "to_act0": 5, "to_act1": 5, "to_act2": 5, "to_act3": 5, "negm": 4, "probs_turned": 16,
    "reuse weighed": 24, "weighed": 24, "probs_free": 1, "logw_ready": 8, "gate_in": 12, "silu_in": 11,
    "hid": 11, "chunks": 72}
DVE_LAYER = {
    "squares": 2, "rstd": 2, "act_hi": 24, "to_dve0": 8, "to_dve1": 8, "to_dve2": 8, "to_dve3": 7,
    "reuse probs_turned": 16, "exped": 4, "l_ready": 8, "rows_loaded": 16, "gate_out": 12, "silu_done": 11,
    "hid_hi": 11, "chunks": 72}
POOL_LAYER = {"rstd_in": 2, "n_ready": 8, "weighed": 24}
PE_UNIT = {
    "reuse bank_free0": 7, "reuse bank_free1": 7, "reuse bank_free2": 8, "reuse bank_free3": 1,
    "reuse bank_free4": 1, "reuse bank_free5": 1, "reuse bank_free6": 3, "reuse bank_free7": 2,
    "hid_ready": 7, "picks_ready": 1, "x_here": 1, "y_rows": 1, "h_rows": 7, "chunks": 42}
ACT_UNIT = {"to_act2": 7, "to_act6": 1, "to_act7": 1, "reuse h_rows": 7, "chunks": 42}
DVE_UNIT = {
    "act_hi": 2, "to_dve2": 1, "to_dve3": 1, "silu_done": 7, "hid_hi": 7, "to_dve6": 2, "to_dve7": 1,
    "chunks": 42}
PE_STEP = {
    "reuse bank_free0": 1, "reuse bank_free1": 1, "reuse bank_free2": 1, "hid_ready": 1, "h_rows": 1,
    "chunks": 6}
ACT_STEP = {"to_act2": 1, "reuse h_rows": 1, "chunks": 6}
DVE_STEP = {"silu_done": 1, "hid_hi": 1, "chunks": 6}


def program(nc, inp, out):
    with ExitStack() as ctx:
        m = Memory(nc, ctx)
        block = ctx.enter_context(nc.Block())

        @block.sync
        def _(sp):
            w = Waits(sp)
            w.rings = 0
            sp.dma_start(m.x[:], inp["x"][0].rearrange("(t p) d -> p t d", p=P)).then_inc(m.x_loaded, 16)
            sp.dma_start(m.all_cols[:], inp["cols_a"]).then_inc(m.cols_loaded, 16)
            sp.dma_start(m.tables[:, 0:A_COLS], inp["tables_a"]).then_inc(m.tables_loaded, 16)

            def load(chunk):
                raw, _, _, number = w.take()
                sp.wait_ge(m.lo_ready, number + 1)
                sp.dma_start(m.raw[:, raw, :], inp["weights"][chunk]).then_inc(m.raw_full[raw], 16)

            static = FIXED + RAW
            with w.repeat(static // RAW, {"chunks": RAW}) as i:
                for j in range(RAW):
                    load(i * RAW + j)
            for c in range(static // RAW * RAW, static):
                load(c)
            sp.wait_ge(m.units_ready, w.next(m.units_ready))
            units = sp.value_load(m.units[0:1, COUNT:COUNT + 1], min_val=8, max_val=11)
            with w.repeat(units, {"chunks": UNIT}) as u:
                for at, first, end in ((0, RAW, UNIT), (1, 0, RAW)):
                    expert = sp.value_load(m.units[0:1, bass.ds(u + at, 1)], min_val=0, max_val=N_EXP - 1)
                    for j in range(first, end):
                        load(expert * UNIT + (FIXED + j))
            sp.wait_ge(m.result_ready, w.next(m.result_ready))
            sp.dma_start(out[0].rearrange("(t p) d -> p t d", p=P), m.x[:]).then_inc(m.stored, 16)
            sp.wait_ge(m.stored, w.next(m.stored, 16))

        @block.gpsimd
        def _(pool):
            e = Pool(nc, m, pool, nc.gpsimd)
            nc.gpsimd.memset(m.small[:, HALF:HALF + 8], -0.5)
            nc.gpsimd.memset(m.zeros[:].bitcast(F32), 0.0)
            pool.drain().then_inc(m.start, 1)
            for sem in [m.hi_ready, m.lo_ready, m.w_used, m.probs_turned, m.weighed, m.h_rows] + m.free:
                pool.sem_inc(sem, FREE_AT_START[sem.name])
            pool.wait_ge(m.start, e.w.next(m.start))
            with e.w.repeat(DEPTH, POOL_LAYER) as layer:
                e.power((2, 4), 4)
                e.stick_heads(m.tab(A_TABLES, "before01"))
                pool.wait_ge(m.weighed, e.w.next(m.weighed, 24))
                pool.dma_start(m.arena[:, 0:3 * D], inp["b_gate"][layer].partition_broadcast(P)) \
                    .then_inc(m.rows_loaded, 16)
                e.power((2, 4), 4)
            pool.dma_start(m.arena[:, 0:D], inp["norm_final"].partition_broadcast(P)).then_inc(m.rows_loaded, 16)
            pool.dma_start(m.tables[:, SHARED:B_COLS], inp["tables_b"]).then_inc(m.tables_b_loaded, 16)
            pool.dma_start(m.all_cols[:, 0:DEPTH * B_PARAMS], inp["cols_b"]).then_inc(m.cols_b_loaded, 16)
            e.power((2, 4), 4)
            for layer in range(DEPTH):
                e.power((CMS, CMS + 4), CRS)
                e.power((VAR, VAR + 8), RSTD8)
                e.power((VAR, VAR + 8), RSTD8)
                pool.wait_ge(m.weighed, e.w.next(m.weighed, 8))
                pool.dma_start(m.arena[:, 0:4 * D], inp["norms"][layer].partition_broadcast(P)) \
                    .then_inc(m.rows_loaded, 16)
                e.power((VAR, VAR + 2), RSTD8)
                e.power((VAR, VAR + 2), RSTD8)

        @block.scalar
        def _(act):
            a = ScalarA(nc, m, act, nc.scalar)
            act.wait_ge(m.cols_loaded, a.w.next(m.cols_loaded, 16))
            a.split(AHEAD)
            with a.w.repeat(DEPTH, ACT_LAYER):
                a.layer()
            b = ScalarB(nc, m, act, nc.scalar, a)
            act.wait_ge(m.x_ready, b.w.next(m.x_ready))
            b.squares(m.x)
            act.wait_ge(m.cols_b_loaded, b.w.next(m.cols_b_loaded, 16))
            b.mixer(0)
            b.feed_forward()
            b.mixer(1)
            b.experts()

        @block.vector
        def _(dve):
            a = VectorA(nc, m, dve, nc.vector)
            dve.wait_ge(m.x_loaded, a.w.next(m.x_loaded, 16))
            dve.wait_ge(m.tables_loaded, a.w.next(m.tables_loaded, 16))
            dve.wait_ge(m.cols_loaded, a.w.next(m.cols_loaded, 16))
            dve.drain().then_inc(m.x_ready, 1)
            a.split(AHEAD)
            with a.w.repeat(DEPTH, DVE_LAYER) as layer:
                a.layer(layer)
            b = VectorB(nc, m, dve, nc.vector, a)
            b.normed_start()
            dve.wait_ge(m.tables_b_loaded, b.w.next(m.tables_b_loaded, 16))
            dve.wait_ge(m.cols_b_loaded, b.w.next(m.cols_b_loaded, 16))
            b.mixer(0)
            b.feed_forward()
            b.mixer(1)
            b.route()
            b.experts()

        @block.tensor
        def _(pe):
            a = TensorA(nc, m, pe, nc.tensor)
            pe.wait_ge(m.tables_loaded, a.w.next(m.tables_loaded, 16))
            pe.wait_ge(m.start, a.w.next(m.start))
            with a.w.repeat(DEPTH, PE_LAYER):
                a.layer()
            b = TensorB(nc, m, pe, nc.tensor, a)
            b.w.skip(m.nat_ready, 1)
            pe.wait_ge(m.tables_b_loaded, b.w.next(m.tables_b_loaded, 16))
            for layer in range(DEPTH):
                b.mixer()
                pe.wait_ge(m.nat_ready, b.w.next(m.nat_ready))
                b.turn_rows(m.x, (0, 1, 2, 3), m.tab(B_TABLES, "ident"))
                pe.wait_ge(m.hT_ready, b.w.next(m.hT_ready))
                if layer == 0:
                    b.feed_forward()
            b.route()
            b.experts()



def turning_tables(half):
    inv = np.float32(10000.0) ** (-np.arange(half, dtype=np.float32) / np.float32(half))
    ang = np.arange(S, dtype=np.float32)[None, :] * np.tile(inv, P // half)[:, None]
    return np.cos(ang), np.sin(ang)


def rotation(half):
    r = np.zeros((P, P), np.float32)
    for i in range(P):
        if i % (2 * half) < half:
            r[i + half, i] = -1.0
        else:
            r[i - half, i] = 1.0
    return r


def tables_a():
    i = np.arange(P)
    causal = np.where(i[None, :] <= i[:, None], 0.0, NEG)
    window = np.where(i[None, :] > i[:, None], 0.0, NEG)
    before = i[:, None] < i[None, :]
    one = np.ones((P, P))
    cos, sin = turning_tables(DH // 2)
    parts = dict(
        ident=np.eye(P), rot64=rotation(DH // 2), cos64=cos, sin64=sin,
        band=np.concatenate([window, causal], 1), causal=np.concatenate([0 * one, causal], 1),
        before01=np.concatenate([before, one, before], 1),
        before=np.concatenate([np.where(before, 0.0, NEG), 0 * one, np.where(before, 0.0, NEG)], 1),
        tri=np.where(i[:, None] >= i[None, :], -1.0, 0.0), ones=-one)
    return np.concatenate([parts[n] for n in A_TABLES], 1).astype(np.float32)


def chunk_of(w, kt=None):
    k, n = w.shape
    out = w.reshape(k // P, P, n).transpose(1, 0, 2).reshape(P, -1)
    assert out.shape[1] <= CH
    return np.pad(out, ((0, 0), (0, CH - out.shape[1])))


def layer_chunks_a(w_in, w_branch, w_out, w_up, w_down):
    o = np.cumsum([0, 512, 128, 128, 512, 512, 512, 512, 512, 512])
    qa, ka, va, qb, kb, vb, qc, kc, vc = (w_in[:, o[i]:o[i + 1]] for i in range(9))
    heads = qa.reshape(D, 8, DH)
    paired = np.stack([heads[:, 0:4], heads[:, 4:8]], 2).reshape(D, 512)
    out = []

    def turned(w):
        out.extend(chunk_of(w[:, c:c + S]) for c in range(0, w.shape[1], S))

    def rows(w, k=512):
        out.extend(chunk_of(w[a:a + k]) for a in range(0, w.shape[0], k))

    turned(paired)
    turned(np.concatenate([ka, va], 1))
    turned(qb), turned(kb), rows(vb), turned(qc), turned(kc), rows(vc)
    for u in range(6):
        i, h = u // 2, u % 2
        rows(w_in[:, o[9] + i * D + 512 * h:o[9] + i * D + 512 * h + 512])
        rows(w_branch[i][:, 512 * h:512 * h + 512])
    for a, b in ((0, 256), (256, 512), (512, 640), (640, 768), (768, 896), (896, 1024)):
        out.append(chunk_of(w_out[a:b]))

    def up(j):
        turned(w_up[:, j * S:(j + 1) * S])
        turned(w_up[:, D_FF + j * S:D_FF + (j + 1) * S])

    up(0)
    for j in range(1, FF_SUBS):
        up(j)
        rows(w_down[(j - 1) * S:j * S], S)
    rows(w_down[(FF_SUBS - 1) * S:], S)
    assert len(out) == A_LAYER, len(out)
    return out


def columns_a(norm_mix, norm_ffn, conv_w, conv_b, sinks):
    taps = np.concatenate([conv_w, conv_b[None]], 0).reshape(4, 2, FF_SUBS, 2, P)
    return np.concatenate([
        norm_mix.reshape(KT, P).T, norm_ffn.reshape(KT, P).T,
        taps.transpose(4, 2, 1, 3, 0).reshape(P, -1), np.broadcast_to(sinks, (P, 8))], 1)


def tables_b():
    i = np.arange(P)
    one = np.ones((P, P))
    cos, sin = turning_tables(16)
    before = i[:, None] < i[None, :]
    limit = (i // 64 + 1) * 64
    in_block = np.where(i[None, :] < limit[:, None], 0.0, NEG)
    ago = (i[None, :] - i[:, None]).astype(np.float64)
    decay = []
    for h in range(4):
        log_gamma = np.log1p(-2.0 ** (-5.0 - h))
        decay += [np.where(ago >= 0, np.exp(np.maximum(ago, 0) * log_gamma), 0.0) * SCALE,
                  np.exp((ago + P) * log_gamma) * SCALE]
    parts = dict(
        rot32=rotation(16), cos32=cos, sin32=sin, blocks=np.concatenate([0 * one, in_block], 1),
        decay=np.concatenate(decay, 1), causalT=np.where(i[None, :] < i[:, None], -NEG, 0.0), ones=one,
        below=np.where(before, 1.0, 0.0), slots=np.broadcast_to(i, (P, P)))
    return np.concatenate([parts[n] for n in B_TABLES if n in parts], 1).astype(np.float32)


def ffn_steps(w_gate, w_up, w_down, n):
    steps = w_gate.shape[1] // n
    rows = CH // n
    out = []

    def add(w, k):
        out.extend(chunk_of(w[a:a + k]) for a in range(0, w.shape[0], k))

    for s in range(steps + 1):
        if s < steps:
            for w in (w_gate, w_up):
                add(w[:, s * n:(s + 1) * n], rows * P)
        if s:
            add(w_down[(s - 1) * n:s * n], CH // D * P)
    return out


def mixer_chunks_b(w_in, w_uq, w_ukv, w_out):
    def cut(a, n):
        return w_in[:, a:a + n]

    out = [chunk_of(cut(0, 256)), chunk_of(cut(256, 256)),
           chunk_of(np.concatenate([cut(1408, 32)] * 4 + [cut(2464, 8)], 1))]

    def rows(w, k=512):
        out.extend(chunk_of(w[a:a + k]) for a in range(0, w.shape[0], k))

    rows(cut(512, 512))
    rows(cut(1024, 384))
    out.extend([chunk_of(cut(1440, 256)), chunk_of(cut(1696, 256))])
    rows(cut(1952, 512))
    uq = w_uq.reshape(256, 8, 96)
    out.append(chunk_of(np.concatenate([uq[:, :, 0:64].reshape(256, 512), uq[:, :, 64:].reshape(256, 256)], 1)))
    ukv = w_ukv.reshape(128, 8, 128)
    out.append(chunk_of(np.concatenate([ukv[:, :, 0:64].reshape(128, 512), ukv[:, :, 64:].reshape(128, 512)], 1)))
    rows(w_out, 256)
    assert len(out) == B_MIXER, len(out)
    return out


def columns_b(q_norm, kv_norm, ret_gn, mlstm_gn, conv_w, conv_b, b_i, b_f):
    taps = np.concatenate([conv_w, conv_b[None]], 0).reshape(5, 4, P)
    biases = np.zeros((P, 2), np.float32)
    biases[0:4, 0], biases[0:4, 1] = b_i, b_f
    return np.concatenate([q_norm.reshape(2, P).T, kv_norm.reshape(1, P).T, ret_gn.reshape(2, P).T,
                           mlstm_gn.reshape(2, P).T, taps.transpose(2, 1, 0).reshape(P, 20), biases], 1)


def laid_out(a):
    layers = range(DEPTH)
    chunks = []
    for i in layers:
        chunks += layer_chunks_a(a["w_in"][i], a["w_branch"][i], a["w_out"][i], a["w_up"][i], a["w_down"][i])
    for i in layers:
        chunks += mixer_chunks_b(a["w_in_2"][i], a["mla_w_uq_2"][i], a["mla_w_ukv_2"][i], a["w_out_2"][i])
        if i == 0:
            chunks += ffn_steps(a["ffn_w_gate_2"][0], a["ffn_w_up_2"][0], a["ffn_w_down_2"][0], S)
    chunks.append(chunk_of(a["moe_router_2"][0]))
    assert len(chunks) == FIXED, len(chunks)
    for e in range(N_EXP):
        chunks += ffn_steps(a["moe_w_gate_2"][0, e], a["moe_w_up_2"][0, e], a["moe_w_down_2"][0, e], 512)
    norms = np.stack([np.concatenate([a[n][i] for n in ("ln1_w_2", "ln1_b_2", "ln2_w_2", "ln2_b_2")]) for i in layers])
    return {
        "x": a["x"],
        "weights": np.stack(chunks),
        "tables_a": tables_a(),
        "tables_b": tables_b(),
        "cols_a": np.concatenate([columns_a(a["norm_mix"][i], a["norm_ffn"][i], a["conv_w"][i], a["conv_b"][i],
                                            a["sinks"][i]) for i in layers], 1),
        "cols_b": np.concatenate([columns_b(*(a[n + "_2"][i] for n in (
            "mla_q_norm_w", "mla_kv_norm_w", "ret_gn_w", "mlstm_gn_w", "mlstm_conv_w", "mlstm_conv_b",
            "mlstm_b_i", "mlstm_b_f"))) for i in layers], 1),
        "b_gate": a["b_gate"],
        "norm_final": a["norm_final"],
        "norms": norms,
    }


def kernel(**inputs):
    import concourse.bacc as _bacc
    from concourse.bass_utils import run_bass_kernel_spmd as _run

    nc = _bacc.Bacc("TRN2", target_bir_lowering=False, num_devices=1)
    arrays, args = {}, {}
    for name, a in laid_out({k: np.asarray(v) for k, v in inputs.items()}).items():
        arrays[f"in_{name}_dram"] = np.ascontiguousarray(a)
        args[name] = nc.dram_tensor(f"in_{name}_dram", a.shape, F32, kind="ExternalInput").ap()
    out = nc.dram_tensor("out_0_dram", (1, S, D), F32, kind="ExternalOutput").ap()
    program(nc, args, out)
    r = _run(nc, [arrays], core_ids=[0])
    return r.results[0]["out_0_dram"]
```

```python
from contextlib import ExitStack, contextmanager

import numpy as np

import concourse.bass as bass
from concourse import mybir

F32 = mybir.dt.float32
F32R = mybir.dt.float32r
I32 = mybir.dt.int32
ALU = mybir.AluOpType
ACT = mybir.ActivationFunctionType
AX = mybir.AxisListType

P = 128
S = 256
TT = S // P
D = 1024
KT = D // P
DEPTH = 2
DH = 64
D_FF = 2816
D_EXP = 3584
N_EXP = 8
CH = 2048
RAW = 6
SPLIT = 3
AHEAD = 2
NEG = -1e30
SCALE = DH**-0.5
FF_SUBS = D_FF // 256
EXP_STEPS = D_EXP // 512

A_LAYER = 15 + 18 + 6 + 3 * FF_SUBS
assert A_LAYER % RAW == 0


FREE_AT_START = {"hi_ready": RAW, "lo_ready": RAW, "w_used": RAW, "probs_turned": 4, "weighed": 2, "h_rows": 1}
FREE_AT_START.update({f"bank_free{i}": 1 for i in range(8)})


class Waits:

    def __init__(self, engine):
        self.engine = engine
        self.passed = {}
        self.turns = {}
        self.chunk = 0
        self.rings = 1

    def _count(self, key, n, start):
        self.passed[key] = self.passed.get(key, 0) + n
        return self.turns.get(key, 0) + (start + self.passed[key])

    def next(self, sem, n=1):
        return self._count(sem.name, n, FREE_AT_START.get(sem.name, 0))

    def reuse(self, sem):
        return self._count("reuse " + sem.name, 1, 0)

    def all_free(self, sem):
        return self._count("reuse " + sem.name, 0, FREE_AT_START[sem.name])

    def skip(self, sem, n):
        self._count(sem.name, n, 0)

    def product_done(self):
        return self.rings * RAW + (self.chunk - AHEAD)

    @contextmanager
    def repeat(self, count, per, end=lambda: None):
        before, turns, chunk, rings = dict(self.passed), dict(self.turns), self.chunk, self.rings
        with self.engine.Fori(0, count) as i:
            for name, n in per.items():
                if name != "chunks":
                    self.turns[name] = i * n + turns.get(name, 0)
            if per.get("chunks"):
                self.rings = i * (per["chunks"] // RAW) + rings
            yield i
            found = {k: v - before.get(k, 0) for k, v in self.passed.items() if v != before.get(k, 0)}
            if self.chunk != chunk:
                found["chunks"] = self.chunk - chunk
            assert found == per, f"{self.engine.engine}: a turn waits for {found}, not {per}"
        self.passed, self.turns, self.chunk, self.rings = before, turns, chunk, rings
        for name, n in per.items():
            if name == "chunks":
                if type(count) is int:
                    self.chunk = chunk + count * n
                else:
                    self.rings = count * (n // RAW) + rings
            elif type(count) is int:
                self.passed[name] = before.get(name, 0) + count * n
            else:
                self.turns[name] = count * n + turns.get(name, 0)

    def take(self):
        c, self.chunk = self.chunk, self.chunk + 1
        return c % RAW, c % SPLIT, self.rings + c // RAW, self.rings * RAW + c



def table_columns(parts):
    at, out = 0, {}
    for name, n in parts:
        out[name] = (at, at + n)
        at += n
    return out, at


SHARED_TABLES = [("ident", P), ("rot64", P), ("cos64", S), ("sin64", S)]
A_TABLES, A_COLS = table_columns(SHARED_TABLES + [
    ("band", S), ("causal", S), ("before01", 3 * P), ("before", 3 * P), ("tri", P), ("ones", P)])
B_TABLES, B_COLS = table_columns(SHARED_TABLES + [
    ("rot32", P), ("cos32", S), ("sin32", S), ("blocks", S), ("decay", 4 * 2 * P), ("causalT", P),
    ("ones", P), ("below", P), ("slots", P)])
TAB = max(A_COLS, B_COLS)

WARM = 30
COUNT = 12
HALF = 56
QA, KA, QB, KB, QC, KC, A_TILES = 0, 4, 5, 9, 13, 17, 21


class Memory:

    def __init__(self, nc, ctx):
        def sb(name, shape, dt=F32):
            return ctx.enter_context(nc.sbuf_tensor(name, shape, dt))

        def sem(name):
            return ctx.enter_context(nc.semaphore(name))

        self.raw = sb("raw", [P, RAW, CH])
        self.w_hi = sb("w_hi", [P, SPLIT, CH], F32R)
        self.w_lo = sb("w_lo", [P, SPLIT, CH], F32R)
        self.hT_hi = sb("hT_hi", [P, KT, S], F32R)
        self.hT_lo = sb("hT_lo", [P, KT, S], F32R)
        self.oT_hi = sb("oT_hi", [P, 12, S], F32R)
        self.oT_lo = sb("oT_lo", [P, 12, S], F32R)
        self.x = sb("x_tok", [P, TT, D])
        self.nat = sb("nat", [P, TT, D])
        self.arena = sb("arena", [P, 7680])
        self.probs = sb("probs", [P, 4, 384])
        self.probsT = sb("probsT", [P, 2, 384])
        self.tables = sb("tables", [P, TAB])
        self.all_cols = sb("all_cols", [P, DEPTH * A_PARAMS])
        self.cols = sb("cols", [P, A_PARAMS])
        self.small = sb("small", [P, 256])
        self.units = sb("units", [P, COUNT + 1], I32)
        self.zeros = sb("zeros", [P, P], F32R)
        self.bank = [ctx.enter_context(nc.psum_tensor(f"bank{i}", [P, 512], F32))[:] for i in range(8)]

        self.raw_full = [sem(f"raw_full{i}") for i in range(RAW)]
        self.hi_ready = sem("hi_ready")
        self.lo_ready = sem("lo_ready")
        self.w_used = sem("w_used")
        self.to_act = [sem(f"to_act{i}") for i in range(8)]
        self.to_dve = [sem(f"to_dve{i}") for i in range(8)]
        self.free = [sem(f"bank_free{i}") for i in range(8)]
        self.x_loaded = sem("x_loaded")
        self.tables_loaded = sem("tables_loaded")
        self.cols_loaded = sem("cols_loaded")
        self.shared_loaded = sem("shared_loaded")
        self.tables_b_loaded = sem("tables_b_loaded")
        self.cols_b_loaded = sem("cols_b_loaded")
        self.rows_loaded = sem("rows_loaded")
        self.stored = sem("stored")
        self.start = sem("start")
        self.cols_ready = sem("cols_ready")
        self.squares = sem("squares")
        self.rstd_in = sem("rstd_in")
        self.rstd = sem("rstd")
        self.nat_ready = sem("nat_ready")
        self.act_hi = sem("act_hi")
        self.hT_ready = sem("hT_ready")
        self.x_ready = sem("x_ready")
        self.kq_copied = sem("kq_copied")
        self.roped = sem("roped")
        self.copied = sem("copied")
        self.negm = sem("negm")
        self.exped = sem("exped")
        self.probs_ready = sem("probs_ready")
        self.probs_turned = sem("probs_turned")
        self.pt_ready = sem("pt_ready")
        self.weighed = sem("weighed")
        self.oT_ready = sem("oT_ready")
        self.probs_free = sem("probs_free")
        self.l_ready = sem("l_ready")
        self.kept = sem("kept")
        self.z_ready = sem("z_ready")
        self.scans_ready = sem("scans_ready")
        self.cols_turned = sem("cols_turned")
        self.decay_ready = sem("decay_ready")
        self.conv_in = sem("conv_in")
        self.conv_out = sem("conv_out")
        self.pairs_ready = sem("pairs_ready")
        self.selected = sem("selected")
        self.placed = sem("placed")
        self.d_ready = sem("d_ready")
        self.e_ready = sem("e_ready")
        self.units_ready = sem("units_ready")
        self.picks_ready = sem("picks_ready")
        self.x_here = sem("x_here")
        self.result_ready = sem("result_ready")
        self.h_rows = sem("h_rows")
        self.y_rows = sem("y_rows")
        self.n_ready = sem("n_ready")
        self.lom_ready = sem("lom_ready")
        self.logw_ready = sem("logw_ready")
        self.gate_in = sem("gate_in")
        self.gate_out = sem("gate_out")
        self.silu_in = sem("silu_in")
        self.silu_done = sem("silu_done")
        self.hid = sem("hid")
        self.hid_hi = sem("hid_hi")
        self.hid_ready = sem("hid_ready")

    def tab(self, tables, name, a=0, b=None):
        lo, hi = tables[name]
        return self.tables[:, lo + a:hi if b is None else lo + b]



class Engine:
    def __init__(self, nc, mem, engine, isa, before=None):
        self.nc, self.m, self.eng, self.isa = nc, mem, engine, isa
        self.w = before.w if before else Waits(engine)


class Tensor(Engine):

    def __init__(self, nc, mem, engine, isa, before=None):
        super().__init__(nc, mem, engine, isa, before)
        self.known = set()
        self.coming = set()

    def bank(self, b):
        if b in self.known:
            self.known.remove(b)
        else:
            self.eng.wait_ge(self.m.free[b], self.w.reuse(self.m.free[b]))
        return self.m.bank[b]

    def chunk(self):
        _, slot, _, number = self.w.take()
        self.eng.wait_ge(self.m.lo_ready, number + 1)
        return self.m.w_hi[:, slot, :], self.m.w_lo[:, slot, :]

    def three(self, out, st, mv, start, stop):
        mm = self.isa.matmul
        mm(out, st[0], mv[0], start=start, stop=False, skip_group_check=True)
        mm(out, st[0], mv[1], start=False, stop=False, skip_group_check=True)
        return mm(out, st[1], mv[0], start=False, stop=stop, skip_group_check=True)

    def tile(self, x, k):
        if k in self.coming:
            self.coming.remove(k)
            self.eng.wait_ge(self.m.hT_ready, self.w.next(self.m.hT_ready))
        return x[0][:, k, :], x[1][:, k, :]

    def turned(self, outs, w, width, x, kt, n=S, col=0, m=P):
        hi, lo = (a[:, 0:kt * width].rearrange("p (k c) -> p k c", k=kt) for a in w)
        for g, out in enumerate(outs):
            for k in range(kt):
                c = slice(col + g * m, col + (g + 1) * m)
                xs = tuple(a[:, 0:n] for a in self.tile(x, k))
                last = self.three(out, (hi[:, k, c], lo[:, k, c]), xs, k == 0, k == kt - 1)
        return last

    def rows(self, outs, w, width, x, kt, k0, total, col=0, n=512, opened=False, t0=0):
        hi, lo = (a[:, 0:kt * width].rearrange("p (k c) -> p k c", k=kt) for a in w)
        for k in range(kt):
            for t, out in enumerate(outs):
                xs = tuple(a[:, (t0 + t) * P:(t0 + t + 1) * P] for a in self.tile(x, k0 + k))
                last = self.three(out, xs,
                                  (hi[:, k, col:col + n], lo[:, k, col:col + n]),
                                  k0 + k == 0 and not opened, k0 + k == total - 1)
        return last

    def zero(self, b):
        bank, zeros = self.bank(b), self.m.zeros[:]
        for i in range(4):
            self.isa.matmul(bank[:, i * P:(i + 1) * P], zeros, zeros, start=i == 0, stop=False,
                            skip_group_check=True)

    def used(self, last):
        last.then_inc(self.m.w_used, 1)

    def stay_warm(self, n=WARM):
        bank, zeros = self.bank(0), self.m.zeros[:]
        for _ in range(n):
            self.isa.matmul(bank, zeros, zeros.unsqueeze(1).to_broadcast([P, 4, P]), start=True, stop=True)
        self.known.add(0)

    def turn_x(self, ident):
        m = self.m
        self.stay_warm()
        banks = [self.bank(b) for b in range(4)]
        for t in range(TT):
            self.eng.wait_ge(m.nat_ready, self.w.next(m.nat_ready))
            for k in range(KT):
                at = (k % 2) * S + t * P
                last = self.isa.transpose(banks[k // 2][:, at:at + P], m.x[:, t, k * P:(k + 1) * P], ident)
                if k % 2 and t == TT - 1:
                    last.then_inc(m.to_act[k // 2], 1)
        self.coming = {0, 2, 4, 6}

    def turn_rows(self, src, banks, ident, tiles=KT):
        for j, b in enumerate(banks):
            bank = self.bank(b)
            for k in range(2 * j, min(2 * j + 2, tiles)):
                for t in range(TT):
                    at = (k % 2) * S + t * P
                    last = self.isa.transpose(bank[:, at:at + P], src[:, t, k * P:(k + 1) * P], ident)
            last.then_inc(self.m.to_act[b], 1)

    def rotate(self, src, b, rot, n):
        m = self.m
        self.eng.wait_ge(m.kq_copied, self.w.next(m.kq_copied))
        bank = self.bank(b)
        last = self.isa.matmul(bank[:, 0:n * S], rot, src, start=True, stop=True)
        last.then_inc(m.to_dve[b], 1)

    def scores(self, b, parts):
        bank = self.bank(b)
        for at, q0, n in ((0, 0, P), (P, P, S)):
            for i, (q, k) in enumerate(parts):
                last = self.isa.matmul(bank[:, at:at + n], q[:, q0:q0 + P], k[:, 0:n],
                                       start=i == 0, stop=i == len(parts) - 1, skip_group_check=True)
        last.then_inc(self.m.to_dve[b], 1)

    def turn_probs(self, hh, b, ident):
        m = self.m
        self.eng.wait_ge(m.probs_ready, self.w.next(m.probs_ready))
        bank = self.bank(b)
        for i in range(3):
            last = self.isa.transpose(bank[:, i * P:(i + 1) * P], m.probs[:, hh, i * P:(i + 1) * P], ident)
        last.then_inc(m.probs_turned, 1)

    def weigh(self, h, v, turn_bank=None):
        m = self.m
        self.eng.wait_ge(m.pt_ready, self.w.next(m.pt_ready))
        if turn_bank is not None:
            self.known.add(turn_bank)
        b = 6 + (h // 2) % 2
        if h % 2 == 0:
            self.bank(b)
        pt = m.probsT[:, h % 2, :]
        base = (h % 2) * DH
        out = m.bank[b][base:base + DH, 0:S]
        self.isa.matmul(out, v[0], pt[:, 0:S], start=True, stop=False, skip_group_check=True)
        self.isa.matmul(out[:, P:S], v[1], pt[:, S:S + P], start=False, stop=True,
                        skip_group_check=True).then_inc(m.weighed, 1)

    def softmax_heads(self, parts_of, v_of, ident):
        for h in range(8):
            self.scores(h % 4, parts_of(h))
        for h in range(8):
            self.turn_probs(h % 4, 4 + h % 2, ident)
            if h:
                self.weigh(h - 1, v_of(h - 1), 4 + (h - 1) % 2)
        self.weigh(7, v_of(7), 5)

    def stick_heads(self, q_of, k_of, v_of, tri, ones):
        m = self.m

        def logits(h):
            bank, q, k = self.bank(h % 4), q_of(h), k_of(h)
            self.isa.matmul(bank[:, 0:S], k[:, 0:P], q, start=True, stop=False, skip_group_check=True)
            self.isa.matmul(bank[:, S:S + P], k[:, P:S], q[:, P:S], start=False, stop=False,
                            skip_group_check=True).then_inc(m.to_act[h % 4], 1)

        def sums(h):
            bank, lom = m.bank[h % 4], m.probs[:, h % 4, :]
            self.eng.wait_ge(m.lom_ready, self.w.next(m.lom_ready))
            self.isa.matmul(bank[:, 0:S], tri, lom[:, 0:S], start=False, stop=False, skip_group_check=True)
            self.isa.matmul(bank[:, P:S], ones, lom[:, S:S + P], start=False, stop=False, skip_group_check=True)
            self.isa.matmul(bank[:, S:S + P], tri, lom[:, S:S + P], start=False, stop=True,
                            skip_group_check=True).then_inc(m.to_dve[h % 4], 1)

        for h in range(4):
            logits(h)
        for g in range(2):
            for hh in range(4):
                sums(4 * g + hh)
            for hh in range(4):
                if g == 0:
                    logits(4 + hh)
                self.weigh(4 * g + hh, v_of(4 * g + hh))


class Scalar(Engine):

    def settle(self):
        self.eng.drain()

    def split(self, n=1):
        m = self.m
        for _ in range(n):
            raw, slot, loads, number = self.w.take()
            self.eng.wait_ge(m.raw_full[raw], loads * 16)
            self.eng.wait_ge(m.w_used, number + 1 - SPLIT)
            self.isa.copy(m.w_hi[:, slot, :], m.raw[:, raw, :]).then_inc(m.hi_ready, 1)

    def squares(self):
        m = self.m
        for half in range(2):
            c = slice(512 * half, 512 * half + 512)
            self.eng.wait_ge(m.x_ready, self.w.next(m.x_ready))
            for t in range(TT):
                last = self.isa.activation(m.nat[:, t, c], m.x[:, t, c], ACT.Square,
                                           accum_out=m.small[:, 6 * half + t:6 * half + t + 1])
        last.then_inc(m.squares, 1)

    def scaled_rows(self):
        m = self.m
        self.settle()
        self.eng.wait_ge(m.rstd, self.w.next(m.rstd))
        self.isa.activation(m.nat[:, 1, :], m.x[:, 1, :], ACT.Copy, scale=m.small[:, 5:6]).then_inc(m.nat_ready, 1)

    def high_turned(self, banks, hi, scales=None, tiles=range(KT)):
        m = self.m
        for j, b in enumerate(banks):
            self.eng.wait_ge(m.to_act[b], self.w.next(m.to_act[b]))
            for k in range(2 * j, min(2 * j + 2, len(tiles))):
                at = (k % 2) * S
                last = self.isa.activation(hi[:, tiles[k], :], m.bank[b][:, at:at + S], ACT.Copy,
                                           scale=1.0 if scales is None else scales[:, k:k + 1])
            last.then_inc(m.act_hi, 1)

    def copy_out(self, b, pairs, to=None, scale=1.0):
        m = self.m
        for dst, src in pairs:
            last = self.isa.activation(dst, src, ACT.Copy, scale=scale)
        last.then_inc(m.free[b] if to is None else to, 1)
        if to is not None:
            self.eng.drain().then_inc(m.free[b], 1)

    def exp_pair(self, pair, sinks):
        m = self.m
        first = 4 * (pair % 2)
        self.eng.wait_ge(m.negm, self.w.next(m.negm))
        for i in range(first, first + 4):
            a, b = ((0, P), (P, 384))[i % 2]
            last = self.isa.activation(m.probs[:, i // 2, a:b], m.probs[:, i // 2, a:b], ACT.Exp,
                                       bias=m.small[:, 24 + i:25 + i], accum_out=m.small[:, 32 + i:33 + i])
        if sinks:
            last = self.isa.activation(m.small[:, 40 + first:44 + first], m.small[:, 48 + first:52 + first], ACT.Exp)
        last.then_inc(m.exped, 1)

    def softmax_heads(self, tile0, sinks=False):
        m = self.m
        self.exp_pair(0, sinks)
        self.exp_pair(1, sinks)
        for h in range(8):
            self.eng.wait_ge(m.probs_turned, self.w.next(m.probs_turned))
            self.eng.wait_ge(m.weighed, self.w.reuse(m.weighed))
            self.isa.copy(m.probsT[:, h % 2, :], m.bank[4 + h % 2][:, 0:384]).then_inc(m.pt_ready, 1)
            if h >= 1:
                self.oT_high(h - 1, tile0)
            if h in (2, 3):
                self.exp_pair(h, sinks)
        self.oT_high(7, tile0)

    def oT_high(self, h, tile0):
        m = self.m
        if h % 2:
            self.eng.wait_ge(m.weighed, self.w.next(m.weighed, 2))
            self.isa.copy(m.oT_hi[:, tile0 + h // 2, :], m.bank[6 + (h // 2) % 2][:, 0:S]).then_inc(m.act_hi, 1)

    def stick_heads(self, tile0):
        m = self.m

        def magnitude(h):
            if h >= 4:
                self.settle()
            self.eng.wait_ge(m.to_act[h % 4], self.w.next(m.to_act[h % 4]))
            self.isa.activation(m.probs[:, h % 4, :], m.bank[h % 4][:, 0:384], ACT.Abs)

        self.settle()
        self.eng.wait_ge(m.probs_free, self.w.next(m.probs_free))
        for h in range(4):
            magnitude(h)
        for g in range(2):
            self.settle()
            for hh in range(4):
                self.isa.activation(m.probs[:, hh, :], m.probs[:, hh, :], ACT.Exp, scale=-1.0)
            if g:
                self.oT_high(3, tile0)
            self.settle()
            for hh in range(4):
                self.isa.activation(m.probs[:, hh, :], m.probs[:, hh, :], ACT.Ln, bias=1.0).then_inc(m.l_ready, 1)
            for hh in range(4):
                self.eng.wait_ge(m.logw_ready, self.w.next(m.logw_ready))
                self.eng.wait_ge(m.weighed, self.w.reuse(m.weighed))
                self.isa.activation(m.probsT[:, hh % 2, :], m.probs[:, hh, :], ACT.Exp).then_inc(m.pt_ready, 1)
                if hh == 2:
                    self.oT_high(4 * g + 1, tile0)
                if g == 0:
                    magnitude(4 + hh)
        self.oT_high(7, tile0)


class Vector(Engine):

    def settle(self):
        self.eng.drain()

    def split(self, n=1):
        m = self.m
        for _ in range(n):
            raw, slot, _, number = self.w.take()
            self.eng.wait_ge(m.hi_ready, number + 1)
            self.isa.tensor_tensor(m.w_lo[:, slot, :], m.raw[:, raw, :], m.w_hi[:, slot, :].bitcast(F32),
                                   ALU.subtract).then_inc(m.lo_ready, 1)

    def low_turned(self, banks, hi, lo, scales=None, tiles=range(KT)):
        m = self.m
        for j, b in enumerate(banks):
            self.eng.wait_ge(m.act_hi, self.w.next(m.act_hi))
            for k in range(2 * j, min(2 * j + 2, len(tiles))):
                at = (k % 2) * S
                src = m.bank[b][:, at:at + S]
                h = hi[:, tiles[k], :].bitcast(F32)
                if scales is None:
                    last = self.isa.tensor_tensor(lo[:, tiles[k], :], src, h, ALU.subtract)
                else:
                    last = self.isa.scalar_tensor_tensor(lo[:, tiles[k], :], src, scales[:, k:k + 1], h,
                                                         ALU.mult, ALU.subtract)
            last.then_inc(m.free[b], 1)
            self.eng.drain().then_inc(m.hT_ready, 1)

    def mean_squares(self, width, eps):
        m = self.m
        self.eng.wait_ge(m.squares, self.w.next(m.squares))
        self.isa.tensor_tensor(m.small[:, 0:2], m.small[:, 0:2], m.small[:, 6:8], ALU.add)
        self.settle()
        self.isa.tensor_scalar(m.small[:, 2:4], m.small[:, 0:2], 1.0 / width, eps, ALU.mult, ALU.add) \
            .then_inc(m.rstd_in, 1)
        self.eng.wait_ge(m.rstd, self.w.next(m.rstd))

    def rms_rows(self):
        m = self.m
        self.mean_squares(D, 1e-6)
        self.isa.tensor_scalar(m.nat[:, 0, :], m.x[:, 0, :], m.small[:, 4:5], None, ALU.mult) \
            .then_inc(m.nat_ready, 1)

    def roped(self, b, tile, n, cos, sin, scratch=None):
        m = self.m
        self.settle()
        self.eng.wait_ge(m.to_dve[b], self.w.next(m.to_dve[b]))
        dst = m.arena[:, tile * S:(tile + n) * S].rearrange("p (n s) -> p n s", n=n)
        rot = m.bank[b][:, 0:n * S].rearrange("p (n s) -> p n s", n=n)
        tmp = m.probs[:, 0:2, 0:S] if scratch is None else scratch.rearrange("p (n s) -> p n s", s=S)
        tmp = tmp[:, 0:n, :]
        c = cos.unsqueeze(1).to_broadcast([P, n, S])
        s = sin.unsqueeze(1).to_broadcast([P, n, S])
        self.isa.tensor_tensor(dst, dst, c, ALU.mult)
        self.isa.tensor_tensor(tmp, rot, s, ALU.mult).then_inc(m.free[b], 1)
        self.settle()
        self.isa.tensor_tensor(dst, dst, tmp, ALU.add).then_inc(m.roped, 1)

    def maxima(self, h, mask, first):
        m = self.m
        b, hh = h % 4, h % 4
        self.settle()
        self.eng.wait_ge(m.to_dve[b], self.w.next(m.to_dve[b]))
        self.eng.wait_ge(m.probs_turned, self.w.reuse(m.probs_turned))
        self.isa.memset(m.small[:, 10:11], 0.0)
        for t, a, e, mk in ((0, 0, P, mask[:, P:S]), (1, P, 384, mask)):
            i = 2 * hh + t
            last = self.isa.tensor_tensor_reduce(m.probs[:, hh, a:e], m.bank[b][:, a:e], mk, self.scale, first(h),
                                                 ALU.add, ALU.max, m.small[:, 16 + i:17 + i])
        last.then_inc(m.free[b], 1)

    def softmax_heads(self, tile0, mask, scale, sink=None):
        m = self.m
        self.scale = scale

        def subtrahends(pair):
            first = 4 * (pair % 2)
            for hh in (2 * pair, 2 * pair + 1):
                self.maxima(hh, mask, lambda h: NEG if sink is None else sink[:, h:h + 1])
            self.settle()
            maxi = m.small[:, 16 + first:20 + first]
            if sink is not None:
                by_token = [a.rearrange("p (h t) -> p h t", t=TT) for a in (m.small[:, 48 + first:52 + first], maxi)]
                for t in range(TT):
                    self.isa.tensor_tensor(by_token[0][:, :, t], sink[:, 2 * pair:2 * pair + 2], by_token[1][:, :, t],
                                           ALU.subtract)
            self.isa.tensor_scalar(m.small[:, 24 + first:28 + first], maxi, -1.0, None, ALU.mult)
            self.eng.drain().then_inc(m.negm, 1)

        def divided(pair):
            first = 4 * (pair % 2)
            sums = m.small[:, 32 + first:36 + first]
            self.eng.wait_ge(m.exped, self.w.next(m.exped))
            if sink is not None:
                self.isa.tensor_tensor(sums, sums, m.small[:, 40 + first:44 + first], ALU.add)
                self.settle()
            self.isa.reciprocal(sums, sums)
            self.settle()
            for i in range(first, first + 4):
                a, b = ((0, P), (P, 384))[i % 2]
                last = self.isa.tensor_scalar(m.probs[:, i // 2, a:b], m.probs[:, i // 2, a:b],
                                              m.small[:, 32 + i:33 + i], None, ALU.mult)
                if i % 2:
                    last.then_inc(m.probs_ready, 1)

        subtrahends(0)
        subtrahends(1)
        divided(0)
        divided(1)
        subtrahends(2)
        subtrahends(3)
        self.oT_low(0, tile0)
        divided(2)
        divided(3)
        for pair in (1, 2, 3):
            self.oT_low(pair, tile0)

    def oT_low(self, pair, tile0):
        m = self.m
        b = 6 + pair % 2
        self.eng.wait_ge(m.act_hi, self.w.next(m.act_hi))
        self.isa.tensor_tensor(m.oT_lo[:, tile0 + pair, :], m.bank[b][:, 0:S],
                               m.oT_hi[:, tile0 + pair, :].bitcast(F32), ALU.subtract).then_inc(m.free[b], 1)

    def stick_heads(self, tile0, neg):
        m = self.m
        self.settle()
        self.eng.wait_ge(m.probs_turned, self.w.all_free(m.probs_turned))
        self.isa.memset(m.small[:, 11:12], 0.0).then_inc(m.probs_free, 1)
        for g in range(2):
            for hh in range(4):
                a = m.probs[:, hh, :]
                self.eng.wait_ge(m.l_ready, self.w.next(m.l_ready))
                self.isa.scalar_tensor_tensor(a, m.bank[hh][:, 0:384], 0.0, a, ALU.max, ALU.add) \
                    .then_inc(m.n_ready, 1)
            for hh in range(4):
                self.eng.wait_ge(m.to_dve[hh], self.w.next(m.to_dve[hh]))
                self.isa.tensor_tensor(m.probs[:, hh, :], m.bank[hh][:, 0:384], neg, ALU.add) \
                    .then_inc(m.logw_ready, 1)
                self.eng.drain().then_inc(m.free[hh], 1)
            self.oT_low(2 * g, tile0)
            self.oT_low(2 * g + 1, tile0)


class Pool(Engine):

    def power(self, a, b):
        m = self.m
        n = a[1] - a[0]
        self.eng.wait_ge(m.rstd_in, self.w.next(m.rstd_in))
        self.isa.tensor_tensor(m.small[:, b:b + n], m.small[:, a[0]:a[1]], m.small[:, HALF:HALF + n], ALU.pow) \
            .then_inc(m.rstd, 1)

    def stick_heads(self, before):
        m = self.m
        for h in range(8):
            a = m.probs[:, h % 4, :]
            self.eng.wait_ge(m.n_ready, self.w.next(m.n_ready))
            self.isa.tensor_tensor(a, a, before, ALU.mult).then_inc(m.lom_ready, 1)



A_QKV = [
    ("turned", QA, 4, 0), ("turned", QA + 2, 5, 1), ("k and v", KA, 6, 2),
    ("turned", QB, 7, None), ("turned", QB + 2, 4, None), ("turned", KB, 5, None), ("turned", KB + 2, 6, None),
    ("rows", P, (7, 4), None),
    ("turned", QC, 5, 3), ("turned", QC + 2, 6, 0), ("turned", KC, 7, 1), ("turned", KC + 2, 4, 2),
    ("rows", P + 512, (5, 6), None),
]
A_V = A_TILES * S
A_VW = P + 512 + 512
NORM_MIX, NORM_FFN, CONV, SINKS, A_PARAMS = 0, 8, 16, 16 + 16 * FF_SUBS, 24 + 16 * FF_SUBS


def a_tile(m, i, n=1):
    return m.arena[:, i * S:(i + n) * S]


def a_v(m, t, a, b):
    return m.arena[:, A_V + t * A_VW + a:A_V + t * A_VW + b]


class TensorA(Tensor):
    def layer(self):
        m, w = self.m, self.w
        ident, rot = m.tab(A_TABLES, "ident"), m.tab(A_TABLES, "rot64")
        hT = (m.hT_hi, m.hT_lo)
        oT = (m.oT_hi, m.oT_lo)
        self.stay_warm()
        self.eng.wait_ge(m.nat_ready, w.next(m.nat_ready, 2))
        self.turn_rows(m.nat, (0, 1, 2, 3), ident)
        self.coming = {0, 2, 4, 6}

        def rotation(job):
            kind, tile, _, b = job
            if b is not None:
                n = 1 if kind == "k and v" else 2
                self.rotate(a_tile(m, tile, n), b, rot, n)

        for i, (kind, tile, b, _) in enumerate(A_QKV):
            if kind == "rows":
                banks = [self.bank(x) for x in b]
                for half in range(2):
                    last = self.rows(banks, self.chunk(), 512, hT, 4, 4 * half, KT)
                    if half == 0:
                        self.used(last)
                self.used(last)
            else:
                bank, c = self.bank(b), self.chunk()
                if kind == "turned":
                    last = self.turned([bank[:, 0:S], bank[:, S:2 * S]], c, S, hT, KT)
                else:
                    self.turned([bank[:, 0:S]], c, S, hT, KT)
                    for t in range(TT):
                        last = self.rows([bank[:, S + t * P:S + (t + 1) * P]], c, S, hT, KT, 0, KT, col=P, n=P, t0=t)
                self.used(last)
            if i:
                rotation(A_QKV[i - 1])
        rotation(A_QKV[-1])

        self.eng.wait_ge(m.roped, w.next(m.roped, 3))
        self.softmax_heads(
            lambda h: [(a_tile(m, QA + h % 4)[(h // 4) * DH:(h // 4 + 1) * DH, :],
                        a_tile(m, KA)[(h // 4) * DH:(h // 4 + 1) * DH, :])],
            lambda h: [a_v(m, t, (h // 4) * DH, (h // 4 + 1) * DH) for t in range(TT)], ident)
        self.eng.wait_ge(m.copied, w.next(m.copied, 6))
        self.stick_heads(
            lambda h: a_tile(m, QB + h // 2)[(h % 2) * DH:(h % 2 + 1) * DH, :],
            lambda h: a_tile(m, KB + h // 2)[(h % 2) * DH:(h % 2 + 1) * DH, :],
            lambda h: [a_v(m, t, P + h * DH, P + (h + 1) * DH) for t in range(TT)],
            m.tab(A_TABLES, "tri"), m.tab(A_TABLES, "ones"))
        self.eng.wait_ge(m.roped, w.next(m.roped, 4))
        self.eng.wait_ge(m.copied, w.next(m.copied, 2))
        self.softmax_heads(
            lambda h: [(a_tile(m, QC + h // 2)[(h % 2) * DH:(h % 2 + 1) * DH, :],
                        a_tile(m, KC + h // 2)[(h % 2) * DH:(h % 2 + 1) * DH, :])],
            lambda h: [a_v(m, t, P + 512 + h * DH, P + 512 + (h + 1) * DH) for t in range(TT)], ident)

        self.eng.wait_ge(m.oT_ready, w.next(m.oT_ready))
        for u in range(6):
            base = 4 * (u % 2)
            gates = [self.bank(base), self.bank(base + 1)]
            for half in range(2):
                self.used(self.rows(gates, self.chunk(), 512, hT, 4, 4 * half, KT))
            outs = [self.bank(base + 2), self.bank(base + 3)]
            branch = tuple(a[:, 4 * (u // 2):4 * (u // 2) + 4, :] for a in oT)
            self.used(self.rows(outs, self.chunk(), 512, branch, 4, 0, 4))
        self.stay_warm(WARM // 3)
        self.eng.wait_ge(m.nat_ready, w.next(m.nat_ready))
        self.turn_rows(m.nat, (0, 1, 2, 3), ident)
        self.coming = {0, 2, 4, 6}
        self.project((2, 2, 1, 1, 1, 1))
        self.stay_warm()
        self.eng.wait_ge(m.nat_ready, w.next(m.nat_ready, 2))
        self.turn_rows(m.nat, (0, 1, 2, 3), ident)
        self.coming = {0, 2, 4, 6}
        self.feed_forward()

    def project(self, tiles, x=None):
        m = self.m
        acc = [self.bank(b) for b in (4, 5, 6, 7)]
        k0 = 0
        for kt in tiles:
            c = self.chunk()
            for half in range(2):
                last = self.rows(acc[2 * half:2 * half + 2], c, D, x or (m.hT_hi, m.hT_lo), kt, k0, KT, col=512 * half)
                if half == 0 and k0 + kt == KT:
                    last.then_inc(m.to_dve[4], 1)
            self.used(last)
            k0 += kt

    def up(self, p):
        m = self.m
        for b in (2 * p, 2 * p + 1):
            bank = self.bank(b)
            self.used(self.turned([bank[:, 0:S], bank[:, S:2 * S]], self.chunk(), S, (m.hT_hi, m.hT_lo), KT))

    def down(self, p, last_step=False):
        m = self.m
        self.eng.wait_ge(m.hid_ready, self.w.next(m.hid_ready))
        c = self.chunk()
        hid = (m.oT_hi[:, 2 * p:2 * p + 2, :], m.oT_lo[:, 2 * p:2 * p + 2, :])
        for half in range(2):
            last = self.rows([m.bank[4 + 2 * half], m.bank[5 + 2 * half]], c, D, hid, 2, 0, 2 if last_step else 3,
                             col=512 * half, opened=True)
            if half == 0 and last_step:
                last.then_inc(m.to_dve[4], 1)
        self.used(last)

    def feed_forward(self):
        m = self.m
        for b in (4, 5, 6, 7):
            self.zero(b)
        self.up(0)
        with self.w.repeat((FF_SUBS - 1) // 2, PE_FFN_TURN):
            for p in (1, 0):
                self.up(p)
                self.down(1 - p)
        self.down(0, last_step=True)


class ScalarA(Scalar):
    def layer(self):
        m = self.m
        self.eng.wait_ge(m.cols_ready, self.w.next(m.cols_ready))
        self.high_turned((0, 1, 2, 3), m.hT_hi, m.cols[:, NORM_MIX:NORM_MIX + KT])
        for kind, tile, b, rot in A_QKV:
            if kind == "rows":
                self.split(2)
                self.eng.wait_ge(m.w_used, self.w.product_done())
                for t in range(TT):
                    self.copy_out(b[t], [(a_v(m, t, tile, tile + 512), m.bank[b[t]][:])], m.copied)
            elif kind == "turned":
                self.split(1)
                self.eng.wait_ge(m.w_used, self.w.product_done())
                self.copy_out(b, [(a_tile(m, tile, 2), m.bank[b][:])], m.kq_copied if rot is not None else m.copied,
                              SCALE if tile in (QB, QB + 2) else 1.0)
            else:
                self.split(1)
                self.eng.wait_ge(m.w_used, self.w.product_done())
                self.copy_out(b, [(a_tile(m, tile), m.bank[b][:, 0:S])]
                              + [(a_v(m, t, 0, P), m.bank[b][:, S + t * P:S + (t + 1) * P]) for t in range(TT)],
                              m.kq_copied)
        self.softmax_heads(0, sinks=True)
        self.stick_heads(4)
        self.softmax_heads(8)
        for u in range(6):
            self.split(2)
            for t in range(TT):
                self.eng.wait_ge(m.gate_in, self.w.next(m.gate_in))
                g = gate_rows(m, t)
                self.isa.activation(g, g, ACT.Sigmoid).then_inc(m.gate_out, 1)
            self.split(1)
        self.high_turned((0, 1, 2, 3), m.hT_hi)
        self.split(6)
        self.squares()
        self.scaled_rows()
        self.high_turned((0, 1, 2, 3), m.hT_hi, m.cols[:, NORM_FFN:NORM_FFN + KT])
        self.split(2)
        self.hidden(0)
        with self.w.repeat((FF_SUBS - 1) // 2, ACT_FFN_TURN):
            for p in (1, 0):
                self.split(2)
                self.hidden(p, 1)
        self.split(1)
        self.squares()
        self.scaled_rows()

    def hidden(self, p, ahead=0):
        m = self.m
        self.eng.wait_ge(m.silu_in, self.w.next(m.silu_in))
        g = hidden_gate(m)
        self.isa.activation(g, g, ACT.Silu).then_inc(m.silu_done, 1)
        self.split(ahead)
        self.eng.wait_ge(m.hid, self.w.next(m.hid))
        self.isa.copy(m.oT_hi[:, 2 * p:2 * p + 2, :], hidden_value(m)).then_inc(m.hid_hi, 1)


def gate_rows(m, t):
    return m.probs[:, :, :].rearrange("p a b -> p (a b)")[:, t * 512:(t + 1) * 512]


def hidden_gate(m):
    return m.probs[:, :, :].rearrange("p a b -> p (a b)")[:, 0:512]


def hidden_value(m):
    return m.probs[:, :, :].rearrange("p a b -> p (a b)")[:, 512:1024].rearrange("p (a b) -> p a b", a=2)


class VectorA(Vector):
    def layer(self, layer):
        m, w = self.m, self.w
        self.isa.tensor_copy(m.cols[:, 0:A_PARAMS], m.all_cols[:, bass.ds(layer * A_PARAMS, A_PARAMS)]) \
            .then_inc(m.cols_ready, 1)
        sinks = m.cols[:, SINKS:SINKS + 8]
        self.low_turned((0, 1, 2, 3), m.hT_hi, m.hT_lo, m.cols[:, NORM_MIX:NORM_MIX + KT])
        cos, sin = m.tab(A_TABLES, "cos64"), m.tab(A_TABLES, "sin64")

        def rope(job):
            kind, tile, _, b = job
            if b is not None:
                self.roped(b, tile, 1 if kind == "k and v" else 2, cos, sin)

        for i, job in enumerate(A_QKV):
            self.split(2 if job[0] == "rows" else 1)
            if i:
                rope(A_QKV[i - 1])
        rope(A_QKV[-1])
        self.eng.wait_ge(m.tables_loaded, 16)
        self.softmax_heads(0, m.tab(A_TABLES, "band"), SCALE, sinks)
        self.stick_heads(4, m.tab(A_TABLES, "before"))
        self.softmax_heads(8, m.tab(A_TABLES, "causal"), SCALE)
        self.eng.drain().then_inc(m.oT_ready, 1)
        self.eng.wait_ge(m.probs_turned, w.all_free(m.probs_turned))
        self.eng.wait_ge(m.rows_loaded, w.next(m.rows_loaded, 32))
        for u in range(6):
            i, half, base = u // 2, u % 2, 4 * (u % 2)
            bias = m.arena[:, i * D + 512 * half:i * D + 512 * half + 512]
            self.split(2)
            self.settle()
            self.eng.wait_ge(m.w_used, self.w.product_done())
            for t in range(TT):
                self.isa.tensor_tensor(gate_rows(m, t), m.bank[base + t][:], bias, ALU.add).then_inc(m.gate_in, 1)
                self.eng.drain().then_inc(m.free[base + t], 1)
            self.split(1)
            self.eng.wait_ge(m.w_used, self.w.product_done())
            for t in range(TT):
                self.eng.wait_ge(m.gate_out, w.next(m.gate_out))
                out = m.nat[:, t, 512 * half:512 * half + 512]
                dst = gate_rows(m, t) if i else out
                self.isa.tensor_tensor(dst, gate_rows(m, t), m.bank[base + 2 + t][:], ALU.mult) \
                    .then_inc(m.free[base + 2 + t], 1)
                if i:
                    self.settle()
                    self.isa.tensor_tensor(out, out, dst, ALU.add)
        self.eng.drain().then_inc(m.nat_ready, 1)
        self.low_turned((0, 1, 2, 3), m.hT_hi, m.hT_lo)
        self.split(6)
        self.add_banks()
        self.rms_rows()
        self.low_turned((0, 1, 2, 3), m.hT_hi, m.hT_lo, m.cols[:, NORM_FFN:NORM_FFN + KT])
        self.hidden(0, 0)
        with w.repeat((FF_SUBS - 1) // 2, DVE_FFN_TURN) as i:
            for n, p in enumerate((1, 0)):
                self.hidden(p, i * 2 + (n + 1), 1)
        self.split(1)
        self.add_banks()
        self.rms_rows()

    def add_banks(self):
        m = self.m
        for half in range(2):
            if half == 0:
                self.eng.wait_ge(m.to_dve[4], self.w.next(m.to_dve[4]))
            else:
                self.eng.wait_ge(m.w_used, self.w.product_done())
            for t in range(TT):
                b = 4 + 2 * half + t
                x = m.x[:, t, 512 * half:512 * half + 512]
                self.isa.tensor_tensor(x, x, m.bank[b][:], ALU.add).then_inc(m.free[b], 1)
            self.eng.drain().then_inc(m.x_ready, 1)

    def conv(self, bank, dst, at):
        m = self.m

        def col(g, i):
            if type(at) is int:
                return m.cols[:, at + 4 * g + i:at + 4 * g + i + 1]
            return m.cols[:, bass.ds(at + (4 * g + i), 1)]

        for g in range(2):
            src = bank[:, g * S:(g + 1) * S]
            self.isa.tensor_scalar(dst[:, g, :], src, col(g, 2), col(g, 3), ALU.mult, ALU.add)
        for back in (1, 2):
            self.settle()
            for g in range(2):
                out = dst[:, g, back:S]
                last = self.isa.scalar_tensor_tensor(out, bank[:, g * S:(g + 1) * S - back], col(g, 2 - back), out,
                                                     ALU.mult, ALU.add)
        return last

    def hidden(self, p, j, ahead=0):
        m = self.m
        gate = hidden_gate(m).rearrange("p (a b) -> p a b", a=2)
        value = hidden_value(m)
        for b, dst, half in ((2 * p, gate, 0), (2 * p + 1, value, 1)):
            self.split(1)
            self.settle()
            self.eng.wait_ge(m.w_used, self.w.product_done())
            last = self.conv(m.bank[b], dst, j * 16 + (CONV + 8 * half))
            last.then_inc(m.silu_in if half == 0 else m.free[b], 1)
            if half == 0:
                self.eng.drain().then_inc(m.free[b], 1)
        self.settle()
        self.eng.wait_ge(m.silu_done, self.w.next(m.silu_done))
        self.isa.tensor_tensor(value, value, gate, ALU.mult).then_inc(m.hid, 1)
        self.split(ahead)
        self.eng.wait_ge(m.hid_hi, self.w.next(m.hid_hi))
        self.isa.tensor_tensor(m.oT_lo[:, 2 * p:2 * p + 2, :], value, m.oT_hi[:, 2 * p:2 * p + 2, :].bitcast(F32),
                               ALU.subtract).then_inc(m.hid_ready, 1)



RQ, RK, KR, MQ, MK, QN, QR, KN, B_TILES = 0, 2, 4, 5, 7, 9, 13, 15, 19
B_RV = B_TILES * S
B_VA = B_RV + TT * S
B_VM = B_VA + TT * 4 * (DH + 1)
B_ROWS = B_VM + TT * 512
M_BANKS = (6, 7, 4, 5)
B_EXP = 0
B_MIXER = 17
UNIT = 6 * EXP_STEPS
FIXED = DEPTH * (A_LAYER + B_MIXER) + 3 * FF_SUBS + 1
SHARED = B_TABLES["rot32"][0]
ALPHA = (2 * DEPTH) ** 0.25

LN1, LN2 = 0, 2 * D
QKV_NORM, GN, CONV4, BIAS_I, BIAS_F, B_PARAMS = 0, 3, 7, 27, 28, 29
ST, MV, VAR, RSTD8 = 96, 80, 64, 72
CSS, CMS, CRS = 144, 148, 152
AT, EN, DEN = 156, 164, 172
LG = 180


def b_tile(m, i, n=1):
    return m.arena[:, i * S:(i + n) * S]


def gate_row(m, i):
    if i < 2:
        return m.arena[0:4, B_ROWS + i * S:B_ROWS + (i + 1) * S]
    return m.probsT[0:4, i - 2, 0:S]


def r_v(m, t):
    return m.arena[:, B_RV + t * S:B_RV + (t + 1) * S]


def v_aug(m, t):
    w = 4 * (DH + 1)
    return m.arena[:, B_VA + t * w:B_VA + (t + 1) * w].rearrange("p (h d) -> p h d", h=4)


def v_mla(m, t, a=0, b=512):
    return m.arena[:, B_VM + t * 512 + a:B_VM + t * 512 + b]


def by_head(ap, h=4):
    return ap.rearrange("p (h d) -> p h d", h=h)


class TensorB(TensorA):
    def mixer(self):
        m, w = self.m, self.w
        ident = m.tab(B_TABLES, "ident")
        rot64, rot32 = m.tab(B_TABLES, "rot64"), m.tab(B_TABLES, "rot32")
        hT = (m.hT_hi, m.hT_lo)
        self.turn_x(ident)

        def two_tiles(b):
            bank = self.bank(b)
            self.used(self.turned([bank[:, 0:S], bank[:, S:2 * S]], self.chunk(), S, hT, KT))

        def two_chunks(b, n):
            banks = [self.bank(b)[:, 0:n], self.bank(b + 1)[:, 0:n]]
            for half in range(2):
                self.used(self.rows(banks, self.chunk(), n, hT, 4, 4 * half, KT, n=n))

        two_tiles(4)
        two_tiles(5)
        self.rotate(b_tile(m, RQ, 2), 0, rot64, 2)
        c, keys, gates = self.chunk(), self.bank(6), self.bank(7)
        self.turned([keys[:, 0:S]], c, P + 8, hT, KT)
        self.turned([gates[0:4, 0:S]], c, P + 8, hT, KT, col=P, m=4)
        self.used(self.turned([gates[0:4, S:2 * S]], c, P + 8, hT, KT, col=P + 4, m=4))
        self.rotate(b_tile(m, RK, 2), 1, rot64, 2)
        two_chunks(4, 512)
        self.eng.wait_ge(m.tables_b_loaded, 16)
        self.rotate(b_tile(m, KR), 2, rot32, 1)
        two_chunks(6, 384)
        two_tiles(0)
        two_tiles(1)
        self.eng.wait_ge(m.nat_ready, w.next(m.nat_ready))
        self.turn_rows(m.probs[:, 2:4, :], (2, 3), ident, 3)
        two_chunks(4, 512)
        self.eng.wait_ge(m.roped, w.next(m.roped, 2))
        self.key_rows(RQ, RK)
        self.eng.wait_ge(m.hT_ready, w.next(m.hT_ready, 2))
        c = self.chunk()
        cq, ckv = ((m.oT_hi[:, a:b, :], m.oT_lo[:, a:b, :]) for a, b in ((8, 10), (10, 11)))
        outs = []
        for b in (6, 7, 4):
            bank = self.bank(b)
            outs += [bank[:, 0:S], bank[:, S:2 * S]]
        self.used(self.turned(outs, c, 768, cq, 2))
        c, outs = self.chunk(), []
        for b in (2, 3):
            bank = self.bank(b)
            outs += [bank[:, 0:S], bank[:, S:2 * S]]
        self.turned(outs, c, D, ckv, 1)
        self.used(self.rows([self.bank(5), self.bank(0)], c, D, ckv, 1, 0, 1, col=512))
        self.rotate(b_tile(m, QR, 2), 1, rot32, 2)

        self.eng.wait_ge(m.scans_ready, w.next(m.scans_ready))
        bank = self.bank(6)
        for i, row in enumerate((gate_row(m, 2), gate_row(m, 0))):
            for t in range(TT):
                last = self.isa.transpose(bank[:, 8 * i + 4 * t:8 * i + 4 * t + 4], row[:, t * P:(t + 1) * P],
                                          ident[0:4, 0:4])
        last.then_inc(m.to_dve[6], 1)

        self.eng.wait_ge(m.copied, w.next(m.copied, 2))
        self.out_rows(lambda t, h: r_v(m, t)[:, h * DH:(h + 1) * DH], DH, (m.to_act[4], m.to_act[5]))
        self.eng.wait_ge(m.conv_out, w.next(m.conv_out, 2))
        self.key_rows(MQ, MK)
        self.eng.wait_ge(m.roped, w.next(m.roped, 2))
        for h in range(4):
            pick = ident[0:4, h:h + 1].to_broadcast([4, P])
            bank = self.bank(M_BANKS[h])
            mm = self.isa.matmul
            mm(bank[:, 0:S], pick, gate_row(m, 3), start=True, stop=False, skip_group_check=True)
            mm(bank[:, S:S + P], pick, gate_row(m, 3)[:, P:S], start=False, stop=False, skip_group_check=True)
            for at in (0, S):
                last = mm(bank[:, at:at + P], ident, m.tab(B_TABLES, "causalT"), start=False, stop=at == S,
                          skip_group_check=True)
            last.then_inc(m.to_act[M_BANKS[h]], 1)
        self.eng.wait_ge(m.copied, w.next(m.copied, 2))
        self.out_rows(lambda t, h: v_aug(m, t)[:, h, :], DH + 1, (m.to_dve[4], m.to_dve[5]))

        self.eng.wait_ge(m.copied, w.next(m.copied, 6))
        self.softmax_heads(
            lambda h: [(b_tile(m, a + h // 2)[(h % 2) * DH:(h % 2 + 1) * DH, :],
                        b_tile(m, b + h // 2)[(h % 2) * DH:(h % 2 + 1) * DH, :]) for a, b in ((QN, KN),)]
            + [(b_tile(m, QR + h // 4)[(h % 4) * 32:(h % 4 + 1) * 32, :],
                b_tile(m, KR)[(h % 4) * 32:(h % 4 + 1) * 32, :])],
            lambda h: [v_mla(m, t, h * DH, (h + 1) * DH) for t in range(TT)], ident)
        self.eng.wait_ge(m.nat_ready, w.next(m.nat_ready))
        self.turn_rows(m.nat[:, :, 0:512], (0, 1), ident, 4)
        self.coming = {0, 6}
        self.project((2, 2, 2, 2), (m.oT_hi, m.oT_lo))

    def key_rows(self, q, k):
        m = self.m
        for h in range(4):
            bank = self.bank(h)
            qh, kh = (b_tile(m, x + h // 2)[(h % 2) * DH:(h % 2 + 1) * DH, :] for x in (q, k))
            self.isa.matmul(bank[:, 0:S], kh[:, 0:P], qh, start=True, stop=False, skip_group_check=True)
            self.isa.matmul(bank[:, S:S + P], kh[:, P:S], qh[:, P:S], start=False, stop=True,
                            skip_group_check=True).then_inc(m.to_dve[h], 1)

    def out_rows(self, v_of, n, to):
        m = self.m
        banks = [self.bank(4), self.bank(5)]
        for h in range(4):
            self.eng.wait_ge(m.pairs_ready, self.w.next(m.pairs_ready))
            pt = m.probs[:, h, :]
            at = slice(h * n, (h + 1) * n)
            mm = self.isa.matmul
            first = mm(banks[0][:, at], pt[:, 0:P], v_of(0, h), start=True, stop=True, skip_group_check=True)
            mm(banks[1][:, at], pt[:, P:S], v_of(0, h), start=True, stop=False, skip_group_check=True)
            last = mm(banks[1][:, at], pt[:, S:S + P], v_of(1, h), start=False, stop=True, skip_group_check=True)
        first.then_inc(to[0], 1)
        last.then_inc(to[1], 1)

    def route(self):
        m, w = self.m, self.w
        logits = [self.bank(b)[:, 0:N_EXP] for b in range(TT)]
        self.used(self.rows(logits, self.chunk(), N_EXP, (m.hT_hi, m.hT_lo), KT, 0, KT, n=N_EXP))
        self.eng.wait_ge(m.selected, w.next(m.selected))
        bank = self.bank(2)
        below, ones = m.tab(B_TABLES, "below"), m.tab(B_TABLES, "ones")
        sel = [chosen(m, t) for t in range(TT)]
        mm = self.isa.matmul
        mm(bank[:, 0:8], below, sel[0], start=True, stop=True, skip_group_check=True)
        mm(bank[:, 8:16], ones, sel[0], start=True, stop=False, skip_group_check=True)
        mm(bank[:, 8:16], below, sel[1], start=False, stop=True, skip_group_check=True)
        mm(bank[:, 16:24], ones, sel[0], start=True, stop=False, skip_group_check=True)
        mm(bank[:, 16:24], ones, sel[1], start=False, stop=True, skip_group_check=True).then_inc(m.placed, 1)

    def experts(self):
        m, w = self.m, self.w
        self.gather()
        self.eng.wait_ge(m.units_ready, w.next(m.units_ready))
        units = self.isa.value_load(m.units[0:1, COUNT:COUNT + 1], min_val=8, max_val=11)
        self.eng.wait_ge(m.x_here, w.next(m.x_here))
        with w.repeat(units, PE_UNIT):
            self.rows_up(0)
            self.rows_up(1)
            for b in (4, 5):
                self.zero(b)
            self.scatter()
            self.turn_picks()
            with w.repeat(EXP_STEPS - 1, PE_STEP):
                self.rows_up(0)
                self.turn_hidden()
                self.rows_up(1)
                self.rows_down()
            self.turn_hidden()
            self.gather()
            self.rows_down(last_step=True)
            self.eng.wait_ge(m.x_here, w.next(m.x_here))
        self.scatter()

    def gather(self):
        m = self.m
        self.eng.wait_ge(m.picks_ready, self.w.next(m.picks_ready))
        for j, b in enumerate((6, 7)):
            bank = self.bank(b)
            for k in range(4 * j, 4 * j + 4):
                for t in range(TT):
                    last = self.isa.matmul(bank[:, (k % 4) * P:(k % 4 + 1) * P], m.x[:, t, k * P:(k + 1) * P],
                                           picks(m, t), start=t == 0, stop=t == TT - 1, skip_group_check=True)
            last.then_inc(m.to_act[b], 1)

    def rows_up(self, b):
        m = self.m
        bank = self.bank(b)
        for half in range(2):
            self.used(self.rows([bank], self.chunk(), 512, (m.hT_hi, m.hT_lo), 4, 4 * half, KT))

    def turn_hidden(self):
        m = self.m
        self.eng.wait_ge(m.h_rows, self.w.next(m.h_rows))
        bank = self.bank(2)
        for k in range(4):
            last = self.isa.transpose(bank[:, k * P:(k + 1) * P], h_rows(m)[:, k * P:(k + 1) * P],
                                      m.tab(B_TABLES, "ident"))
        last.then_inc(m.to_act[2], 1)

    def rows_down(self, last_step=False):
        m = self.m
        self.eng.wait_ge(m.hid_ready, self.w.next(m.hid_ready))
        for c in range(2):
            chunk = self.chunk()
            hid = tuple(a[:, 2 * c:2 * c + 2, 0:P] for a in (m.oT_hi, m.oT_lo))
            for half in range(2):
                last = self.rows([m.bank[4 + half]], chunk, D, hid, 2, 0, 2 if last_step and c else 3,
                                 col=512 * half, opened=True)
            self.used(last)

    def turn_picks(self):
        m = self.m
        bank = self.bank(6)
        for t in range(TT):
            last = self.isa.transpose(bank[:, t * P:(t + 1) * P], weighted(m, t), m.tab(B_TABLES, "ident"))
        last.then_inc(m.to_dve[6], 1)

    def scatter(self):
        m = self.m
        self.eng.wait_ge(m.y_rows, self.w.next(m.y_rows))
        for t, banks in ((0, (6, 7)), (1, (3, 2))):
            for half, b in enumerate(banks):
                self.isa.matmul(self.bank(b), picksT(m)[:, t * P:(t + 1) * P], y_rows(m)[:, 512 * half:512 * half + 512],
                                start=True, stop=True).then_inc(m.to_dve[b], 1)


def arena_part(at, n):
    return lambda m, t=0: m.arena[:, at + t * n:at + (t + 1) * n]


picks, weighted, picksT = arena_part(0, P), arena_part(2 * P, P), arena_part(4 * P, S)
g_rows, h_rows = arena_part(768, 512), arena_part(1280, 512)
UPOS, UGATE, ROUTE = 4 * D, 4 * D + 24, 4 * D + 48


def y_rows(m):
    return m.probs[:, :, :].rearrange("p a b -> p (a b)")[:, 0:D]


def route_part(m, i, n=16):
    return m.arena[:, ROUTE + 16 * i:ROUTE + 16 * i + n]


def chosen(m, t):
    return route_part(m, 0)[:, 8 * t:8 * t + 8]


class ScalarB(ScalarA):
    def mixer(self, layer):
        m, w = self.m, self.w
        par = m.all_cols[:, layer * B_PARAMS:(layer + 1) * B_PARAMS]
        self.high_turned((0, 1, 2, 3), m.hT_hi)
        for tile, b, n in ((RQ, 4, 2), (RK, 5, 2), (KR, 6, 1)):
            self.split(1)
            self.eng.wait_ge(m.w_used, self.w.product_done())
            self.copy_out(b, [(b_tile(m, tile, n), m.bank[b][:, 0:n * S])], m.kq_copied)
        self.split(2)
        self.eng.wait_ge(m.w_used, self.w.product_done())
        for t in range(TT):
            self.isa.activation(r_v(m, t), m.bank[4 + t][:, 0:S], ACT.Copy)
            self.isa.activation(m.nat[:, t, 512:768], m.bank[4 + t][:, S:2 * S], ACT.Silu).then_inc(m.free[4 + t], 1)
            self.eng.drain().then_inc(m.copied, 1)
        self.split(2)
        self.eng.wait_ge(m.w_used, self.w.product_done())
        for t in range(TT):
            c = m.probs[:, 2 + t, :]
            self.isa.activation(c, m.bank[6 + t][:, 0:384], ACT.Copy)
            self.settle()
            self.isa.activation(m.bank[6 + t][:, 0:S], c[:, 0:S], ACT.Square, accum_out=m.small[:, CSS + t:CSS + t + 1])
            self.isa.activation(m.bank[6 + t][:, S:S + P], c[:, S:S + P], ACT.Square,
                                accum_out=m.small[:, CSS + 2 + t:CSS + 3 + t])
            self.eng.drain().then_inc(m.free[6 + t], 1)
        self.eng.drain().then_inc(m.squares, 1)
        self.split(2)
        z, l = gate_row(m, 0), gate_row(m, 1)
        self.eng.wait_ge(m.z_ready, w.next(m.z_ready))
        self.isa.activation(l, z, ACT.Abs)
        self.settle()
        self.isa.activation(l, l, ACT.Exp, scale=-1.0)
        self.settle()
        self.isa.activation(l, l, ACT.Ln, bias=1.0).then_inc(m.l_ready, 1)
        for tile in (MQ, MK):
            if tile == MK:
                self.eng.wait_ge(m.cols_b_loaded, 16)
                self.high_turned((2, 3), m.oT_hi, par[:, QKV_NORM:QKV_NORM + 3], (8, 9, 10))
            self.eng.wait_ge(m.conv_in, w.next(m.conv_in))
            self.isa.activation(b_tile(m, tile, 2), b_tile(m, tile, 2), ACT.Silu).then_inc(m.conv_out, 1)
        self.split(2)
        self.eng.wait_ge(m.w_used, self.w.product_done())
        for t in range(TT):
            self.isa.activation(v_aug(m, t)[:, :, 0:DH], by_head(m.bank[4 + t][:, 0:S]), ACT.Copy)
            self.isa.activation(m.nat[:, t, 768:D], m.bank[4 + t][:, S:2 * S], ACT.Sigmoid).then_inc(m.free[4 + t], 1)
            self.eng.drain().then_inc(m.copied, 1)
        self.split(1)
        self.eng.wait_ge(m.w_used, self.w.product_done())
        for b, tile, to in ((4, QR, m.kq_copied), (6, QN, m.copied), (7, QN + 2, m.copied)):
            self.copy_out(b, [(b_tile(m, tile, 2), m.bank[b])], to)
        self.split(1)
        self.eng.wait_ge(m.w_used, self.w.product_done())
        for b, tile in ((2, KN), (3, KN + 2)):
            self.copy_out(b, [(b_tile(m, tile, 2), m.bank[b])], m.copied)
        for t, b in ((0, 5), (1, 0)):
            self.copy_out(b, [(v_mla(m, t), m.bank[b])], m.copied)
        for t in range(TT):
            self.eng.wait_ge(m.to_act[4 + t], w.next(m.to_act[4 + t]))
            self.copy_out(4 + t, [(m.nat[:, t, 0:S], m.bank[4 + t][:, 0:S])], m.kept)
        self.eng.wait_ge(m.cols_turned, w.next(m.cols_turned))
        w.skip(m.pairs_ready, 4)
        self.isa.activation(m.small[:, EN:EN + 8], m.small[:, EN:EN + 8], ACT.Exp)
        for h in range(4):
            if h >= 2:
                self.settle()
                self.eng.wait_ge(m.pairs_ready, w.next(m.pairs_ready))
            bank = M_BANKS[h]
            self.eng.wait_ge(m.to_act[bank], w.next(m.to_act[bank]))
            e = decays(m, h)
            for a, b, t in ((0, S, 0), (S, 384, 1)):
                last = self.isa.activation(e[:, a:b], m.bank[bank][:, a:b], ACT.Exp, scale=-1.0,
                                           bias=m.small[:, AT + 4 * t + h:AT + 4 * t + h + 1])
            last.then_inc(m.free[bank], 1)
            self.eng.drain().then_inc(m.decay_ready, 1)
        w.skip(m.pairs_ready, 2)
        self.softmax_heads(2)
        self.high_turned((0, 1), m.oT_hi, par[:, GN:GN + 4], (0, 1, 6, 7))
        self.split(4)

    def feed_forward(self):
        m, w = self.m, self.w
        self.high_turned((0, 1, 2, 3), m.hT_hi)
        self.hidden(0)
        with w.repeat((FF_SUBS - 1) // 2, ACT_SWIGLU_TURN):
            for p in (1, 0):
                self.hidden(p, 1)
        self.split(1)

    def hidden(self, p, ahead=0):
        m = self.m
        self.split(1)
        self.settle()
        self.eng.wait_ge(m.w_used, self.w.product_done())
        self.isa.activation(hidden_gate(m), m.bank[2 * p], ACT.Silu).then_inc(m.silu_done, 1)
        self.eng.drain().then_inc(m.free[2 * p], 1)
        self.split(1 + ahead)
        self.eng.wait_ge(m.hid, self.w.next(m.hid))
        self.isa.copy(m.oT_hi[:, 2 * p:2 * p + 2, :], hidden_value(m)).then_inc(m.hid_hi, 1)

    def experts(self):
        m, w = self.m, self.w
        self.high_turned((0, 1, 2, 3), m.hT_hi)
        self.split(1)
        self.eng.wait_ge(m.d_ready, w.next(m.d_ready))
        d = route_part(m, 10, 2)
        self.isa.activation(d, d, ACT.Exp).then_inc(m.e_ready, 1)
        self.gathered()
        self.eng.wait_ge(m.units_ready, w.next(m.units_ready))
        units = self.isa.value_load(m.units[0:1, COUNT:COUNT + 1], min_val=8, max_val=11)
        with w.repeat(units, ACT_UNIT):
            self.split(2)
            self.gate_rows()
            self.split(2)
            with w.repeat(EXP_STEPS - 1, ACT_STEP):
                self.split(2)
                self.gate_rows()
                self.hidden_turned()
                self.split(4)
            self.hidden_turned()
            self.gathered()
            self.split(2)
            self.eng.wait_ge(m.w_used, self.w.product_done())
            for half in range(2):
                self.isa.activation(y_rows(m)[:, 512 * half:512 * half + 512], m.bank[4 + half], ACT.Copy) \
                    .then_inc(m.free[4 + half], 1)
            self.eng.drain().then_inc(m.y_rows, 1)

    def gate_rows(self):
        m = self.m
        self.eng.wait_ge(m.h_rows, self.w.reuse(m.h_rows))
        self.eng.wait_ge(m.w_used, self.w.product_done())
        self.isa.activation(g_rows(m), m.bank[0], ACT.Silu).then_inc(m.silu_done, 1)
        self.eng.drain().then_inc(m.free[0], 1)

    def hidden_turned(self):
        m = self.m
        self.eng.wait_ge(m.to_act[2], self.w.next(m.to_act[2]))
        self.isa.copy(m.oT_hi[:, 0:4, 0:P], by_head(m.bank[2])).then_inc(m.hid_hi, 1)

    def gathered(self):
        m = self.m
        for j, b in enumerate((6, 7)):
            self.eng.wait_ge(m.to_act[b], self.w.next(m.to_act[b]))
            self.isa.copy(m.hT_hi[:, 4 * j:4 * j + 4, 0:P], by_head(m.bank[b])).then_inc(m.act_hi, 1)


def decays(m, h):
    return m.arena[:, B_EXP + (h % 2) * 512:B_EXP + (h % 2) * 512 + 384]


class VectorB(VectorA):
    def normed_start(self):
        m = self.m
        self.w.skip(m.nat_ready, 5 * DEPTH)
        self.eng.wait_ge(m.nat_ready, self.w.next(m.nat_ready, 2))
        for t in range(TT):
            self.isa.memset(v_aug(m, t)[:, :, DH], 1.0)
            self.isa.tensor_tensor(m.x[:, t, :], m.nat[:, t, :], m.arena[:, 3 * D:4 * D], ALU.mult).then_inc(m.nat_ready, 1)

    def mixer(self, layer):
        m, w = self.m, self.w
        par = m.all_cols[:, layer * B_PARAMS:(layer + 1) * B_PARAMS]
        self.low_turned((0, 1, 2, 3), m.hT_hi, m.hT_lo)
        cos64, sin64 = m.tab(B_TABLES, "cos64"), m.tab(B_TABLES, "sin64")
        cos32, sin32 = m.tab(B_TABLES, "cos32"), m.tab(B_TABLES, "sin32")
        self.split(3)
        self.eng.wait_ge(m.cols_b_loaded, 16)
        self.eng.wait_ge(m.w_used, self.w.product_done())
        gates = m.bank[7][0:4, :]
        self.isa.tensor_scalar(gate_row(m, 2), gates[:, 0:S], par[0:4, BIAS_I:BIAS_I + 1], None, ALU.add)
        self.isa.tensor_scalar(gate_row(m, 0), gates[:, S:2 * S], par[0:4, BIAS_F:BIAS_F + 1], None, ALU.add) \
            .then_inc(m.free[7], 1)
        self.eng.drain().then_inc(m.z_ready, 1)
        self.roped(0, RQ, 2, cos64, sin64)
        self.split(2)
        self.roped(1, RK, 2, cos64, sin64)
        self.split(2)
        self.settle()
        self.eng.wait_ge(m.tables_b_loaded, 16)
        self.roped(2, KR, 1, cos32, sin32)
        self.eng.wait_ge(m.squares, w.next(m.squares))
        self.isa.tensor_scalar(m.small[:, CMS:CMS + 2], m.small[:, CSS:CSS + 2], 1 / 256, 1e-5, ALU.mult, ALU.add)
        self.isa.tensor_scalar(m.small[:, CMS + 2:CMS + 4], m.small[:, CSS + 2:CSS + 4], 1 / P, 1e-5, ALU.mult, ALU.add)
        self.eng.drain().then_inc(m.rstd_in, 1)
        self.eng.wait_ge(m.rstd, w.next(m.rstd))
        for t in range(TT):
            c = m.probs[:, 2 + t, :]
            for a, b, i in ((0, S, t), (S, 384, 2 + t)):
                self.isa.tensor_scalar(c[:, a:b], c[:, a:b], m.small[:, CRS + i:CRS + i + 1], None, ALU.mult)
        self.eng.drain().then_inc(m.nat_ready, 1)
        for tile, b in ((MQ, 0), (MK, 1)):
            self.split(1)
            self.settle()
            self.eng.wait_ge(m.w_used, self.w.product_done())
            self.conv4(m.bank[b], b_tile(m, tile, 2), par[:, CONV4 + 5 * (tile - MQ):CONV4 + 5 * (tile - MQ) + 10])
            self.eng.drain().then_inc(m.free[b], 1)
        self.low_turned((2, 3), m.oT_hi, m.oT_lo, par[:, QKV_NORM:QKV_NORM + 3], (8, 9, 10))
        self.split(2)
        r0, r1, r2, r3 = (gate_row(m, i) for i in range(4))
        self.isa.tensor_scalar(m.small[0:4, 11:12], m.small[0:4, 11:12], 0.0, None, ALU.mult)
        self.eng.wait_ge(m.l_ready, w.next(m.l_ready))
        self.isa.tensor_scalar(r0, r0, -1.0, 0.0, ALU.mult, ALU.max)
        self.settle()
        self.isa.tensor_tensor(r0, r0, r1, ALU.add)
        self.settle()
        one = m.tab(B_TABLES, "ones")[0:4, 0:1].to_broadcast([4, S])
        self.isa.tensor_tensor_scan(r1, one, r0, 0.0, ALU.mult, ALU.add)
        self.settle()
        self.isa.tensor_tensor(r2, r2, r1, ALU.add)
        self.settle()
        self.isa.tensor_tensor_scan(r3, r2, r2, NEG, ALU.max, ALU.max)
        self.settle()
        self.isa.tensor_tensor(r0, r1, r3, ALU.subtract)
        self.eng.drain().then_inc(m.scans_ready, 1)
        for h in range(4):
            self.eng.wait_ge(m.to_dve[h], w.next(m.to_dve[h]))
            if h == 0:
                self.eng.wait_ge(m.probs_turned, w.all_free(m.probs_turned))
            decay = m.tab(B_TABLES, "decay", h * S, (h + 1) * S)
            self.isa.tensor_tensor(m.probs[:, h, 0:S], m.bank[h][:, 0:S], decay, ALU.mult)
            self.isa.tensor_tensor(m.probs[:, h, S:384], m.bank[h][:, S:384], decay[:, 0:P], ALU.mult) \
                .then_inc(m.free[h], 1)
            self.eng.drain().then_inc(m.pairs_ready, 1)
        self.split(2)
        self.roped(1, QR, 2, cos32, sin32, b_tile(m, RQ, 2))
        self.eng.wait_ge(m.to_dve[6], w.next(m.to_dve[6]))
        self.isa.tensor_copy(m.small[:, AT:AT + 16], m.bank[6][:, 0:16]).then_inc(m.free[6], 1)
        self.eng.drain().then_inc(m.cols_turned, 1)
        ret_rows = [by_head(m.nat[:, t, 0:S]) for t in range(TT)]
        for t in range(TT):
            self.eng.wait_ge(m.kept, w.next(m.kept))
            self.head_stats(t, ret_rows[t])
        self.head_variances()
        for h in range(4):
            self.settle()
            self.eng.wait_ge(m.decay_ready, w.next(m.decay_ready))
            self.eng.wait_ge(m.to_dve[h], w.next(m.to_dve[h]))
            self.isa.scalar_tensor_tensor(m.probs[:, h, :], m.bank[h][:, 0:384], SCALE, decays(m, h),
                                          ALU.mult, ALU.mult).then_inc(m.pairs_ready, 1)
            self.eng.drain().then_inc(m.free[h], 1)
        self.head_norm(lambda t: ret_rows[t], 0)
        for t in range(TT):
            self.isa.tensor_tensor(m.nat[:, t, 0:S], m.nat[:, t, 0:S], m.nat[:, t, 512:768], ALU.mult)
        for t in range(TT):
            out = by_head(m.bank[4 + t][:, 0:4 * (DH + 1)])
            den = out[:, :, DH]
            e = m.small[:, EN + 4 * t:EN + 4 * t + 4]
            d = m.small[:, DEN + 4 * t:DEN + 4 * t + 4]
            self.eng.wait_ge(m.to_dve[4 + t], w.next(m.to_dve[4 + t]))
            self.isa.scalar_tensor_tensor(d, den, -1.0, e, ALU.mult, ALU.max)
            self.settle()
            self.isa.tensor_tensor(d, den, d, ALU.max)
            self.settle()
            self.isa.reciprocal(d, d)
            self.settle()
            h = by_head(m.nat[:, t, S:2 * S])
            self.isa.tensor_tensor(h, out[:, :, 0:DH], d.unsqueeze(2).to_broadcast([P, 4, DH]), ALU.mult) \
                .then_inc(m.free[4 + t], 1)
            self.settle()
            self.isa.tensor_tensor(m.nat[:, t, S:2 * S], m.nat[:, t, S:2 * S], m.nat[:, t, 768:D], ALU.mult)
            self.settle()
            self.head_stats(t, h)
        self.head_variances()
        self.head_norm(lambda t: by_head(m.nat[:, t, S:2 * S]), S)
        self.eng.drain().then_inc(m.nat_ready, 1)
        self.softmax_heads(2, m.tab(B_TABLES, "blocks"), (DH + 32) ** -0.5)
        self.low_turned((0, 1), m.oT_hi, m.oT_lo, par[:, GN:GN + 4], (0, 1, 6, 7))
        self.split(4)
        self.scaled_add_banks()
        self.layer_norm(LN1, m.nat_ready, load=True)

    def conv4(self, bank, dst, par):
        m = self.m
        for g in range(2):
            self.isa.tensor_scalar(dst[:, g * S:(g + 1) * S], bank[:, g * S:(g + 1) * S], par[:, 5 * g + 3:5 * g + 4],
                                   par[:, 5 * g + 4:5 * g + 5], ALU.mult, ALU.add)
        for back in (1, 2, 3):
            self.settle()
            for g in range(2):
                out = dst[:, g * S + back:(g + 1) * S]
                last = self.isa.scalar_tensor_tensor(out, bank[:, g * S:(g + 1) * S - back],
                                                     par[:, 5 * g + 3 - back:5 * g + 4 - back], out, ALU.mult, ALU.add)
        self.eng.drain().then_inc(m.conv_in, 1)

    def head_stats(self, t, rows):
        m = self.m
        for h in range(4):
            i = 4 * t + h
            self.isa.bn_stats(m.small[:, ST + 6 * i:ST + 6 * i + 6], rows[:, h, :])
        self.settle()
        for h in range(4):
            i = 4 * t + h
            self.isa.bn_aggr(m.small[:, MV + 2 * i:MV + 2 * i + 2], m.small[:, ST + 6 * i:ST + 6 * i + 6])
        self.settle()

    def head_variances(self):
        m = self.m
        mv = m.small[:, MV:MV + 16].rearrange("p (i two) -> p i two", two=2)
        self.isa.tensor_scalar(m.small[:, VAR:VAR + 8], mv[:, :, 1], 1e-5, None, ALU.add).then_inc(m.rstd_in, 1)

    def head_norm(self, rows_of, col):
        m = self.m
        self.eng.wait_ge(m.rstd, self.w.next(m.rstd))
        for t in range(TT):
            for h in range(4):
                i = 4 * t + h
                self.isa.tensor_scalar(m.nat[:, t, col + h * DH:col + (h + 1) * DH], rows_of(t)[:, h, :],
                                       m.small[:, MV + 2 * i:MV + 2 * i + 1], m.small[:, RSTD8 + i:RSTD8 + i + 1],
                                       ALU.subtract, ALU.mult)
        self.settle()

    def scaled_add_banks(self):
        m = self.m
        for half in range(2):
            if half == 0:
                self.eng.wait_ge(m.to_dve[4], self.w.next(m.to_dve[4]))
            else:
                self.eng.wait_ge(m.w_used, self.w.product_done())
            for t in range(TT):
                b = 4 + 2 * half + t
                x = m.x[:, t, 512 * half:512 * half + 512]
                self.isa.scalar_tensor_tensor(x, x, ALPHA, m.bank[b], ALU.mult, ALU.add).then_inc(m.free[b], 1)
            self.settle()
            self.row_stats(half)

    def row_stats(self, half):
        m = self.m
        for t in range(TT):
            i = ST + 12 * t + 6 * half
            self.isa.bn_stats(m.small[:, i:i + 6], m.x[:, t, 512 * half:512 * half + 512])

    def layer_norm(self, at, ready, load=False):
        m = self.m
        self.settle()
        for t in range(TT):
            self.isa.bn_aggr(m.small[:, MV + 2 * t:MV + 2 * t + 2], m.small[:, ST + 12 * t:ST + 12 * t + 12])
        self.settle()
        mv = m.small[:, MV:MV + 4].rearrange("p (i two) -> p i two", two=2)
        self.isa.tensor_scalar(m.small[:, VAR:VAR + 2], mv[:, :, 1], 1e-5, None, ALU.add).then_inc(m.rstd_in, 1)
        self.eng.wait_ge(m.rstd, self.w.next(m.rstd))
        if load:
            self.eng.wait_ge(m.rows_loaded, self.w.next(m.rows_loaded, 16))
        for t in range(TT):
            x = m.x[:, t, :]
            self.isa.scalar_tensor_tensor(x, x, m.small[:, MV + 2 * t:MV + 2 * t + 1], m.arena[:, at:at + D],
                                          ALU.subtract, ALU.mult)
            self.settle()
            self.isa.scalar_tensor_tensor(x, x, m.small[:, RSTD8 + t:RSTD8 + t + 1], m.arena[:, at + D:at + 2 * D],
                                          ALU.mult, ALU.add).then_inc(ready, 1)

    def feed_forward(self):
        m, w = self.m, self.w
        self.low_turned((0, 1, 2, 3), m.hT_hi, m.hT_lo)
        self.hidden(0)
        with w.repeat((FF_SUBS - 1) // 2, DVE_SWIGLU_TURN):
            for p in (1, 0):
                self.hidden(p, 1)
        self.split(1)
        self.scaled_add_banks()
        self.layer_norm(LN2, m.nat_ready)

    def hidden(self, p, ahead=0):
        m = self.m
        self.split(2)
        self.settle()
        self.eng.wait_ge(m.silu_done, self.w.next(m.silu_done))
        self.eng.wait_ge(m.w_used, self.w.product_done())
        self.isa.tensor_tensor(hidden_value(m), hidden_gate(m).rearrange("p (a b) -> p a b", a=2),
                               by_head(m.bank[2 * p + 1], 2), ALU.mult).then_inc(m.hid, 1)
        self.split(ahead)
        self.eng.wait_ge(m.hid_hi, self.w.next(m.hid_hi))
        self.isa.tensor_tensor(m.oT_lo[:, 2 * p:2 * p + 2, :], hidden_value(m), m.oT_hi[:, 2 * p:2 * p + 2, :].bitcast(F32),
                               ALU.subtract).then_inc(m.hid_ready, 1)
        self.eng.drain().then_inc(m.free[2 * p + 1], 1)

    def route(self):
        m, w = self.m, self.w
        self.low_turned((0, 1, 2, 3), m.hT_hi, m.hT_lo)
        self.split(1)
        self.settle()
        self.eng.wait_ge(m.w_used, self.w.product_done())
        tt, ts = self.isa.tensor_tensor, self.isa.tensor_scalar
        sel, lg, gate, place = (route_part(m, i) for i in (0, 1, 2, 3))
        best, second, tmp = (route_part(m, i) for i in (4, 5, 6))
        vals, d, s = route_part(m, 8, 4), route_part(m, 10, 2), route_part(m, 11, 4)
        counts = route_part(m, 12, 8)
        eights = [m.arena[:, ROUTE + 256 + 128 * i:ROUTE + 384 + 128 * i] for i in range(3)]
        after, better, greater = (a.rearrange("p (t e j) -> p t e j", t=TT, e=8) for a in eights)
        for t in range(TT):
            self.isa.tensor_copy(lg[:, 8 * t:8 * t + 8], m.bank[t][:, 0:8]).then_inc(m.free[t], 1)
        slots = m.tab(B_TABLES, "slots")

        def by_tile(a):
            return a.rearrange("p (t e) -> p t e", t=TT)

        shape = [P, TT, 8, 8]
        mine, other = (by_tile(lg).unsqueeze(a).to_broadcast(shape) for a in (3, 2))
        j = slots[:, 0:8].unsqueeze(1).unsqueeze(1).to_broadcast(shape)
        e = slots[:, 0:8].unsqueeze(1).unsqueeze(3).to_broadcast(shape)
        tt(after, j, e, ALU.is_lt)
        self.settle()
        tt(better, other, mine, ALU.is_equal)
        tt(greater, other, mine, ALU.is_gt)
        self.settle()
        tt(better, better, after, ALU.mult)
        self.settle()
        tt(better, better, greater, ALU.add)
        self.settle()
        self.isa.tensor_reduce(by_tile(tmp), better, AX.X, ALU.add)
        self.settle()
        ts(sel, tmp, 1.5, None, ALU.is_lt)
        self.eng.drain().then_inc(m.selected, 1)
        ts(best, tmp, 0.0, None, ALU.is_equal)
        ts(second, tmp, 1.0, None, ALU.is_equal)
        self.settle()
        both = eights[0][:, 0:32]
        tt(both[:, 0:16], best, lg, ALU.mult)
        tt(both[:, 16:32], second, lg, ALU.mult)
        self.settle()
        self.isa.tensor_reduce(vals, both.rearrange("p (i e) -> p i e", e=8), AX.X, ALU.add)
        self.settle()
        tt(d, vals[:, 2:4], vals[:, 0:2], ALU.subtract).then_inc(m.d_ready, 1)
        self.isa.memset(m.nat[:, :, :], 0.0)
        self.isa.memset(picksT(m), 0.0)
        upos, ugate = (m.arena[:, a:a + 24].rearrange("p (t u) -> p t u", t=TT) for a in (UPOS, UGATE))
        self.isa.memset(m.arena[:, UPOS:UPOS + 48], -1.0)
        self.eng.wait_ge(m.e_ready, w.next(m.e_ready))
        ts(s[:, 0:2], d, 1.0, None, ALU.add)
        self.settle()
        self.isa.reciprocal(s[:, 0:2], s[:, 0:2])
        self.settle()
        tt(s[:, 2:4], s[:, 0:2], d, ALU.mult)
        self.settle()
        for which, at in ((best, 0), (second, 2)):
            tt(by_tile(which), by_tile(which), s[:, at:at + 2].unsqueeze(2).to_broadcast([P, TT, 8]), ALU.mult)
        self.settle()
        tt(gate, best, second, ALU.add)
        self.eng.wait_ge(m.placed, w.next(m.placed))
        self.isa.scalar_tensor_tensor(place, m.bank[2][:, 0:16], 1.0, sel, ALU.add, ALU.mult)
        self.isa.tensor_copy(counts, m.bank[2][:, 16:24]).then_inc(m.free[2], 1)
        self.settle()
        ts(place, place, -1.0, None, ALU.add)
        self.settle()
        self.isa.tensor_copy(upos[:, :, 0:8], by_tile(place))
        self.isa.tensor_copy(ugate[:, :, 0:8], by_tile(gate))
        self.settle()
        self.make_picks(0)
        full, rank = (route_part(m, i, 8) for i in (4, 5))
        ts(full, counts, float(P), None, ALU.is_gt)
        self.isa.memset(y_rows(m), 0.0)
        self.isa.tensor_copy(m.units[:, 0:8], slots[:, 0:8])
        self.isa.tensor_scalar(m.units[:, 11:12], slots[:, 0:1], 0.0, None, ALU.mult)
        self.settle()
        one = m.tab(B_TABLES, "ones")[:, 0:8]
        self.isa.tensor_tensor_scan(rank, one, full, 0.0, ALU.mult, ALU.add)
        self.settle()
        ts(m.units[:, COUNT:COUNT + 1], rank[:, 7:8], 8.0, None, ALU.add)
        shape = [P, 3, 8]
        mine = eights[1][:, 0:24].rearrange("p (k e) -> p k e", k=3)
        tt(mine, rank.unsqueeze(1).to_broadcast(shape), slots[:, 1:4].unsqueeze(2).to_broadcast(shape), ALU.is_equal)
        self.settle()
        tt(mine, mine, full.unsqueeze(1).to_broadcast(shape), ALU.mult)
        self.settle()
        picked = eights[2][:, 0:120].rearrange("p (i k e) -> p i k e", i=5, k=3)
        for i, src in enumerate((slots[:, 0:8], place[:, 0:8], place[:, 8:16], gate[:, 0:8], gate[:, 8:16])):
            tt(picked[:, i], mine, src.unsqueeze(1).to_broadcast(shape), ALU.mult)
        self.settle()
        rests = eights[0][:, 0:15].rearrange("p (i k) -> p i k", i=5)
        self.isa.tensor_reduce(rests, picked, AX.X, ALU.add)
        self.settle()
        self.isa.tensor_copy(m.units[:, 8:11], rests[:, 0])
        ts(upos[:, :, 8:11], rests[:, 1:3], -float(P), None, ALU.add)
        self.isa.tensor_copy(ugate[:, :, 8:11], rests[:, 3:5])
        self.eng.drain().then_inc(m.units_ready, 1)
        self.eng.drain().then_inc(m.y_rows, 1)

    def make_picks(self, unit):
        m = self.m
        slots = m.tab(B_TABLES, "slots")
        for t in range(TT):
            if type(unit) is int:
                pos, gate = (m.arena[:, a + 12 * t + unit:a + 12 * t + unit + 1] for a in (UPOS, UGATE))
            else:
                pos, gate = (m.arena[:, bass.ds(unit + (a + 12 * t), 1)] for a in (UPOS, UGATE))
            self.isa.tensor_scalar(picks(m, t), slots, pos, None, ALU.is_equal)
            self.isa.tensor_scalar(weighted(m, t), slots, pos, gate, ALU.is_equal, ALU.mult)
        self.eng.drain().then_inc(m.picks_ready, 1)

    def gathered(self):
        m = self.m
        for j, b in enumerate((6, 7)):
            self.eng.wait_ge(m.act_hi, self.w.next(m.act_hi))
            self.isa.tensor_tensor(m.hT_lo[:, 4 * j:4 * j + 4, 0:P], by_head(m.bank[b]),
                                   m.hT_hi[:, 4 * j:4 * j + 4, 0:P].bitcast(F32), ALU.subtract).then_inc(m.free[b], 1)
        self.eng.drain().then_inc(m.x_here, 1)

    def hidden_rows(self):
        m = self.m
        self.settle()
        self.eng.wait_ge(m.silu_done, self.w.next(m.silu_done))
        self.eng.wait_ge(m.w_used, self.w.product_done())
        self.isa.tensor_tensor(h_rows(m), g_rows(m), m.bank[1], ALU.mult).then_inc(m.h_rows, 1)
        self.eng.drain().then_inc(m.free[1], 1)

    def hidden_turned(self):
        m = self.m
        self.eng.wait_ge(m.hid_hi, self.w.next(m.hid_hi))
        self.isa.tensor_tensor(m.oT_lo[:, 0:4, 0:P], by_head(m.bank[2]), m.oT_hi[:, 0:4, 0:P].bitcast(F32),
                               ALU.subtract).then_inc(m.hid_ready, 1)
        self.eng.drain().then_inc(m.free[2], 1)

    def gather_shares(self):
        m = self.m
        self.settle()
        for t, banks in ((0, (6, 7)), (1, (3, 2))):
            for half, b in enumerate(banks):
                y = m.nat[:, t, 512 * half:512 * half + 512]
                self.eng.wait_ge(m.to_dve[b], self.w.next(m.to_dve[b]))
                self.isa.tensor_tensor(y, y, m.bank[b], ALU.add).then_inc(m.free[b], 1)

    def experts(self):
        m, w = self.m, self.w
        self.eng.wait_ge(m.units_ready, w.next(m.units_ready))
        units = self.isa.value_load(m.units[0:1, COUNT:COUNT + 1], min_val=8, max_val=11)
        self.gathered()
        with w.repeat(units, DVE_UNIT) as u:
            self.split(4)
            self.hidden_rows()
            self.gather_shares()
            self.eng.wait_ge(m.to_dve[6], w.next(m.to_dve[6]))
            self.isa.tensor_copy(picksT(m), m.bank[6][:, 0:S]).then_inc(m.free[6], 1)
            self.make_picks(u + 1)
            with w.repeat(EXP_STEPS - 1, DVE_STEP):
                self.split(2)
                self.hidden_turned()
                self.split(2)
                self.hidden_rows()
                self.split(2)
            self.hidden_turned()
            self.gathered()
            self.split(2)
        self.gather_shares()
        self.settle()
        for t in range(TT):
            self.isa.scalar_tensor_tensor(m.x[:, t, :], m.x[:, t, :], ALPHA, m.nat[:, t, :], ALU.mult, ALU.add)
        self.settle()
        for half in range(2):
            self.row_stats(half)
        self.layer_norm(LN2, m.result_ready)


PE_FFN_TURN = {
    "reuse bank_free0": 1, "reuse bank_free1": 1, "reuse bank_free2": 1, "reuse bank_free3": 1,
    "hid_ready": 2, "chunks": 6}
ACT_FFN_TURN = {"silu_in": 2, "hid": 2, "chunks": 6}
DVE_FFN_TURN = {"silu_done": 2, "hid_hi": 2, "chunks": 6}
ACT_SWIGLU_TURN = {"hid": 2, "chunks": 6}
DVE_SWIGLU_TURN = {"silu_done": 2, "hid_hi": 2, "chunks": 6}
PE_LAYER = {
    "reuse bank_free0": 20, "nat_ready": 5, "reuse bank_free1": 20, "reuse bank_free2": 19,
    "reuse bank_free3": 18, "reuse bank_free4": 9, "hT_ready": 12, "reuse bank_free5": 9, "kq_copied": 7,
    "reuse bank_free6": 15, "reuse bank_free7": 14, "roped": 7, "probs_ready": 16, "pt_ready": 24,
    "copied": 8, "lom_ready": 8, "oT_ready": 1, "hid_ready": 11, "chunks": 72}
ACT_LAYER = {
    "x_ready": 4, "rstd": 2, "cols_ready": 1, "to_act0": 5, "to_act1": 5, "to_act2": 5, "to_act3": 5,
    "negm": 8, "probs_turned": 16, "reuse weighed": 24, "weighed": 24, "probs_free": 1, "logw_ready": 8,
    "gate_in": 12, "silu_in": 11, "hid": 11, "chunks": 72}
DVE_LAYER = {
    "squares": 2, "rstd": 2, "act_hi": 24, "to_dve0": 8, "to_dve1": 8, "to_dve2": 8, "to_dve3": 7,
    "reuse probs_turned": 16, "exped": 8, "l_ready": 8, "rows_loaded": 32, "gate_out": 12, "to_dve4": 2,
    "silu_done": 11, "hid_hi": 11, "chunks": 72}
POOL_LAYER = {"rstd_in": 2, "n_ready": 8, "weighed": 24}
PE_UNIT = {
    "reuse bank_free0": 7, "reuse bank_free1": 7, "reuse bank_free2": 8, "reuse bank_free3": 1,
    "reuse bank_free4": 1, "reuse bank_free5": 1, "reuse bank_free6": 3, "reuse bank_free7": 2,
    "hid_ready": 7, "picks_ready": 1, "x_here": 1, "y_rows": 1, "h_rows": 7, "chunks": 42}
ACT_UNIT = {"to_act2": 7, "to_act6": 1, "to_act7": 1, "reuse h_rows": 7, "chunks": 42}
DVE_UNIT = {
    "act_hi": 2, "to_dve2": 1, "to_dve3": 1, "silu_done": 7, "hid_hi": 7, "to_dve6": 2, "to_dve7": 1,
    "chunks": 42}
PE_STEP = {
    "reuse bank_free0": 1, "reuse bank_free1": 1, "reuse bank_free2": 1, "hid_ready": 1, "h_rows": 1,
    "chunks": 6}
ACT_STEP = {"to_act2": 1, "reuse h_rows": 1, "chunks": 6}
DVE_STEP = {"silu_done": 1, "hid_hi": 1, "chunks": 6}


def program(nc, inp, out):
    with ExitStack() as ctx:
        m = Memory(nc, ctx)
        block = ctx.enter_context(nc.Block())

        @block.sync
        def _(sp):
            w = Waits(sp)
            w.rings = 0
            sp.dma_start(m.x[:], inp["x"][0].rearrange("(t p) d -> p t d", p=P)).then_inc(m.x_loaded, 16)
            sp.dma_start(m.all_cols[:], inp["cols_a"]).then_inc(m.cols_loaded, 16)
            sp.dma_start(m.tables[:, 0:SHARED], inp["tables_a"][:, 0:SHARED]).then_inc(m.shared_loaded, 16)

            def load(chunk):
                raw, _, _, number = w.take()
                sp.wait_ge(m.lo_ready, number + 1)
                sp.dma_start(m.raw[:, raw, :], inp["weights"][chunk]).then_inc(m.raw_full[raw], 16)

            static = FIXED + RAW
            with w.repeat(static // RAW, {"chunks": RAW}) as i:
                for j in range(RAW):
                    load(i * RAW + j)
            for c in range(static // RAW * RAW, static):
                load(c)
            sp.wait_ge(m.units_ready, w.next(m.units_ready))
            units = sp.value_load(m.units[0:1, COUNT:COUNT + 1], min_val=8, max_val=11)
            with w.repeat(units, {"chunks": UNIT}) as u:
                for at, first, end in ((0, RAW, UNIT), (1, 0, RAW)):
                    expert = sp.value_load(m.units[0:1, bass.ds(u + at, 1)], min_val=0, max_val=N_EXP - 1)
                    for j in range(first, end):
                        load(expert * UNIT + (FIXED + j))
            for t in range(TT):
                sp.wait_ge(m.result_ready, w.next(m.result_ready))
                sp.dma_start(out[0, t * P:(t + 1) * P], m.x[:, t, :]).then_inc(m.stored, 16)
            sp.wait_ge(m.stored, w.next(m.stored, 16 * TT))

        @block.gpsimd
        def _(pool):
            e = Pool(nc, m, pool, nc.gpsimd)
            nc.gpsimd.memset(m.small[:, HALF:HALF + 8], -0.5)
            nc.gpsimd.memset(m.zeros[:].bitcast(F32), 0.0)
            pool.drain().then_inc(m.start, 1)
            for sem in [m.hi_ready, m.lo_ready, m.w_used, m.probs_turned, m.weighed, m.h_rows] + m.free:
                pool.sem_inc(sem, FREE_AT_START[sem.name])
            pool.wait_ge(m.start, e.w.next(m.start))
            e.power((2, 4), 4)
            pool.dma_start(m.tables[:, SHARED:A_COLS], inp["tables_a"][:, SHARED:A_COLS]).then_inc(m.tables_loaded, 16)
            with e.w.repeat(DEPTH, POOL_LAYER) as layer:
                e.stick_heads(m.tab(A_TABLES, "before01"))
                pool.wait_ge(m.weighed, e.w.next(m.weighed, 24))
                pool.dma_start(m.arena[:, 0:3 * D], inp["b_gate"][layer].partition_broadcast(P)) \
                    .then_inc(m.rows_loaded, 16)
                pool.dma_start(m.arena[:, 3 * D:4 * D], inp["norm_final"].partition_broadcast(P)) \
                    .then_inc(m.rows_loaded, 16)
                e.power((2, 4), 4)
                e.power((2, 4), 4)
            pool.dma_start(m.tables[:, SHARED:B_COLS], inp["tables_b"]).then_inc(m.tables_b_loaded, 16)
            pool.dma_start(m.all_cols[:, 0:DEPTH * B_PARAMS], inp["cols_b"]).then_inc(m.cols_b_loaded, 16)
            for layer in range(DEPTH):
                e.power((CMS, CMS + 4), CRS)
                e.power((VAR, VAR + 8), RSTD8)
                e.power((VAR, VAR + 8), RSTD8)
                pool.wait_ge(m.weighed, e.w.next(m.weighed, 8))
                pool.dma_start(m.arena[:, 0:4 * D], inp["norms"][layer].partition_broadcast(P)) \
                    .then_inc(m.rows_loaded, 16)
                e.power((VAR, VAR + 2), RSTD8)
                e.power((VAR, VAR + 2), RSTD8)

        @block.scalar
        def _(act):
            a = ScalarA(nc, m, act, nc.scalar)
            a.squares()
            a.scaled_rows()
            a.split(AHEAD)
            with a.w.repeat(DEPTH, ACT_LAYER):
                a.layer()
            b = ScalarB(nc, m, act, nc.scalar, a)
            b.mixer(0)
            b.feed_forward()
            b.mixer(1)
            b.experts()

        @block.vector
        def _(dve):
            a = VectorA(nc, m, dve, nc.vector)
            dve.wait_ge(m.x_loaded, a.w.next(m.x_loaded, 16))
            dve.drain().then_inc(m.x_ready, 2)
            a.rms_rows()
            dve.wait_ge(m.cols_loaded, a.w.next(m.cols_loaded, 16))
            dve.wait_ge(m.shared_loaded, a.w.next(m.shared_loaded, 16))
            a.split(AHEAD)
            with a.w.repeat(DEPTH, DVE_LAYER) as layer:
                a.layer(layer)
            b = VectorB(nc, m, dve, nc.vector, a)
            b.normed_start()
            b.mixer(0)
            b.feed_forward()
            b.mixer(1)
            b.route()
            b.experts()

        @block.tensor
        def _(pe):
            a = TensorA(nc, m, pe, nc.tensor)
            pe.wait_ge(m.shared_loaded, a.w.next(m.shared_loaded, 16))
            pe.wait_ge(m.start, a.w.next(m.start))
            with a.w.repeat(DEPTH, PE_LAYER):
                a.layer()
            b = TensorB(nc, m, pe, nc.tensor, a)
            b.w.skip(m.nat_ready, 2)
            for layer in range(DEPTH):
                b.mixer()
                b.turn_x(m.tab(B_TABLES, "ident"))
                if layer == 0:
                    b.feed_forward()
            b.route()
            b.experts()



def turning_tables(half):
    inv = np.float32(10000.0) ** (-np.arange(half, dtype=np.float32) / np.float32(half))
    ang = np.arange(S, dtype=np.float32)[None, :] * np.tile(inv, P // half)[:, None]
    return np.cos(ang), np.sin(ang)


def rotation(half):
    r = np.zeros((P, P), np.float32)
    for i in range(P):
        if i % (2 * half) < half:
            r[i + half, i] = -1.0
        else:
            r[i - half, i] = 1.0
    return r


def tables_a():
    i = np.arange(P)
    causal = np.where(i[None, :] <= i[:, None], 0.0, NEG)
    window = np.where(i[None, :] > i[:, None], 0.0, NEG)
    before = i[:, None] < i[None, :]
    one = np.ones((P, P))
    cos, sin = turning_tables(DH // 2)
    parts = dict(
        ident=np.eye(P), rot64=rotation(DH // 2), cos64=cos, sin64=sin,
        band=np.concatenate([window, causal], 1), causal=np.concatenate([0 * one, causal], 1),
        before01=np.concatenate([before, one, before], 1),
        before=np.concatenate([np.where(before, 0.0, NEG), 0 * one, np.where(before, 0.0, NEG)], 1),
        tri=np.where(i[:, None] >= i[None, :], -1.0, 0.0), ones=-one)
    return np.concatenate([parts[n] for n in A_TABLES], 1).astype(np.float32)


def chunk_of(w, kt=None):
    k, n = w.shape
    out = w.reshape(k // P, P, n).transpose(1, 0, 2).reshape(P, -1)
    assert out.shape[1] <= CH
    return np.pad(out, ((0, 0), (0, CH - out.shape[1])))


def layer_chunks_a(w_in, w_branch, w_out, w_up, w_down):
    o = np.cumsum([0, 512, 128, 128, 512, 512, 512, 512, 512, 512])
    qa, ka, va, qb, kb, vb, qc, kc, vc = (w_in[:, o[i]:o[i + 1]] for i in range(9))
    heads = qa.reshape(D, 8, DH)
    paired = np.stack([heads[:, 0:4], heads[:, 4:8]], 2).reshape(D, 512)
    out = []

    def turned(w):
        out.extend(chunk_of(w[:, c:c + S]) for c in range(0, w.shape[1], S))

    def rows(w, k=512):
        out.extend(chunk_of(w[a:a + k]) for a in range(0, w.shape[0], k))

    turned(paired)
    turned(np.concatenate([ka, va], 1))
    turned(qb), turned(kb), rows(vb), turned(qc), turned(kc), rows(vc)
    for u in range(6):
        i, h = u // 2, u % 2
        rows(w_in[:, o[9] + i * D + 512 * h:o[9] + i * D + 512 * h + 512])
        rows(w_branch[i][:, 512 * h:512 * h + 512])
    for a, b in ((0, 256), (256, 512), (512, 640), (640, 768), (768, 896), (896, 1024)):
        out.append(chunk_of(w_out[a:b]))

    def up(j):
        turned(w_up[:, j * S:(j + 1) * S])
        turned(w_up[:, D_FF + j * S:D_FF + (j + 1) * S])

    up(0)
    for j in range(1, FF_SUBS):
        up(j)
        rows(w_down[(j - 1) * S:j * S], S)
    rows(w_down[(FF_SUBS - 1) * S:], S)
    assert len(out) == A_LAYER, len(out)
    return out


def columns_a(norm_mix, norm_ffn, conv_w, conv_b, sinks):
    taps = np.concatenate([conv_w, conv_b[None]], 0).reshape(4, 2, FF_SUBS, 2, P)
    return np.concatenate([
        norm_mix.reshape(KT, P).T, norm_ffn.reshape(KT, P).T,
        taps.transpose(4, 2, 1, 3, 0).reshape(P, -1), np.broadcast_to(sinks, (P, 8))], 1)


def tables_b():
    i = np.arange(P)
    one = np.ones((P, P))
    cos, sin = turning_tables(16)
    before = i[:, None] < i[None, :]
    limit = (i // 64 + 1) * 64
    in_block = np.where(i[None, :] < limit[:, None], 0.0, NEG)
    ago = (i[None, :] - i[:, None]).astype(np.float64)
    decay = []
    for h in range(4):
        log_gamma = np.log1p(-2.0 ** (-5.0 - h))
        decay += [np.where(ago >= 0, np.exp(np.maximum(ago, 0) * log_gamma), 0.0) * SCALE,
                  np.exp((ago + P) * log_gamma) * SCALE]
    parts = dict(
        rot32=rotation(16), cos32=cos, sin32=sin, blocks=np.concatenate([0 * one, in_block], 1),
        decay=np.concatenate(decay, 1), causalT=np.where(i[None, :] < i[:, None], -NEG, 0.0), ones=one,
        below=np.where(before, 1.0, 0.0), slots=np.broadcast_to(i, (P, P)))
    return np.concatenate([parts[n] for n in B_TABLES if n in parts], 1).astype(np.float32)


def ffn_steps(w_gate, w_up, w_down, n):
    steps = w_gate.shape[1] // n
    rows = CH // n
    out = []

    def add(w, k):
        out.extend(chunk_of(w[a:a + k]) for a in range(0, w.shape[0], k))

    for s in range(steps + 1):
        if s < steps:
            for w in (w_gate, w_up):
                add(w[:, s * n:(s + 1) * n], rows * P)
        if s:
            add(w_down[(s - 1) * n:s * n], CH // D * P)
    return out


def mixer_chunks_b(w_in, w_uq, w_ukv, w_out):
    def cut(a, n):
        return w_in[:, a:a + n]

    out = [chunk_of(cut(0, 256)), chunk_of(cut(256, 256)),
           chunk_of(np.concatenate([cut(1408, 32)] * 4 + [cut(2464, 8)], 1))]

    def rows(w, k=512):
        out.extend(chunk_of(w[a:a + k]) for a in range(0, w.shape[0], k))

    rows(cut(512, 512))
    rows(cut(1024, 384))
    out.extend([chunk_of(cut(1440, 256)), chunk_of(cut(1696, 256))])
    rows(cut(1952, 512))
    uq = w_uq.reshape(256, 8, 96)
    out.append(chunk_of(np.concatenate([uq[:, :, 0:64].reshape(256, 512), uq[:, :, 64:].reshape(256, 256)], 1)))
    ukv = w_ukv.reshape(128, 8, 128)
    out.append(chunk_of(np.concatenate([ukv[:, :, 0:64].reshape(128, 512), ukv[:, :, 64:].reshape(128, 512)], 1)))
    rows(w_out, 256)
    assert len(out) == B_MIXER, len(out)
    return out


def columns_b(q_norm, kv_norm, ret_gn, mlstm_gn, conv_w, conv_b, b_i, b_f):
    taps = np.concatenate([conv_w, conv_b[None]], 0).reshape(5, 4, P)
    biases = np.zeros((P, 2), np.float32)
    biases[0:4, 0], biases[0:4, 1] = b_i, b_f
    return np.concatenate([q_norm.reshape(2, P).T, kv_norm.reshape(1, P).T, ret_gn.reshape(2, P).T,
                           mlstm_gn.reshape(2, P).T, taps.transpose(2, 1, 0).reshape(P, 20), biases], 1)


def laid_out(a):
    layers = range(DEPTH)
    chunks = []
    for i in layers:
        chunks += layer_chunks_a(a["w_in"][i], a["w_branch"][i], a["w_out"][i], a["w_up"][i], a["w_down"][i])
    for i in layers:
        chunks += mixer_chunks_b(a["w_in_2"][i], a["mla_w_uq_2"][i], a["mla_w_ukv_2"][i], a["w_out_2"][i])
        if i == 0:
            chunks += ffn_steps(a["ffn_w_gate_2"][0], a["ffn_w_up_2"][0], a["ffn_w_down_2"][0], S)
    chunks.append(chunk_of(a["moe_router_2"][0]))
    assert len(chunks) == FIXED, len(chunks)
    for e in range(N_EXP):
        chunks += ffn_steps(a["moe_w_gate_2"][0, e], a["moe_w_up_2"][0, e], a["moe_w_down_2"][0, e], 512)
    norms = np.stack([np.concatenate([a[n][i] for n in ("ln1_w_2", "ln1_b_2", "ln2_w_2", "ln2_b_2")]) for i in layers])
    return {
        "x": a["x"],
        "weights": np.stack(chunks),
        "tables_a": tables_a(),
        "tables_b": tables_b(),
        "cols_a": np.concatenate([columns_a(a["norm_mix"][i], a["norm_ffn"][i], a["conv_w"][i], a["conv_b"][i],
                                            a["sinks"][i]) for i in layers], 1),
        "cols_b": np.concatenate([columns_b(*(a[n + "_2"][i] for n in (
            "mla_q_norm_w", "mla_kv_norm_w", "ret_gn_w", "mlstm_gn_w", "mlstm_conv_w", "mlstm_conv_b",
            "mlstm_b_i", "mlstm_b_f"))) for i in layers], 1),
        "b_gate": a["b_gate"],
        "norm_final": a["norm_final"],
        "norms": norms,
    }


def kernel(**inputs):
    import concourse.bacc as _bacc
    from concourse.bass_utils import run_bass_kernel_spmd as _run

    nc = _bacc.Bacc("TRN2", target_bir_lowering=False, num_devices=1)
    arrays, args = {}, {}
    for name, a in laid_out({k: np.asarray(v) for k, v in inputs.items()}).items():
        arrays[f"in_{name}_dram"] = np.ascontiguousarray(a)
        args[name] = nc.dram_tensor(f"in_{name}_dram", a.shape, F32, kind="ExternalInput").ap()
    out = nc.dram_tensor("out_0_dram", (1, S, D), F32, kind="ExternalOutput").ap()
    program(nc, args, out)
    r = _run(nc, [arrays], core_ids=[0])
    return r.results[0]["out_0_dram"]
```
